# Optimizing a Trainium2 kernel written in Bass

```python
import math
import jax, jax.numpy as jnp
from jax import lax
import numpy as np

D_MODEL = 1024
BATCH = 1
SEQ = 256
DEPTH = 2

HEAD_DIM = 64
CONV_CH = 256
CONV_K = 31
SC_CH = 256
SC_K = 3
SWA_Q_HEADS = 4
SWA_KV_HEADS = 2
WINDOW = 128
BLOCK = 128
FOX_HEADS = 4
N_BUCKETS = 32
MAX_DISTANCE = 128
D_FF = 2816
N_BRANCH = 4
EPS = 1e-6
NEG_INF = -1e30

SWA_COLS = (SWA_Q_HEADS + 2 * SWA_KV_HEADS) * HEAD_DIM
FOX_COLS = 3 * FOX_HEADS * HEAD_DIM + FOX_HEADS
_SIZES = (CONV_CH, CONV_CH,
          SC_CH, SC_CH, SC_CH,
          SWA_Q_HEADS * HEAD_DIM, SWA_KV_HEADS * HEAD_DIM, SWA_KV_HEADS * HEAD_DIM,
          FOX_HEADS * HEAD_DIM, FOX_HEADS * HEAD_DIM, FOX_HEADS * HEAD_DIM, FOX_HEADS,
          N_BRANCH * D_MODEL)
SPLITS = tuple(int(s) for s in np.cumsum(_SIZES)[:-1])
IN_COLS = int(sum(_SIZES))


def _rmsnorm(x, g):
    xf = x.astype(jnp.float32)
    y = xf * lax.rsqrt(jnp.mean(xf * xf, axis=-1, keepdims=True) + EPS)
    return (y * g.astype(jnp.float32)).astype(x.dtype)

def _layernorm(x, g, b):
    xf = x.astype(jnp.float32)
    mu = jnp.mean(xf, axis=-1, keepdims=True)
    var = jnp.mean(jnp.square(xf - mu), axis=-1, keepdims=True)
    y = (xf - mu) * lax.rsqrt(var + EPS)
    return (y * g.astype(jnp.float32) + b.astype(jnp.float32)).astype(x.dtype)

def _swiglu(x, w_gate, w_up, w_down):
    return (jax.nn.silu(x @ w_gate) * (x @ w_up)) @ w_down

def _causal_depthwise_conv(x, w):
    k = w.shape[0]
    return lax.conv_general_dilated(
        x, w[:, None, :].astype(x.dtype), window_strides=(1,), padding=[(k - 1, 0)],
        dimension_numbers=("NWC", "WIO", "NWC"), feature_group_count=x.shape[-1])

def _t5_bucket(dist):
    max_exact = N_BUCKETS // 2
    d = jnp.maximum(dist, 1).astype(jnp.float32)
    large = max_exact + (jnp.log(d / max_exact) / math.log(MAX_DISTANCE / max_exact)
                         * (N_BUCKETS - max_exact)).astype(jnp.int32)
    large = jnp.minimum(large, N_BUCKETS - 1)
    return jnp.where(dist < max_exact, dist, large)

def _sliding_window_attention(q, k, v, sink, rel_bias):
    b, t, hq, dh = q.shape
    hkv = k.shape[2]
    grp = hq // hkv
    nb = t // BLOCK
    qb = q.reshape(b, nb, BLOCK, hkv, grp, dh)
    kb = k.reshape(b, nb, BLOCK, hkv, dh)
    vb = v.reshape(b, nb, BLOCK, hkv, dh)
    pad = ((0, 0), (1, 0), (0, 0), (0, 0), (0, 0))
    kk = jnp.concatenate([jnp.pad(kb, pad)[:, :-1], kb], axis=2)
    vv = jnp.concatenate([jnp.pad(vb, pad)[:, :-1], vb], axis=2)
    s = jnp.einsum("bnqhgd,bnkhd->bnhgqk", qb, kk,
                   preferred_element_type=jnp.float32) * (dh ** -0.5)
    qi = jnp.arange(BLOCK)[:, None] + BLOCK
    ki = jnp.arange(2 * BLOCK)[None, :]
    dist = qi - ki
    local_ok = (dist >= 0) & (dist < WINDOW)
    blk_ok = (jnp.arange(nb)[:, None, None] > 0) | (ki[None] >= BLOCK)
    mask = local_ok[None] & blk_ok
    bias = rel_bias[_t5_bucket(jnp.maximum(dist, 0))]
    bias = bias.transpose(2, 0, 1).reshape(hkv, grp, BLOCK, 2 * BLOCK).astype(jnp.float32)
    s = jnp.where(mask[None, :, None, None], s + bias, NEG_INF)
    sk = sink.astype(jnp.float32).reshape(hkv, grp)[:, :, None, None]
    m = jnp.maximum(jnp.max(s, axis=-1, keepdims=True), sk)
    p = jnp.exp(s - m)
    p = p / (jnp.sum(p, axis=-1, keepdims=True) + jnp.exp(sk - m))
    o = jnp.einsum("bnhgqk,bnkhd->bnqhgd", p.astype(v.dtype), vv)
    return o.reshape(b, t, hq * dh)

def _forgetting_attention(q, k, v, log_f):
    b, t, h, dh = q.shape
    nb = t // BLOCK
    cum = jnp.cumsum(log_f, axis=1)
    cum_k = cum.transpose(0, 2, 1)
    qb = q.reshape(b, nb, BLOCK, h, dh).transpose(1, 0, 2, 3, 4)
    cq = cum.reshape(b, nb, BLOCK, h).transpose(1, 0, 3, 2)
    kpos = jnp.arange(t)

    def one_block(args):
        q_blk, c_blk, bi = args
        s = jnp.einsum("bqhd,bkhd->bhqk", q_blk, k,
                       preferred_element_type=jnp.float32) * (dh ** -0.5)
        s = s + (c_blk[..., :, None] - cum_k[:, :, None, :])
        qpos = bi * BLOCK + jnp.arange(BLOCK)
        s = jnp.where(kpos[None, :] <= qpos[:, None], s, NEG_INF)
        p = jax.nn.softmax(s, axis=-1)
        return jnp.einsum("bhqk,bkhd->bqhd", p.astype(v.dtype), v)

    o = lax.map(one_block, (qb, cq, jnp.arange(nb)))
    return o.transpose(1, 0, 2, 3, 4).reshape(b, t, h * dh)

def _normal(k, shape, scale):
    return scale * jax.random.normal(k, shape, jnp.float32)

def first_inputs(seed: int = 0) -> dict:
    key = jax.random.key(seed)
    ks = jax.random.split(key, 32)
    L, D = DEPTH, D_MODEL
    return {
        "x": _normal(ks[0], (BATCH, SEQ, D), 1.0),
        "rel_bias": _normal(ks[1], (N_BUCKETS, SWA_Q_HEADS), 0.5),
        "ffn1_norm": 1.0 + _normal(ks[2], (L, D), 0.05),
        "ffn1_w_gate": _normal(ks[3], (L, D, D_FF), D ** -0.5),
        "ffn1_w_up": _normal(ks[4], (L, D, D_FF), D ** -0.5),
        "ffn1_w_down": _normal(ks[5], (L, D_FF, D), D_FF ** -0.5),
        "mix_norm": 1.0 + _normal(ks[6], (L, D), 0.05),
        "w_in": _normal(ks[7], (L, D, IN_COLS), D ** -0.5),
        "b_forget": 3.0 + _normal(ks[8], (L, FOX_HEADS), 0.5),
        "conf_dw": _normal(ks[9], (L, CONV_K, CONV_CH), CONV_K ** -0.5),
        "conf_dw_b": _normal(ks[10], (L, CONV_CH), 0.02),
        "conf_ln_g": 1.0 + _normal(ks[11], (L, CONV_CH), 0.05),
        "conf_ln_b": _normal(ks[12], (L, CONV_CH), 0.02),
        "conf_w_out": _normal(ks[13], (L, CONV_CH, D), CONV_CH ** -0.5),
        "sc_conv": _normal(ks[14], (L, SC_K, SC_CH), SC_K ** -0.5),
        "sc_w_out": _normal(ks[15], (L, SC_CH, D), SC_CH ** -0.5),
        "swa_q_norm": 1.0 + _normal(ks[16], (L, HEAD_DIM), 0.05),
        "swa_k_norm": 1.0 + _normal(ks[17], (L, HEAD_DIM), 0.05),
        "swa_sink": _normal(ks[18], (L, SWA_Q_HEADS), 0.5),
        "swa_w_o": _normal(ks[19], (L, SWA_Q_HEADS * HEAD_DIM, D), (SWA_Q_HEADS * HEAD_DIM) ** -0.5),
        "fox_q_norm": 1.0 + _normal(ks[20], (L, HEAD_DIM), 0.05),
        "fox_k_norm": 1.0 + _normal(ks[21], (L, HEAD_DIM), 0.05),
        "fox_w_o": _normal(ks[22], (L, FOX_HEADS * HEAD_DIM, D), (FOX_HEADS * HEAD_DIM) ** -0.5),
        "w_out": _normal(ks[23], (L, D, D), D ** -0.5),
        "ffn2_norm": 1.0 + _normal(ks[24], (L, D), 0.05),
        "ffn2_w_gate": _normal(ks[25], (L, D, D_FF), D ** -0.5),
        "ffn2_w_up": _normal(ks[26], (L, D, D_FF), D ** -0.5),
        "ffn2_w_down": _normal(ks[27], (L, D_FF, D), D_FF ** -0.5),
    }

def first_block(x, rel_bias, ffn1_norm, ffn1_w_gate, ffn1_w_up, ffn1_w_down, mix_norm, w_in,
              b_forget, conf_dw, conf_dw_b, conf_ln_g, conf_ln_b, conf_w_out, sc_conv, sc_w_out,
              swa_q_norm, swa_k_norm, swa_sink, swa_w_o, fox_q_norm, fox_k_norm, fox_w_o, w_out,
              ffn2_norm, ffn2_w_gate, ffn2_w_up, ffn2_w_down):
    bsz, t = x.shape[0], x.shape[1]
    for l in range(DEPTH):
        x = x + 0.5 * _swiglu(_rmsnorm(x, ffn1_norm[l]), ffn1_w_gate[l], ffn1_w_up[l], ffn1_w_down[l])

        h = _rmsnorm(x, mix_norm[l])
        z = h @ w_in[l]
        (c_a, c_b, s_b, s_c, s_x, a_q, a_k, a_v,
         f_q, f_k, f_v, f_f, z_gate) = jnp.split(z, SPLITS, axis=-1)

        u = c_a * jax.nn.sigmoid(c_b)
        u = _causal_depthwise_conv(u, conf_dw[l]) + conf_dw_b[l]
        u = jax.nn.silu(_layernorm(u, conf_ln_g[l], conf_ln_b[l]))
        p_conf = u @ conf_w_out[l]

        p_sc = (s_b * _causal_depthwise_conv(s_c * s_x, sc_conv[l])) @ sc_w_out[l]

        q = _rmsnorm(a_q.reshape(bsz, t, SWA_Q_HEADS, HEAD_DIM), swa_q_norm[l])
        k = _rmsnorm(a_k.reshape(bsz, t, SWA_KV_HEADS, HEAD_DIM), swa_k_norm[l])
        v = a_v.reshape(bsz, t, SWA_KV_HEADS, HEAD_DIM)
        p_swa = _sliding_window_attention(q, k, v, swa_sink[l], rel_bias) @ swa_w_o[l]

        q2 = _rmsnorm(f_q.reshape(bsz, t, FOX_HEADS, HEAD_DIM), fox_q_norm[l])
        k2 = _rmsnorm(f_k.reshape(bsz, t, FOX_HEADS, HEAD_DIM), fox_k_norm[l])
        v2 = f_v.reshape(bsz, t, FOX_HEADS, HEAD_DIM)
        log_f = jax.nn.log_sigmoid(f_f.astype(jnp.float32) + b_forget[l].astype(jnp.float32))
        p_fox = _forgetting_attention(q2, k2, v2, log_f) @ fox_w_o[l]

        g = jax.nn.sigmoid(z_gate).reshape(bsz, t, N_BRANCH, D_MODEL)
        merged = (g[:, :, 0] * p_conf + g[:, :, 1] * p_sc
                  + g[:, :, 2] * p_swa + g[:, :, 3] * p_fox)
        x = x + merged @ w_out[l]

        x = x + 0.5 * _swiglu(_rmsnorm(x, ffn2_norm[l]), ffn2_w_gate[l], ffn2_w_up[l], ffn2_w_down[l])
    return x


DEPTH_2 = 1

GRID_W = 64
CTX_LEN = 256
NA_HEADS = 8
NA_HEAD_DIM = 64
NA_WIDTH = NA_HEADS * NA_HEAD_DIM
WIN_H = 8
WIN_W = 16
NA_KEY_COLS = 2 * WIN_W
ML_HEADS = 4
ML_QK_DIM = 64
ML_V_DIM = 128
ML_QK_WIDTH = ML_HEADS * ML_QK_DIM
ML_WIDTH = ML_HEADS * ML_V_DIM
ML_CHUNK = 64
GATE_SOFTCAP = 15.0
ROPE_BASE = 10000.0
N_EXPERTS = 32
TOP_K = 4
D_EXPERT = D_MODEL
SWIGLU_ALPHA = 1.702
SWIGLU_LIMIT = 7.0
EXPERT_BLOCK = 128
NORM_EPS = 1e-6
NEG_INF_2 = -1e30
CTX_SPLITS = (NA_WIDTH, NA_WIDTH, ML_QK_WIDTH, ML_WIDTH, 4 * ML_HEADS)
LAT_SPLITS = (NA_WIDTH, ML_QK_WIDTH, ML_WIDTH, D_MODEL, D_MODEL)
IN_SPLITS = CTX_SPLITS + LAT_SPLITS
N_CTX_COLS = 2 * NA_WIDTH + ML_QK_WIDTH + ML_WIDTH + 4 * ML_HEADS
N_IN_COLS = N_CTX_COLS + NA_WIDTH + ML_QK_WIDTH + ML_WIDTH + 2 * D_MODEL


def _rmsnorm_2(x, g):
    xf = x.astype(jnp.float32)
    y = xf * lax.rsqrt(jnp.mean(xf * xf, axis=-1, keepdims=True) + NORM_EPS)
    return (y * g.astype(jnp.float32)).astype(x.dtype)

def _split(a, sizes):
    return jnp.split(a, np.cumsum(sizes)[:-1].tolist(), axis=-1)

def _na_column_tables():
    n_qb = GRID_W // WIN_W
    qcol = np.arange(GRID_W).reshape(n_qb, WIN_W)
    kstart = np.clip(np.arange(n_qb) * WIN_W - WIN_W // 2, 0, GRID_W - NA_KEY_COLS)
    kcol = kstart[:, None] + np.arange(NA_KEY_COLS)
    cs = np.clip(qcol - WIN_W // 2, 0, GRID_W - WIN_W)
    kc = kcol[:, None, :]
    mask = (kc >= cs[:, :, None]) & (kc < cs[:, :, None] + WIN_W)
    dc = np.clip(kc - qcol[:, :, None], -(WIN_W - 1), WIN_W - 1) + (WIN_W - 1)
    return kcol, mask, dc

def _neighbourhood_attention(q, k, v, k_ctx, v_ctx, rpb):
    B, S, _ = q.shape
    rows = S // GRID_W
    wr = min(WIN_H, rows)
    n_qb = GRID_W // WIN_W
    kcol, mask, dc = _na_column_tables()
    grid = (B, rows, GRID_W, NA_HEADS, NA_HEAD_DIM)
    q = q.reshape(grid) * NA_HEAD_DIM ** -0.5
    k = k.reshape(grid)
    v = v.reshape(grid)
    k_ctx = k_ctx.reshape(B, -1, NA_HEADS, NA_HEAD_DIM)
    v_ctx = v_ctx.reshape(B, -1, NA_HEADS, NA_HEAD_DIM)
    n_loc = wr * NA_KEY_COLS

    def one_row(r):
        rs = jnp.clip(r - WIN_H // 2, 0, rows - wr)
        qb = lax.dynamic_index_in_dim(q, r, axis=1, keepdims=False).reshape(B, n_qb, WIN_W, NA_HEADS, NA_HEAD_DIM)
        kb = lax.dynamic_slice_in_dim(k, rs, wr, axis=1)[:, :, kcol]
        vb = lax.dynamic_slice_in_dim(v, rs, wr, axis=1)[:, :, kcol]
        dr = rs + jnp.arange(wr) - r + (WIN_H - 1)
        bias = rpb[:, dr[None, None, :, None], dc[:, :, None, :]].astype(jnp.float32)
        s_loc = jnp.einsum('bjqhd,brjkhd->bhjqrk', qb, kb).astype(jnp.float32) + bias
        s_loc = jnp.where(mask[:, :, None, :], s_loc, NEG_INF_2).reshape(B, NA_HEADS, n_qb, WIN_W, n_loc)
        s_ctx = jnp.einsum('bjqhd,bchd->bhjqc', qb, k_ctx).astype(jnp.float32)
        p = jax.nn.softmax(jnp.concatenate([s_loc, s_ctx], axis=-1), axis=-1).astype(v.dtype)
        p_loc = p[..., :n_loc].reshape(B, NA_HEADS, n_qb, WIN_W, wr, NA_KEY_COLS)
        o = (jnp.einsum('bhjqrk,brjkhd->bjqhd', p_loc, vb)
             + jnp.einsum('bhjqc,bchd->bjqhd', p[..., n_loc:], v_ctx))
        return o.reshape(B, GRID_W, NA_WIDTH)

    o = lax.map(one_row, jnp.arange(rows, dtype=jnp.int32))
    return jnp.moveaxis(o, 0, 1).reshape(B, S, NA_WIDTH)

def _axial_rope(x, row, col):
    n_freq = ML_QK_DIM // 4
    inv_freq = ROPE_BASE ** (-jnp.arange(n_freq, dtype=jnp.float32) / n_freq)

    def rotate(xh, pos):
        ang = pos[:, None] * inv_freq
        cos = jnp.cos(ang)[:, None, :]
        sin = jnp.sin(ang)[:, None, :]
        x1, x2 = xh[..., :n_freq], xh[..., n_freq:]
        return jnp.concatenate([x1 * cos - x2 * sin, x2 * cos + x1 * sin], axis=-1)

    half = ML_QK_DIM // 2
    return jnp.concatenate([rotate(x[..., :half], row), rotate(x[..., half:], col)], axis=-1)

def _to_chunks(a):
    B, H, T = a.shape[:3]
    a = a.reshape((B, H, T // ML_CHUNK, ML_CHUNK) + a.shape[3:])
    return jnp.moveaxis(a, 2, 0)

def _mlstm_chunkwise(q, k, v, log_i, log_f, state):
    tril = np.tril(np.ones((ML_CHUNK, ML_CHUNK), dtype=bool))
    with_out = q is not None

    def step(carry, inp):
        C, n, m = carry
        if with_out:
            qc, kc, vc, li, lf = inp
        else:
            kc, vc, li, lf = inp
        b = jnp.cumsum(lf, axis=-1)
        bL = b[..., -1]
        dec = bL[..., None] - b + li
        m_new = jnp.maximum(bL + m, jnp.max(dec, axis=-1))
        w_s = jnp.exp(dec - m_new[..., None])
        w_c = jnp.exp(bL + m - m_new)
        C_new = w_c[..., None, None] * C + jnp.einsum('bhs,bhsd,bhse->bhde', w_s, kc, vc)
        n_new = w_c[..., None] * n + jnp.einsum('bhs,bhsd->bhd', w_s, kc)
        if not with_out:
            return (C_new, n_new, m_new), None
        d_mat = jnp.where(tril, b[..., :, None] - b[..., None, :] + li[..., None, :], -jnp.inf)
        m_inter = b + m[..., None]
        m_t = jnp.maximum(m_inter, jnp.max(d_mat, axis=-1))
        w_intra = jnp.exp(d_mat - m_t[..., None])
        w_inter = jnp.exp(m_inter - m_t)
        s = jnp.einsum('bhtd,bhsd->bhts', qc, kc) * w_intra
        num = (w_inter[..., None] * jnp.einsum('bhtd,bhde->bhte', qc, C)
               + jnp.einsum('bhts,bhse->bhte', s, vc))
        den = w_inter * jnp.einsum('bhtd,bhd->bht', qc, n) + jnp.sum(s, axis=-1)
        h = num / jnp.maximum(jnp.abs(den), jnp.exp(-m_t))[..., None]
        return (C_new, n_new, m_new), h

    if with_out:
        xs = (_to_chunks(q), _to_chunks(k), _to_chunks(v), _to_chunks(log_i), _to_chunks(log_f))
    else:
        xs = (_to_chunks(k), _to_chunks(v), _to_chunks(log_i), _to_chunks(log_f))
    final, hs = lax.scan(step, state, xs)
    if not with_out:
        return final
    hs = jnp.moveaxis(hs, 0, 2)
    return hs.reshape(hs.shape[0], hs.shape[1], -1, hs.shape[-1])

def _mlstm_branch(q, k, v, o_pre, gates, k_ctx, v_ctx, gates_ctx, b_gates, g_head, row, col):
    B, S, _ = q.shape
    n_ctx = k_ctx.shape[1]
    f32 = jnp.float32
    qk_scale = ML_QK_DIM ** -0.5

    def heads_first(a):
        return jnp.swapaxes(a, 1, 2)

    def flip(a):
        return jnp.flip(a, axis=2)

    q = heads_first(_axial_rope(q.reshape(B, S, ML_HEADS, ML_QK_DIM).astype(f32), row, col))
    k = heads_first(_axial_rope(k.reshape(B, S, ML_HEADS, ML_QK_DIM).astype(f32), row, col) * qk_scale)
    v = heads_first(v.reshape(B, S, ML_HEADS, ML_V_DIM).astype(f32))
    k_ctx = heads_first(k_ctx.reshape(B, n_ctx, ML_HEADS, ML_QK_DIM).astype(f32) * qk_scale)
    v_ctx = heads_first(v_ctx.reshape(B, n_ctx, ML_HEADS, ML_V_DIM).astype(f32))

    def gate_logs(g):
        t = g.shape[1]
        g = g.reshape(B, t, 4, ML_HEADS).astype(f32) + b_gates.astype(f32)
        g = GATE_SOFTCAP * jnp.tanh(g / GATE_SOFTCAP)
        g = jnp.transpose(g, (2, 0, 3, 1))
        return g[0], jax.nn.log_sigmoid(g[1]), g[2], jax.nn.log_sigmoid(g[3])

    li_f, lf_f, li_b, lf_b = gate_logs(gates)
    lic_f, lfc_f, lic_b, lfc_b = gate_logs(gates_ctx)
    state0 = (jnp.zeros((B, ML_HEADS, ML_QK_DIM, ML_V_DIM), f32),
              jnp.zeros((B, ML_HEADS, ML_QK_DIM), f32),
              jnp.zeros((B, ML_HEADS), f32))
    st_f = _mlstm_chunkwise(None, k_ctx, v_ctx, lic_f, lfc_f, state0)
    h_f = _mlstm_chunkwise(q, k, v, li_f, lf_f, st_f)
    st_b = _mlstm_chunkwise(None, flip(k_ctx), flip(v_ctx), flip(lic_b), flip(lfc_b), state0)
    h_b = flip(_mlstm_chunkwise(flip(q), flip(k), flip(v), flip(li_b), flip(lf_b), st_b))
    h = heads_first(h_f + h_b)
    h = h * lax.rsqrt(jnp.mean(h * h, axis=-1, keepdims=True) + NORM_EPS) * g_head.reshape(ML_HEADS, ML_V_DIM).astype(f32)
    return (jax.nn.sigmoid(o_pre.astype(f32)) * h.reshape(B, S, ML_WIDTH)).astype(o_pre.dtype)

def _clamped_swiglu(g, l):
    g = jnp.minimum(g, SWIGLU_LIMIT)
    l = jnp.clip(l, -SWIGLU_LIMIT, SWIGLU_LIMIT)
    return g * jax.nn.sigmoid(SWIGLU_ALPHA * g) * (l + 1.0)

def _moe_ffn(h, w_router, b_router, w_gate, b_gate, w_lin, b_lin, w_down, b_down):
    B, S, D = h.shape
    n_tok = B * S
    n_assign = n_tok * TOP_K
    xf = h.reshape(n_tok, D)
    logits = (xf @ w_router + b_router).astype(jnp.float32)
    top_logit, top_e = lax.top_k(logits, TOP_K)
    top_w = jax.nn.softmax(top_logit, axis=-1)
    e_flat = top_e.reshape(-1)
    order = jnp.argsort(e_flat)
    e_sorted = e_flat[order]
    counts = jnp.bincount(e_flat, length=N_EXPERTS)
    padded = (counts + EXPERT_BLOCK - 1) // EXPERT_BLOCK * EXPERT_BLOCK
    pad_end = jnp.cumsum(padded)
    pad_start = pad_end - padded
    start = jnp.cumsum(counts) - counts
    dest = pad_start[e_sorted] + jnp.arange(n_assign) - start[e_sorted]
    n_rows = -(-n_assign // EXPERT_BLOCK) * EXPERT_BLOCK + N_EXPERTS * EXPERT_BLOCK
    n_blocks = n_rows // EXPERT_BLOCK
    row_tok = jnp.full((n_rows,), n_tok, jnp.int32).at[dest].set((order // TOP_K).astype(jnp.int32))
    row_w = jnp.zeros((n_rows,), jnp.float32).at[dest].set(top_w.reshape(-1)[order])
    blk_start = jnp.arange(n_blocks) * EXPERT_BLOCK
    blk_e = jnp.minimum(jnp.sum(blk_start[:, None] >= pad_end[None, :], axis=1), N_EXPERTS - 1)
    x_pad = jnp.concatenate([xf, jnp.zeros((1, D), xf.dtype)], axis=0)

    def expert_block(args):
        idx, wts, e = args
        xb = x_pad[idx]
        a = _clamped_swiglu(xb @ w_gate[e] + b_gate[e], xb @ w_lin[e] + b_lin[e])
        y = a @ w_down[e] + b_down[e]
        return (y * wts[:, None]).astype(h.dtype)

    y = lax.map(expert_block, (row_tok.reshape(n_blocks, EXPERT_BLOCK),
                               row_w.reshape(n_blocks, EXPERT_BLOCK), blk_e))
    out = jnp.zeros((n_tok + 1, D), h.dtype).at[row_tok].add(y.reshape(n_rows, D))
    return out[:n_tok].reshape(B, S, D)

def second_inputs(seed: int = 0) -> dict:
    key = jax.random.key(seed)
    ks = jax.random.split(key, 28)
    f32 = jnp.float32
    D, E, F = D_MODEL, N_EXPERTS, D_EXPERT

    def nrm(k, shape, scale):
        return scale * jax.random.normal(k, shape, f32)

    def gain(k, shape):
        return 1.0 + 0.02 * jax.random.normal(k, shape, f32)

    f_bias = 3.0 + 3.0 * jax.random.uniform(ks[11], (DEPTH_2, 2, ML_HEADS), f32)
    i_bias = nrm(ks[12], (DEPTH_2, 2, ML_HEADS), 0.1)
    b_mlstm_gates = jnp.stack([i_bias[:, 0], f_bias[:, 0], i_bias[:, 1], f_bias[:, 1]], axis=1)
    return {
        'x': jax.random.normal(ks[0], (BATCH, SEQ, D), f32),
        'c': jax.random.normal(ks[1], (BATCH, D), f32),
        'ctx': jax.random.normal(ks[2], (BATCH, CTX_LEN, D), f32),
        'c_ctx': jax.random.normal(ks[3], (D,), f32),
        'w_ada': nrm(ks[4], (DEPTH_2, D, 6 * D), 0.5 * D ** -0.5),
        'b_ada': nrm(ks[5], (DEPTH_2, 6 * D), 0.02),
        'g_mix_pre': gain(ks[6], (DEPTH_2, D)),
        'g_mix_post': gain(ks[7], (DEPTH_2, D)),
        'g_ffn_pre': gain(ks[8], (DEPTH_2, D)),
        'g_ffn_post': gain(ks[9], (DEPTH_2, D)),
        'w_in': nrm(ks[10], (DEPTH_2, D, N_IN_COLS), D ** -0.5),
        'b_mlstm_gates': b_mlstm_gates,
        'rpb': nrm(ks[13], (DEPTH_2, NA_HEADS, 2 * WIN_H - 1, 2 * WIN_W - 1), 0.1),
        'g_mlstm_head': gain(ks[14], (DEPTH_2, ML_WIDTH)),
        'w_branch_na': nrm(ks[15], (DEPTH_2, NA_WIDTH, D), NA_WIDTH ** -0.5),
        'w_branch_ml': nrm(ks[16], (DEPTH_2, ML_WIDTH, D), ML_WIDTH ** -0.5),
        'w_out': nrm(ks[17], (DEPTH_2, D, D), D ** -0.5),
        'w_router': nrm(ks[18], (DEPTH_2, D, E), D ** -0.5),
        'b_router': nrm(ks[19], (DEPTH_2, E), 0.01),
        'w_gate': nrm(ks[20], (DEPTH_2, E, D, F), D ** -0.5),
        'b_gate': nrm(ks[21], (DEPTH_2, E, F), 0.01),
        'w_lin': nrm(ks[22], (DEPTH_2, E, D, F), D ** -0.5),
        'b_lin': nrm(ks[23], (DEPTH_2, E, F), 0.01),
        'w_down': nrm(ks[24], (DEPTH_2, E, F, D), F ** -0.5),
        'b_down': nrm(ks[25], (DEPTH_2, E, D), 0.01),
    }

def second_block(x, c, ctx, c_ctx, w_ada, b_ada, g_mix_pre, g_mix_post, g_ffn_pre, g_ffn_post,
              w_in, b_mlstm_gates, rpb, g_mlstm_head, w_branch_na, w_branch_ml, w_out,
              w_router, b_router, w_gate, b_gate, w_lin, b_lin, w_down, b_down):
    B, S, D = x.shape
    t = jnp.arange(S)
    row = (t // GRID_W).astype(jnp.float32)
    col = (t % GRID_W).astype(jnp.float32)
    silu_c = jax.nn.silu(c)
    silu_cc = jax.nn.silu(c_ctx)
    for layer in range(DEPTH_2):
        mod = silu_c @ w_ada[layer] + b_ada[layer]
        sh_m, sc_m, gt_m, sh_f, sc_f, gt_f = jnp.split(mod, 6, axis=-1)
        mod_c = silu_cc @ w_ada[layer][:, :2 * D] + b_ada[layer][:2 * D]
        sh_c, sc_c = jnp.split(mod_c, 2, axis=-1)

        h = _rmsnorm_2(x, g_mix_pre[layer]) * (1.0 + sc_m[:, None]) + sh_m[:, None]
        hc = _rmsnorm_2(ctx, g_mix_pre[layer]) * (1.0 + sc_c) + sh_c
        (na_k, na_v, ml_k, ml_v, ml_g, na_q, ml_q, ml_o, gate_na, gate_ml) = _split(h @ w_in[layer], IN_SPLITS)
        (na_kc, na_vc, ml_kc, ml_vc, ml_gc) = _split(hc @ w_in[layer][:, :N_CTX_COLS], CTX_SPLITS)
        o_na = _neighbourhood_attention(na_q, na_k, na_v, na_kc, na_vc, rpb[layer])
        o_ml = _mlstm_branch(ml_q, ml_k, ml_v, ml_o, ml_g, ml_kc, ml_vc, ml_gc,
                             b_mlstm_gates[layer], g_mlstm_head[layer], row, col)
        merged = (jax.nn.sigmoid(gate_na) * (o_na @ w_branch_na[layer])
                  + jax.nn.sigmoid(gate_ml) * (o_ml @ w_branch_ml[layer]))
        x = x + gt_m[:, None] * _rmsnorm_2(merged @ w_out[layer], g_mix_post[layer])

        h2 = _rmsnorm_2(x, g_ffn_pre[layer]) * (1.0 + sc_f[:, None]) + sh_f[:, None]
        ffn = _moe_ffn(h2, w_router[layer], b_router[layer], w_gate[layer], b_gate[layer],
                       w_lin[layer], b_lin[layer], w_down[layer], b_down[layer])
        x = x + gt_f[:, None] * _rmsnorm_2(ffn, g_ffn_post[layer])
    return x


def setup_inputs(seed=0):
    out = dict(first_inputs(seed))
    for name, value in second_inputs(seed + 1).items():
        if name != "x":
            out[name + "_2"] = value
    return out


def reference(
    x, rel_bias, ffn1_norm, ffn1_w_gate, ffn1_w_up, ffn1_w_down, mix_norm, w_in, b_forget,
    conf_dw, conf_dw_b, conf_ln_g, conf_ln_b, conf_w_out, sc_conv, sc_w_out, swa_q_norm,
    swa_k_norm, swa_sink, swa_w_o, fox_q_norm, fox_k_norm, fox_w_o, w_out, ffn2_norm,
    ffn2_w_gate, ffn2_w_up, ffn2_w_down, c_2, ctx_2, c_ctx_2, w_ada_2, b_ada_2, g_mix_pre_2,
    g_mix_post_2, g_ffn_pre_2, g_ffn_post_2, w_in_2, b_mlstm_gates_2, rpb_2, g_mlstm_head_2,
    w_branch_na_2, w_branch_ml_2, w_out_2, w_router_2, b_router_2, w_gate_2, b_gate_2, w_lin_2,
    b_lin_2, w_down_2, b_down_2,
):
    x = first_block(
        x, rel_bias, ffn1_norm, ffn1_w_gate, ffn1_w_up, ffn1_w_down, mix_norm, w_in, b_forget,
        conf_dw, conf_dw_b, conf_ln_g, conf_ln_b, conf_w_out, sc_conv, sc_w_out, swa_q_norm,
        swa_k_norm, swa_sink, swa_w_o, fox_q_norm, fox_k_norm, fox_w_o, w_out, ffn2_norm,
        ffn2_w_gate, ffn2_w_up, ffn2_w_down,
    )
    return second_block(
        x, c_2, ctx_2, c_ctx_2, w_ada_2, b_ada_2, g_mix_pre_2, g_mix_post_2, g_ffn_pre_2,
        g_ffn_post_2, w_in_2, b_mlstm_gates_2, rpb_2, g_mlstm_head_2, w_branch_na_2,
        w_branch_ml_2, w_out_2, w_router_2, b_router_2, w_gate_2, b_gate_2, w_lin_2, b_lin_2,
        w_down_2, b_down_2,
    )


_drawn_inputs = setup_inputs


def setup_inputs(seed=0):
    import zlib

    import numpy as np

    out = dict(_drawn_inputs(seed))
    spreads = {}
    factors = {'conf_ln_b': 3.665,
     'swa_q_norm': 3.994,
     'swa_k_norm': 5.532,
     'swa_sink': 4.975,
     'fox_q_norm': 3.669,
     'fox_k_norm': 3.429,
     'g_mix_pre_2': 3.087,
     'g_mix_post_2': 7.282,
     'g_ffn_post_2': 8.0,
     'rpb_2': 6.455,
     'g_mlstm_head_2': 8.0,
     'b_router_2': 4.187,
     'b_gate_2': 8.0,
     'b_lin_2': 8.0,
     'b_down_2': 8.0}
    for name, (base, spread) in spreads.items():
        noise = np.random.default_rng([zlib.crc32(name.encode()), seed]).standard_normal(out[name].shape)
        drawn = base * np.exp(spread * noise) if base else spread * noise
        out[name] = __import__('jax').numpy.asarray(drawn.astype(out[name].dtype))
    for name, factor in factors.items():
        out[name] = (out[name] * factor).astype(out[name].dtype)
    return out
```

```python
from contextlib import ExitStack, contextmanager

import numpy as np
import concourse.bass as bass
from concourse import mybir

F32 = mybir.dt.float32
I32 = mybir.dt.int32
ALU = mybir.AluOpType
ACT = mybir.ActivationFunctionType
AX = mybir.AxisListType.X

P = 128
D = 1024
KD = D // P
T = 256
TC = T // P
DEPTH = 2
FF = 2816
FC = FF // P
ZC = 20
GC = 32
HD = 64
CONV_K = 31
SC_K = 3
WINDOW = 128
N_BUCKETS = 32
EPS = 1e-6
NEG = -1e30

GRID_W = 64
ROWS = T // GRID_W
NA_HEADS = 8
WIN_H = 8
WIN_W = 16
ML_HEADS = 4
CAP = 15.0
CX = 14
LX = 10
G2 = 16
E = 32
TOPK = 4
SLOTS = 64
PER = T // SLOTS
ALPHA = 1.702
LIMIT = 7.0
NT2 = 2 * T


def _constants():
    parts, at = {}, {}

    def put(name, a):
        full = np.zeros((P, int(np.prod(a.shape[1:]))), np.float32)
        full[:a.shape[0]] = a.reshape(a.shape[0], -1)
        parts[name] = (full, a.shape)

    i = np.arange(P)
    u = np.arange(T).reshape(TC, P).T[:, :, None]
    s = np.arange(T)[None, None, :]
    put("ident", np.eye(P, dtype=np.float32))
    put("mean_d", np.full((P, P), 1.0 / D))
    put("slots", np.tile(np.arange(SLOTS, dtype=np.float32), (P, 2)))
    put("ones", np.ones((P, P)))
    put("mean_conv", np.full((P, P), 1.0 / 256))
    put("mean_head", np.full((P, P), 1.0 / P))
    put("zeros", np.zeros((P, 512)))
    heads = np.zeros((P, 7, 14))
    for c in range(7):
        heads[:HD, c, 2 * c] = heads[HD:, c, 2 * c + 1] = 1.0 / HD
    put("head_mean", heads)
    spread = np.zeros((14, 7, P))
    for c in range(7):
        spread[2 * c, c, :HD] = spread[2 * c + 1, c, HD:] = 1.0
    put("head_spread", spread)
    one = np.ones((P, TC, T))
    put("after", np.concatenate([(u > s), one], 2))
    put("before", np.concatenate([(u < s), one], 2))
    put("upto", (u <= s))
    put("from", (u >= s))
    put("causal", np.where(s <= u, 0.0, NEG))
    put("anticausal", np.where(s >= u, 0.0, NEG))
    dist = i[:, None] + P - np.arange(2 * P)[None, :]
    own = np.where((dist >= 0) & (dist < WINDOW), 0.0, NEG)
    first = np.full((P, T), NEG)
    first[:, :P] = own[:, P:]
    put("window", np.stack([first, own], 1))
    d = 255 - np.arange(2 * T - 1)
    dd = np.clip(d, 0, WINDOW - 1)
    half = N_BUCKETS // 2
    dm = np.maximum(dd, 1).astype(np.float32)
    large = half + (np.log(dm / np.float32(half)) / np.float32(np.log(P / half)) * np.float32(N_BUCKETS - half)).astype(np.int32)
    bucket = np.where(dd < half, dd, np.minimum(large, N_BUCKETS - 1))
    line = (bucket[None, :] == np.arange(N_BUCKETS)[:, None]).astype(np.float32)
    put("bucket", np.concatenate([line, np.zeros((N_BUCKETS, 1))], 1))
    cs = np.clip(np.arange(GRID_W) - WIN_W // 2, 0, GRID_W - WIN_W)[i % GRID_W][:, None]
    kc = np.arange(GRID_W)[None, :]
    put("na_mask", np.tile(np.where((kc >= cs) & (kc < cs + WIN_W), 0.0, NEG), (1, ROWS)))
    n_freq = HD // 4
    inv = np.float32(10000.0) ** (-np.arange(n_freq, dtype=np.float32) / n_freq)
    t = np.arange(T)
    ang = np.zeros((P, T), np.float32)
    turn = np.zeros((P, P))
    for p in range(P):
        pos = t // GRID_W if (p % HD) < HD // 2 else t % GRID_W
        ang[p] = pos.astype(np.float32) * inv[p % n_freq]
        if p % (2 * n_freq) < n_freq:
            turn[p + n_freq, p] = -1.0
        else:
            turn[p - n_freq, p] = 1.0
    put("cos", np.cos(ang))
    put("sin", np.sin(ang))
    put("turn", turn)
    j = np.arange(E)
    put("earlier", np.tile((j[None, :] < j[:, None]).astype(np.float32), (P, 1, 1)))
    put("block_no", np.tile(np.arange(2 * E, dtype=np.float32), (P, 1)))
    n = 0
    for name, (full, shape) in parts.items():
        at[name] = (n, shape)
        n += full.shape[1]
    return np.ascontiguousarray(np.concatenate([f for f, _ in parts.values()], 1).astype(np.float32)), at


VEC = {}
_n = 0
for _name, _w in (("ffn1", 8), ("mix", 8), ("ffn2", 8), ("dw", 2 * CONV_K), ("dw_b", 2), ("ln_g", 2), ("ln_b", 2),
                  ("sc", 2 * SC_K), ("swa_q", 1), ("swa_k", 1), ("fox_q", 1), ("fox_k", 1), ("b_forget", 4), ("sink", 4)):
    VEC[_name] = (_n, _w)
    _n += _w
NVEC = _n
VEC2 = {}
_n = 0
for _name, _w in (("c", 8), ("c_ctx", 8), ("b_ada", 48), ("mix_pre", 8), ("mix_post", 8), ("ffn_pre", 8), ("ffn_post", 8),
                  ("gates", 16), ("head", 4), ("b_router", 32)):
    VEC2[_name] = (_n, _w)
    _n += _w
NVEC2 = _n


PHASES = []


@contextmanager
def phase(nc, names):
    PHASES.append(len(PHASES))
    sems = {n: nc.alloc_semaphore(f"{n}_phase{len(PHASES)}") for n in names.split()}
    with nc.Block() as block:
        yield block, dict(sems)
    nc.clear_and_free_semaphores(list(sems.values()))
    nc.all_engine_barrier()


class Chain:

    def __init__(self, eng, sem):
        self.eng, self.sem, self.n = eng, sem, 0

    def did(self, ins):
        ins.then_inc(self.sem, 1)
        self.n += 1
        return self.n

    def link(self, ins):
        self.did(ins)
        self.eng.wait_ge(self.sem, self.n)


NORM = "sq_ready ms_ready var_ready std_ready h_normed norm_chain "


def norm_act(act, nc, s, x, sq):
    nc.scalar.activation(sq, x, ACT.Square).then_inc(s["sq_ready"], 1)
    act.wait_ge(s["var_ready"], 1)
    nc.scalar.activation(s["std"], s["var"], ACT.Sqrt).then_inc(s["std_ready"], 1)


def norm_pe(pe, nc, s, sq, ms, mean, n):
    pe.wait_ge(s["sq_ready"], 1)
    for k in range(n):
        mm = nc.tensor.matmul(ms, mean, sq[:, k, :], start=(k == 0), stop=(k == n - 1))
    mm.then_inc(s["ms_ready"], 1)


def norm_dve(dve, nc, s, x, h, ms, gain, n):
    dve.wait_ge(s["ms_ready"], 1)
    nc.vector.tensor_scalar(s["var"], ms, EPS, None, ALU.add).then_inc(s["var_ready"], 1)
    dve.wait_ge(s["std_ready"], 1)
    nc.vector.reciprocal(s["rstd"], s["std"]).then_inc(s["norm_chain"], 1)
    dve.wait_ge(s["norm_chain"], 1)
    for k in range(n):
        last = nc.vector.scalar_tensor_tensor(h[:, k, :], x[:, k, :], gain[:, k:k + 1], s["rstd"], ALU.mult, ALU.mult)
    last.then_inc(s["h_normed"], 1)


def project_sems(tag, ring):
    return " ".join(f"{tag}_w{r}" for r in range(ring)) + f" {tag}_mm {tag}_out "


def project_sp(sp, s, tag, wsrc, wbuf, ring, n):
    for r in range(ring):
        sp.dma_start(wbuf[:, r], wsrc(r)).then_inc(s[f"{tag}_w{r}"], 16)
    if n > ring:
        with sp.Fori(1, n // ring) as i:
            for r in range(ring):
                sp.wait_ge(s[f"{tag}_mm"], (i - 1) * ring + r + 1)
                sp.dma_start(wbuf[:, r], wsrc(i * ring + r)).then_inc(s[f"{tag}_w{r}"], 16)


def project_pe(pe, nc, s, tag, wbuf, src, bank, ring, n, tokens):
    def chunk(i, r):
        pe.wait_ge(s[f"{tag}_w{r}"], i * 16 + 16)
        for k in range(KD):
            mm = nc.tensor.matmul(bank(r)[:, 0:tokens], wbuf[:, r, k * P:(k + 1) * P], src[:, k, :],
                                  start=(k == 0), stop=(k == KD - 1))
        mm.then_inc(s[f"{tag}_mm"], 1)

    for r in range(ring):
        chunk(0, r)
    if n > ring:
        with pe.Fori(1, n // ring) as i:
            for r in range(ring):
                pe.wait_ge(s[f"{tag}_out"], (i - 1) * ring + r + 1)
                chunk(i, r)


def project_out(eng, s, tag, move, ring, n):
    with eng.Fori(0, n // ring) as i:
        for r in range(ring):
            eng.wait_ge(s[f"{tag}_mm"], i * ring + r + 1)
            move(i * ring + r, r).then_inc(s[f"{tag}_out"], 1)


def ffn_phase(nc, B, l, wg, wu, wd, gain):
    x, h, sq, ps, con = B.x, B.h, B.sq, B.ps, B.con
    acc = ps[:, 0:4, :].rearrange("p b (c t) -> p (b c) t", t=T)
    gu = [ps[:, 4 + a, :].rearrange("p (w t) -> p w t", t=T) for a in range(2)]
    ms = ps[:, 6, 0:T]
    with phase(nc, NORM + "wg0 wg1 wu0 wu1 wd0 wd1 cleared gu_done silu_done hidden_ready down_done x_done") as (block, s):
        s.update(std=B.std[:, 0:T], var=B.var[:, 0:T], rstd=B.rstd[:, 0:T])

        @block.sync
        def _(sp):
            def load(c, a):
                sp.dma_start(B.wg[:, a], wg[l, c]).then_inc(s[f"wg{a}"], 16)
                sp.dma_start(B.wu[:, a], wu[l, c]).then_inc(s[f"wu{a}"], 16)

            for a in range(2):
                load(a, a)
                sp.dma_start(B.wd[:, a], wd[l, a]).then_inc(s[f"wd{a}"], 16)
            with sp.Fori(1, FC // 2) as i:
                for a in range(2):
                    sp.wait_ge(s["gu_done"], 2 * i + (a - 1))
                    load(2 * i + a, a)
                    sp.wait_ge(s["down_done"], 2 * i + (a - 1))
                    sp.dma_start(B.wd[:, a], wd[l, 2 * i + a]).then_inc(s[f"wd{a}"], 16)

        @block.tensor
        def _(pe):
            for b in range(4):
                nc.tensor.matmul(ps[:, b, :], con("zeros")[:, 0:P], con("zeros"), start=True, stop=False,
                                 skip_group_check=True)
            norm_pe(pe, nc, s, sq, ms, con("mean_d"), KD)
            pe.wait_ge(s["h_normed"], 1)

            def gate_up(i, a):
                pe.wait_ge(s[f"wg{a}"], i * 16 + 16)
                for k in range(KD):
                    nc.tensor.matmul(gu[a][:, 0, :], B.wg[:, a, k * P:(k + 1) * P], h[:, k, :],
                                     start=(k == 0), stop=(k == KD - 1), skip_group_check=True)
                pe.wait_ge(s[f"wu{a}"], i * 16 + 16)
                for k in range(KD):
                    mm = nc.tensor.matmul(gu[a][:, 1, :], B.wu[:, a, k * P:(k + 1) * P], h[:, k, :],
                                          start=(k == 0), stop=(k == KD - 1), skip_group_check=True)
                mm.then_inc(s["gu_done"], 1)

            def down(i, a):
                pe.wait_ge(s["hidden_ready"], 2 * i + (a + 1))
                pe.wait_ge(s[f"wd{a}"], i * 16 + 16)
                for c in range(KD):
                    mm = nc.tensor.matmul(acc[:, c, :], B.wd[:, a, c * P:(c + 1) * P], B.hid[:, a, :],
                                          start=False, stop=False, skip_group_check=True)
                mm.then_inc(s["down_done"], 1)

            gate_up(0, 0)
            gate_up(0, 1)
            down(0, 0)
            with pe.Fori(1, FC // 2) as i:
                pe.wait_ge(s["hidden_ready"], 2 * i - 1)
                gate_up(i, 0)
                down(i - 1, 1)
                pe.wait_ge(s["hidden_ready"], 2 * i)
                gate_up(i, 1)
                down(i, 0)
            down(FC // 2 - 1, 1)

        @block.scalar
        def _(act):
            norm_act(act, nc, s, x, sq)

            def silu(a):
                nc.scalar.activation(B.sil[:, a, :], gu[a][:, 0, :], ACT.Silu).then_inc(s["silu_done"], 1)

            for a in range(2):
                act.wait_ge(s["gu_done"], a + 1)
                silu(a)
            with act.Fori(1, FC // 2) as i:
                for a in range(2):
                    act.wait_ge(s["gu_done"], 2 * i + (a + 1))
                    act.wait_ge(s["hidden_ready"], 2 * i + (a - 1))
                    silu(a)

        @block.vector
        def _(dve):
            norm_dve(dve, nc, s, x, h, ms, gain, KD)

            def hidden(a):
                nc.vector.tensor_tensor(B.hid[:, a, :], B.sil[:, a, :], gu[a][:, 1, :],
                                        ALU.mult).then_inc(s["hidden_ready"], 1)

            for a in range(2):
                dve.wait_ge(s["silu_done"], a + 1)
                hidden(a)
            with dve.Fori(1, FC // 2) as i:
                for a in range(2):
                    dve.wait_ge(s["silu_done"], 2 * i + (a + 1))
                    dve.wait_ge(s["down_done"], 2 * i + (a - 1))
                    hidden(a)
            dve.wait_ge(s["down_done"], FC)
            for b in range(4):
                nc.vector.scalar_tensor_tensor(x[:, 2 * b:2 * b + 2, :], acc[:, 2 * b:2 * b + 2, :], 0.5,
                                               x[:, 2 * b:2 * b + 2, :], ALU.mult, ALU.add).then_inc(s["x_done"], 1)
            dve.wait_ge(s["x_done"], 4)


def z_phase(nc, B, l, w_z, gain):
    ps, con = B.ps, B.con
    ring = 4
    with phase(nc, NORM + project_sems("z", ring) + "ff_w ff_mm ff_out") as (block, s):
        s.update(std=B.std[:, 0:T], var=B.var[:, 0:T], rstd=B.rstd[:, 0:T])

        @block.sync
        def _(sp):
            sp.dma_start(B.w_ff, B.d_wff[l]).then_inc(s["ff_w"], 16)
            project_sp(sp, s, "z", lambda c: w_z[l, c], B.ring4, ring, ZC)

        @block.tensor
        def _(pe):
            norm_pe(pe, nc, s, B.sq, ps[:, 6, 0:T], con("mean_d"), KD)
            pe.wait_ge(s["h_normed"], 1)
            pe.wait_ge(s["ff_w"], 16)
            for c in range(TC):
                for k in range(KD):
                    mm = nc.tensor.matmul(ps[:, 7, 4 * c:4 * c + 4], B.h[:, k, c * P:(c + 1) * P],
                                          B.w_ff[:, k, :], start=(k == 0), stop=(k == KD - 1))
            mm.then_inc(s["ff_mm"], 1)
            project_pe(pe, nc, s, "z", B.ring4, B.h, lambda r: ps[:, r, :], ring, ZC, T)

        @block.scalar
        def _(act):
            norm_act(act, nc, s, B.x, B.sq)
            project_out(act, s, "z", lambda c, r: nc.scalar.copy(B.z[:, c, :], ps[:, r, 0:T]), ring, ZC)

        @block.vector
        def _(dve):
            norm_dve(dve, nc, s, B.x, B.h, ps[:, 6, 0:T], gain, KD)
            dve.wait_ge(s["ff_mm"], 1)
            nc.vector.tensor_copy(B.ff, ps[:, 7, 0:8]).then_inc(s["ff_out"], 1)
            dve.wait_ge(s["ff_out"], 1)


CA, CB, SB, SC, SX, AQ, AK, AV, FQ, FK, FV = 0, 2, 4, 6, 8, 10, 12, 13, 14, 16, 18


def branch_phase(nc, B, l, w_g):
    ps, con, z, vec = B.ps, B.con, B.z, B.vec
    ring = 4
    v = lambda name, j=0, n=1: vec[:, VEC[name][0] + j:VEC[name][0] + j + n]
    with phase(nc, project_sems("g", ring) + "qk_sq qk_ms qk_var qk_std qk_rstd qk_spread v_turned v_copied sig "
               "ff_in ff_exp ff_in2 ff_ln conv_done conv_sq cen_in mean cen var std ln_in silu chain done") as (block, s):
        msq = ps[0:14, 6, 0:T]

        @block.sync
        def _(sp):
            project_sp(sp, s, "g", lambda c: w_g[l, c], B.ring4, ring, GC)

        @block.tensor
        def _(pe):
            pe.wait_ge(s["qk_sq"], 2)
            for c in range(7):
                mm = nc.tensor.matmul(msq, con("head_mean")[:, c, :], B.qksq[:, c, :], start=(c == 0), stop=(c == 6))
            mm.then_inc(s["qk_ms"], 1)
            for j, c in enumerate((AV, FV, FV + 1)):
                for t in range(TC):
                    n = j * TC + t
                    mm = nc.tensor.transpose(ps[:, 4 + n // 4, (n % 4) * P:(n % 4 + 1) * P],
                                             z[:, c, t * P:(t + 1) * P], con("ident"))
            mm.then_inc(s["v_turned"], 1)
            pe.wait_ge(s["qk_rstd"], 1)
            for c in range(7):
                mm = nc.tensor.matmul(ps[:, c // 2, (c % 2) * T:(c % 2 + 1) * T], con("head_spread")[0:14, c, :],
                                      B.hrstd[0:14, :], start=(c % 2 == 0), stop=True, skip_group_check=True)
            mm.then_inc(s["qk_spread"], 1)
            pe.wait_ge(s["done"], 1)
            project_pe(pe, nc, s, "g", B.ring4, B.h, lambda r: ps[:, r, :], ring, GC, T)
            pe.wait_ge(s["conv_done"], 1)
            for c in range(2):
                mm = nc.tensor.matmul(ps[:, 4, 0:T], con("mean_conv"), B.u[:, c, :], start=(c == 0), stop=(c == 1))
            mm.then_inc(s["mean"], 1)
            pe.wait_ge(s["conv_sq"], 1)
            for c in range(2):
                mm = nc.tensor.matmul(ps[:, 5, 0:T], con("mean_conv"), B.sq[:, c, :], start=(c == 0), stop=(c == 1))
            mm.then_inc(s["var"], 1)

        @block.scalar
        def _(act):
            nc.scalar.activation(B.qksq[:, 0:3, :], z[:, AQ:AQ + 3, :], ACT.Square).then_inc(s["qk_sq"], 1)
            nc.scalar.activation(B.qksq[:, 3:7, :], z[:, FQ:FQ + 4, :], ACT.Square).then_inc(s["qk_sq"], 1)
            nc.scalar.activation(B.u, z[:, CB:CB + 2, :], ACT.Sigmoid).then_inc(s["sig"], 1)
            act.wait_ge(s["qk_var"], 1)
            nc.scalar.activation(B.hstd[0:14, :], B.hvar[0:14, :], ACT.Sqrt).then_inc(s["qk_std"], 1)
            act.wait_ge(s["ff_in"], 1)
            nc.scalar.activation(B.ffe, B.ffn_, ACT.Exp).then_inc(s["ff_exp"], 1)
            act.wait_ge(s["ff_in2"], 1)
            nc.scalar.activation(B.ffn_, B.ffe, ACT.Ln).then_inc(s["ff_ln"], 1)
            project_out(act, s, "g", lambda c, r: nc.scalar.activation(B.gates[:, c, :], ps[:, r, 0:T], ACT.Sigmoid),
                        ring, GC)
            act.wait_ge(s["cen"], 1)
            nc.scalar.activation(B.sq[:, 0:2, :], B.u, ACT.Square).then_inc(s["conv_sq"], 1)
            act.wait_ge(s["cen_in"], 1)
            nc.scalar.activation(B.std[:, 0:T], B.var[:, 0:T], ACT.Sqrt).then_inc(s["std"], 1)
            act.wait_ge(s["ln_in"], 1)
            nc.scalar.activation(B.b_conf, B.u, ACT.Silu).then_inc(s["silu"], 1)
            act.wait_ge(s["silu"], 1)

        @block.vector
        def _(dve):
            ch = Chain(dve, s["chain"])
            dve.wait_ge(s["qk_ms"], 1)
            nc.vector.tensor_scalar(B.hvar[0:14, :], msq, EPS, None, ALU.add).then_inc(s["qk_var"], 1)
            for t in range(TC):
                ch.did(nc.vector.tensor_tensor(B.ff[:, 4 * t:4 * t + 4], B.ff[:, 4 * t:4 * t + 4], v("b_forget", 0, 4), ALU.add))
            dve.wait_ge(s["chain"], ch.n)
            ch.link(nc.vector.tensor_scalar(B.ffe, B.ff, -1.0, None, ALU.mult))
            nc.vector.tensor_tensor(B.ffn_, B.ff, B.ffe, ALU.min).then_inc(s["ff_in"], 1)
            dve.wait_ge(s["qk_std"], 1)
            nc.vector.reciprocal(B.hrstd[0:14, :], B.hstd[0:14, :]).then_inc(s["qk_rstd"], 1)
            dve.wait_ge(s["ff_exp"], 1)
            ch.link(nc.vector.tensor_scalar(B.ffe, B.ffe, 1.0, None, ALU.add))
            nc.vector.tensor_scalar(B.ff, B.ff, 0.0, None, ALU.min).then_inc(s["ff_in2"], 1)
            dve.wait_ge(s["v_turned"], 1)
            for j in range(3):
                for t in range(TC):
                    n = j * TC + t
                    last = nc.vector.tensor_copy(B.vtok[:, t, j * P:(j + 1) * P],
                                                 ps[:, 4 + n // 4, (n % 4) * P:(n % 4 + 1) * P])
            last.then_inc(s["v_copied"], 1)
            for j, name in ((0, "swa_q"), (1, "fox_q")):
                ch.link(nc.vector.tensor_scalar(B.qgain[:, j:j + 1], v(name), HD ** -0.5, None, ALU.mult))
            dve.wait_ge(s["qk_spread"], 1)
            for c, (zc, g) in enumerate(((AQ, B.qgain[:, 0:1]), (AQ + 1, B.qgain[:, 0:1]), (AK, v("swa_k")),
                                         (FQ, B.qgain[:, 1:2]), (FQ + 1, B.qgain[:, 1:2]), (FK, v("fox_k")),
                                         (FK + 1, v("fox_k")))):
                ch.did(nc.vector.scalar_tensor_tensor(z[:, zc, :], z[:, zc, :], g, ps[:, c // 2, (c % 2) * T:(c % 2 + 1) * T],
                                                      ALU.mult, ALU.mult))
            dve.wait_ge(s["chain"], ch.n)
            for g in range(2):
                for half in range(2):
                    last = nc.vector.tensor_copy(B.kdup[half * HD:(half + 1) * HD, g, :], z[g * HD:(g + 1) * HD, AK, :])
            last.then_inc(s["done"], 1)
            dve.wait_ge(s["ff_ln"], 1)
            ch.link(nc.vector.tensor_tensor(B.ff, B.ff, B.ffn_, ALU.subtract))
            for h in range(4):
                ch.did(nc.vector.tensor_scalar(B.lfa0[:, h, :], con("upto")[:, 0, :], B.ff[:, h:h + 1], None, ALU.mult))
                ch.did(nc.vector.tensor_scalar(B.lfa1[:, h, :], con("upto")[:, 1, P:T], B.ff[:, 4 + h:5 + h], None, ALU.mult))
            pad = CONV_K - 1
            for c in range(2):
                ch.did(nc.vector.memset(B.upad[:, c, 0:pad], 0.0))
            ch.did(nc.vector.tensor_tensor(B.upad[:, :, pad:], z[:, SC:SC + 2, :], z[:, SX:SX + 2, :], ALU.mult))
            dve.wait_ge(s["chain"], ch.n)
            for j in range(SC_K):
                for c in range(2):
                    w = v("sc", c * SC_K + j)
                    x_in = B.upad[:, c, pad - SC_K + 1 + j:pad - SC_K + 1 + j + T]
                    if j == 0:
                        ch.did(nc.vector.tensor_scalar(B.b_sc[:, c, :], x_in, w, None, ALU.mult))
                    else:
                        dve.wait_ge(s["chain"], ch.n - 1)
                        ch.did(nc.vector.scalar_tensor_tensor(B.b_sc[:, c, :], x_in, w, B.b_sc[:, c, :], ALU.mult, ALU.add))
            dve.wait_ge(s["chain"], ch.n)
            ch.did(nc.vector.tensor_tensor(B.b_sc, B.b_sc, z[:, SB:SB + 2, :], ALU.mult))
            dve.wait_ge(s["sig"], 1)
            ch.link(nc.vector.tensor_tensor(B.upad[:, :, pad:], z[:, CA:CA + 2, :], B.u, ALU.mult))
            for j in range(CONV_K):
                for c in range(2):
                    w = v("dw", c * CONV_K + j)
                    x_in = B.upad[:, c, j:j + T]
                    if j == 0:
                        ch.did(nc.vector.tensor_scalar(B.u[:, c, :], x_in, w, v("dw_b", c), ALU.mult, ALU.add))
                    else:
                        dve.wait_ge(s["chain"], ch.n - 1)
                        ch.did(nc.vector.scalar_tensor_tensor(B.u[:, c, :], x_in, w, B.u[:, c, :], ALU.mult, ALU.add))
            dve.wait_ge(s["chain"], ch.n)
            dve.sem_inc(s["conv_done"], 1)
            dve.wait_ge(s["mean"], 1)
            for c in range(2):
                ch.did(nc.vector.tensor_tensor(B.u[:, c, :], B.u[:, c, :], ps[:, 4, 0:T], ALU.subtract))
            dve.wait_ge(s["chain"], ch.n)
            dve.sem_inc(s["cen"], 1)
            dve.wait_ge(s["var"], 1)
            nc.vector.tensor_scalar(B.var[:, 0:T], ps[:, 5, 0:T], EPS, None, ALU.add).then_inc(s["cen_in"], 1)
            dve.wait_ge(s["std"], 1)
            ch.link(nc.vector.reciprocal(B.rstd[:, 0:T], B.std[:, 0:T]))
            for c in range(2):
                ch.did(nc.vector.scalar_tensor_tensor(B.u[:, c, :], B.u[:, c, :], v("ln_g", c), B.rstd[:, 0:T],
                                                      ALU.mult, ALU.mult))
            dve.wait_ge(s["chain"], ch.n)
            for c in range(2):
                ch.did(nc.vector.tensor_scalar(B.u[:, c, :], B.u[:, c, :], v("ln_b", c), None, ALU.add))
            dve.wait_ge(s["chain"], ch.n)
            dve.sem_inc(s["ln_in"], 1)


def attention_phase(nc, B, units, width):
    ps, con = B.ps, B.con
    n = len(units)
    with phase(nc, "scores_ready max_ready exp_ready probs_ready turned probs_t_ready out_ready out_copied chain sink_ready") as (block, s):

        @block.tensor
        def _(pe):
            def scores(u):
                if u >= 2:
                    pe.wait_ge(s["max_ready"], u - 1)
                units[u]["scores"](ps[:, u % 2, 0:width]).then_inc(s["scores_ready"], 1)

            def turn(u):
                pe.wait_ge(s["probs_ready"], u + 1)
                if u >= 2:
                    pe.wait_ge(s["probs_t_ready"], u - 1)
                for j in range(width // P):
                    mm = nc.tensor.transpose(ps[:, 2 + u % 2, j * P:(j + 1) * P], B.prob[:, u % 2, j * P:(j + 1) * P],
                                             con("ident"))
                mm.then_inc(s["turned"], 1)

            def values(u):
                pe.wait_ge(s["probs_t_ready"], u + 1)
                if u >= 2:
                    pe.wait_ge(s["out_copied"], u - 1)
                v = units[u]["values"]
                lo = units[u]["row"]
                for j, vj in enumerate(v):
                    mm = nc.tensor.matmul(ps[lo:lo + HD, 4 + u % 2, 0:P], vj, B.prob_t[:, u % 2, j * P:(j + 1) * P],
                                          start=(j == 0), stop=(j == len(v) - 1))
                mm.then_inc(s["out_ready"], 1)

            scores(0)
            for u in range(n):
                if u + 1 < n:
                    scores(u + 1)
                turn(u)
                values(u)

        @block.scalar
        def _(act):
            def turned_copy(u):
                act.wait_ge(s["turned"], u + 1)
                if u >= 2:
                    act.wait_ge(s["out_ready"], u - 1)
                nc.scalar.copy(B.prob_t[:, u % 2, 0:width], ps[:, 2 + u % 2, 0:width]).then_inc(s["probs_t_ready"], 1)

            for u in range(n + 1):
                if u < n:
                    act.wait_ge(s["max_ready"], u + 1)
                    if units[u]["sink"] is not None:
                        nc.scalar.activation(B.stat[:, u % 2, 2:3], units[u]["sink"], ACT.Exp, bias=B.stat[:, u % 2, 0:1])
                    nc.scalar.activation(B.prob[:, u % 2, 0:width], B.prob[:, u % 2, 0:width], ACT.Exp,
                                         bias=B.stat[:, u % 2, 0:1], accum_out=B.stat[:, u % 2, 1:2]).then_inc(s["exp_ready"], 1)
                if u >= 1:
                    turned_copy(u - 1)

        @block.vector
        def _(dve):
            ch = Chain(dve, s["chain"])

            def masked_max(u):
                dve.wait_ge(s["scores_ready"], u + 1)
                if u >= 2:
                    dve.wait_ge(s["turned"], u - 1)
                table = units[u]["table"]
                m = table.shape[1]
                ch.did(nc.vector.tensor_tensor(B.prob[:, u % 2, 0:m], ps[:, u % 2, 0:m], table, ALU.add))
                if m < width:
                    ch.did(nc.vector.tensor_copy(B.prob[:, u % 2, m:width], ps[:, u % 2, m:width]))
                dve.wait_ge(s["chain"], ch.n)
                nm = B.stat[:, u % 2, 0:1]
                red = nc.vector.tensor_reduce(nm, B.prob[:, u % 2, 0:width], AX, ALU.max, negate=True)
                if units[u]["sink"] is not None:
                    ch.link(red)
                    red = nc.vector.tensor_tensor(nm, nm, units[u]["minus_sink"], ALU.min)
                red.then_inc(s["max_ready"], 1)

            def norm(u):
                dve.wait_ge(s["exp_ready"], u + 1)
                den = B.stat[:, u % 2, 1:2]
                if units[u]["sink"] is not None:
                    ch.link(nc.vector.tensor_tensor(den, den, B.stat[:, u % 2, 2:3], ALU.add))
                ch.link(nc.vector.reciprocal(B.stat[:, u % 2, 3:4], den))
                nc.vector.tensor_scalar(B.prob[:, u % 2, 0:width], B.prob[:, u % 2, 0:width], B.stat[:, u % 2, 3:4], None,
                                        ALU.mult).then_inc(s["probs_ready"], 1)

            def out(u):
                dve.wait_ge(s["out_ready"], u + 1)
                lo = units[u]["row"]
                nc.vector.tensor_copy(units[u]["out"], ps[lo:lo + HD, 4 + u % 2, 0:P]).then_inc(s["out_copied"], 1)

            for u in range(n + 2):
                if u < n:
                    masked_max(u)
                if 1 <= u <= n:
                    norm(u - 1)
                if u >= 2:
                    out(u - 2)
            dve.wait_ge(s["out_copied"], n)


def first_attention(nc, B):
    ps, con, z = B.ps, B.con, B.z
    units = []
    for h in range(4):
        lo = (h % 2) * HD
        for qc in range(TC):
            def swa(dst, h=h, lo=lo, qc=qc):
                return nc.tensor.matmul(dst, z[lo:lo + HD, AQ + h // 2, qc * P:(qc + 1) * P], B.kdup[lo:lo + HD, h // 2, :],
                                        start=True, stop=True)

            units.append(dict(scores=swa, table=B.swa_table[:, h * TC + qc, :], sink=B.vec[:, VEC["sink"][0] + h:VEC["sink"][0] + h + 1],
                              minus_sink=B.nsink[:, h:h + 1], row=lo,
                              values=[B.vtok[:, t, (h // 2) * HD:(h // 2 + 1) * HD] for t in range(TC)],
                              out=B.b_swa[lo:lo + HD, h // 2, qc * P:(qc + 1) * P]))
    for h in range(4):
        lo = (h % 2) * HD
        for qc in range(TC):
            def fox(dst, h=h, lo=lo, qc=qc):
                nc.tensor.matmul(dst, z[lo:lo + HD, FQ + h // 2, qc * P:(qc + 1) * P], z[lo:lo + HD, FK + h // 2, :],
                                 start=True, stop=False)
                mm = nc.tensor.matmul(dst, B.lfa0[:, h, qc * P:(qc + 1) * P], con("after")[:, 0, 0:T], start=False, stop=(qc == 0))
                if qc == 1:
                    mm = nc.tensor.matmul(dst, B.lfa1[:, h, :], con("after")[:, 1, 0:T], start=False, stop=True)
                return mm

            units.append(dict(scores=fox, table=con("causal")[:, qc, :], sink=None, row=lo,
                              values=[B.vtok[:, t, P + h * HD:P + (h + 1) * HD] for t in range(TC)],
                              out=B.b_fox[lo:lo + HD, h // 2, qc * P:(qc + 1) * P]))
    attention_phase(nc, B, units, T)


def merge_phase(nc, B, wsrc, acts, per, gates, n_branch):
    ps = B.ps
    with phase(nc, "w prod merged chain") as (block, s):
        nb2 = n_branch // 2

        @block.sync
        def _(sp):
            sp.dma_start(B.wb, wsrc).then_inc(s["w"], 16)

        @block.tensor
        def _(pe):
            pe.wait_ge(s["w"], 16)
            for c in range(KD):
                if c >= 2:
                    pe.wait_ge(s["merged"], c - 1)
                for b in range(n_branch):
                    bank = ps[:, (c % 2) * 2 + b // 2, (b % 2) * T:(b % 2 + 1) * T]
                    for k in range(per):
                        mm = nc.tensor.matmul(bank, B.wb[:, b * per + k, c * P:(c + 1) * P], acts[b][:, k, :],
                                              start=(k == 0), stop=(k == per - 1), skip_group_check=True)
                mm.then_inc(s["prod"], 1)

        @block.vector
        def _(dve):
            ch = Chain(dve, s["chain"])
            for c in range(KD):
                dve.wait_ge(s["prod"], c + 1)
                for b in range(nb2):
                    bank = ps[:, (c % 2) * 2 + b, :].rearrange("p (b t) -> p b t", t=T)
                    g = gates[:, 2 * b * KD + c:2 * b * KD + c + KD + 1:KD, :]
                    ch.did(nc.vector.tensor_tensor(B.mtmp[:, 2 * b:2 * b + 2, :], bank, g, ALU.mult))
                dve.wait_ge(s["chain"], ch.n)
                if nb2 == 2:
                    ch.link(nc.vector.tensor_tensor(B.mtmp[:, 0:2, :], B.mtmp[:, 0:2, :], B.mtmp[:, 2:4, :], ALU.add))
                nc.vector.tensor_tensor(B.sq[:, c, :], B.mtmp[:, 0, :], B.mtmp[:, 1, :], ALU.add).then_inc(s["merged"], 1)
                dve.wait_ge(s["merged"], c + 1)


def out_phase(nc, B, wsrc, dst, add):
    ps = B.ps
    ring = 4
    with phase(nc, project_sems("o", ring)) as (block, s):

        @block.sync
        def _(sp):
            project_sp(sp, s, "o", wsrc, B.ring4, ring, KD)

        @block.tensor
        def _(pe):
            project_pe(pe, nc, s, "o", B.ring4, B.sq, lambda r: ps[:, r, :], ring, KD, T)

        @block.vector
        def _(dve):
            def move(c, r):
                if add:
                    return nc.vector.tensor_tensor(dst[:, c, :], dst[:, c, :], ps[:, r, 0:T], ALU.add)
                return nc.vector.tensor_copy(dst[:, c, :], ps[:, r, 0:T])

            project_out(dve, s, "o", move, ring, KD)
            dve.wait_ge(s["o_out"], KD)


class Bufs:

    stage = "whole"


def alloc(nc, ctx, B, **spec):
    made = []
    for name, shape in spec.items():
        t = ctx.enter_context(nc.sbuf_tensor(f"{name}_{B.stage}", list(shape), F32))
        made.append(t[tuple(slice(None) for _ in shape)])
    return made


def first_block_program(nc, B, I):
    B.stage = "first"
    with ExitStack() as ctx:
        (B.h, B.vec, B.nsink, B.sil, B.hid, B.w_ff, B.z, B.ff, B.ffe, B.ffn_, B.qksq, B.hvar, B.hstd, B.hrstd,
         B.vtok, B.qgain, B.kdup, B.lfa0, B.lfa1, B.upad, B.u, B.b_sc, B.b_conf, B.b_swa, B.b_fox, B.gates,
         B.swa_table, B.prob, B.prob_t, B.stat, B.relb) = alloc(
            nc, ctx, B, h=(P, KD, T), vec=(P, NVEC), nsink=(P, 4), sil=(P, 2, T), hid=(P, 2, T), w_ff=(P, KD, 4),
            z=(P, ZC, T), ff=(P, 8), ffe=(P, 8), ffn_=(P, 8), qksq=(P, 7, T), hvar=(P, T), hstd=(P, T), hrstd=(P, T),
            vtok=(P, TC, 384), qgain=(P, 2), kdup=(P, 2, T), lfa0=(P, 4, T), lfa1=(P, 4, P),
            upad=(P, 2, CONV_K - 1 + T), u=(P, 2, T), b_sc=(P, 2, T), b_conf=(P, 2, T), b_swa=(P, 2, T),
            b_fox=(P, 2, T), gates=(P, GC, T), swa_table=(P, 4 * TC, T), prob=(P, 2, 512), prob_t=(P, 2, 512),
            stat=(P, 2, 4), relb=(N_BUCKETS, 4))
        B.mtmp = B.prob_t.rearrange("p a (b t) -> p (a b) t", t=T)
        B.d_wff = I["w_ff"]
        swa_table_phase(nc, B, I)
        with nc.Fori(0, DEPTH) as l:
            layer_vec_phase(nc, B, I, l)
            v = lambda name: B.vec[:, VEC[name][0]:VEC[name][0] + VEC[name][1]]
            ffn_phase(nc, B, l, I["ffn1_wg"], I["ffn1_wu"], I["ffn1_wd"], v("ffn1"))
            z_phase(nc, B, l, I["w_z"], v("mix"))
            branch_phase(nc, B, l, I["w_g"])
            first_attention(nc, B)
            merge_phase(nc, B, I["w_branch"][l], [B.b_conf, B.b_sc, B.b_swa, B.b_fox], 2, B.gates, 4)
            out_phase(nc, B, lambda c: I["w_out"][l, c], B.x, True)
            ffn_phase(nc, B, l, I["ffn2_wg"], I["ffn2_wu"], I["ffn2_wd"], v("ffn2"))


def swa_table_phase(nc, B, I):
    line = B.gates[:, 0:8, :].rearrange("p (h a) t -> p h (a t)", h=4)
    ps, con = B.ps, B.con
    with phase(nc, "loaded relb_in line_mm line_ready line_out table_in masked") as (block, s):

        @block.sync
        def _(sp):
            sp.dma_start(B.con_all, I["const"]).then_inc(s["loaded"], 16)
            sp.dma_start(B.x, I["x"]).then_inc(s["loaded"], 16)
            sp.dma_start(B.relb, I["rel_bias"]).then_inc(s["relb_in"], 16)
            sp.wait_ge(s["line_ready"], 1)
            sp.dma_start(B.d_line, line).then_inc(s["line_out"], 16)
            sp.wait_ge(s["line_out"], 16)
            for h in range(4):
                for qc in range(TC):
                    skew = bass.AP(tensor=B.d_line.tensor, offset=h * 512 + P - 1 + (0 if qc else P), ap=[[4 * 512 - 1, P], [1, T]])
                    sp.dma_start(B.swa_table[:, h * TC + qc, :], skew).then_inc(s["table_in"], 16)
            sp.wait_ge(s["loaded"], 32)

        @block.tensor
        def _(pe):
            pe.wait_ge(s["loaded"], 32)
            pe.wait_ge(s["relb_in"], 16)
            for h in range(4):
                mm = nc.tensor.matmul(ps[:, h, :], B.relb[:, h:h + 1].broadcast_to([N_BUCKETS, P]), con("bucket")[0:N_BUCKETS, :],
                                      start=True, stop=True)
            mm.then_inc(s["line_mm"], 1)

        @block.vector
        def _(dve):
            dve.wait_ge(s["line_mm"], 1)
            nc.vector.tensor_copy(line, ps[:, 0:4, :]).then_inc(s["line_ready"], 1)
            dve.wait_ge(s["table_in"], 16 * 4 * TC)
            for h in range(4):
                nc.vector.tensor_tensor(B.swa_table[:, h * TC:(h + 1) * TC, :], B.swa_table[:, h * TC:(h + 1) * TC, :],
                                        con("window"), ALU.add).then_inc(s["masked"], 1)
            dve.wait_ge(s["masked"], 4)


def layer_vec_phase(nc, B, I, l):
    with phase(nc, "vec_in nsink_ready") as (block, s):

        @block.sync
        def _(sp):
            sp.dma_start(B.vec, I["vec"][l]).then_inc(s["vec_in"], 16)

        @block.vector
        def _(dve):
            dve.wait_ge(s["vec_in"], 16)
            nc.vector.tensor_scalar(B.nsink, B.vec[:, VEC["sink"][0]:VEC["sink"][0] + 4], -1.0, None,
                                    ALU.mult).then_inc(s["nsink_ready"], 1)
            dve.wait_ge(s["nsink_ready"], 1)


def bcast(a, axis, n):
    a = a.unsqueeze(axis)
    shape = list(a.shape)
    shape[axis] = n
    return a.broadcast_to(shape)


def load2_phase(nc, B, I):
    v2 = B.v2
    with phase(nc, "in table_in silu masked") as (block, s):

        @block.sync
        def _(sp):
            sp.dma_start(B.vec2, I["vec2"]).then_inc(s["in"], 16)
            sp.dma_start(B.ctx, I["ctx"]).then_inc(s["in"], 16)
            rows_kept = 2 * ROWS - 1
            copy = NA_HEADS * rows_kept * P
            for h in range(NA_HEADS):
                for qc in range(TC):
                    for r2 in range(P // GRID_W):
                        r = qc * (P // GRID_W) + r2
                        first = (h * rows_kept + ROWS - 1 - r) * P + GRID_W - 1
                        skew = bass.AP(tensor=I["rpb"].tensor, offset=first, ap=[[copy - 1, GRID_W], [P, ROWS], [1, GRID_W]])
                        dst = B.na_table[r2 * GRID_W:(r2 + 1) * GRID_W, h * TC + qc, :].rearrange("p (r c) -> p r c", c=GRID_W)
                        sp.dma_start(dst, skew).then_inc(s["table_in"], 16)
            sp.wait_ge(s["in"], 32)

        @block.scalar
        def _(act):
            act.wait_ge(s["in"], 32)
            for j, name in enumerate(("c", "c_ctx")):
                nc.scalar.activation(B.cond[:, :, j], v2(name), ACT.Silu).then_inc(s["silu"], 1)
            act.wait_ge(s["silu"], 2)

        @block.vector
        def _(dve):
            dve.wait_ge(s["table_in"], 16 * NA_HEADS * TC * (P // GRID_W))
            mask = bcast(B.con("na_mask"), 1, NA_HEADS * TC)
            nc.vector.tensor_tensor(B.na_table, B.na_table, mask, ALU.add).then_inc(s["masked"], 1)
            dve.wait_ge(s["masked"], 1)


def ada_phase(nc, B, I):
    ring = 8
    with phase(nc, project_sems("m", ring) + "chain") as (block, s):

        @block.sync
        def _(sp):
            project_sp(sp, s, "m", lambda c: I["w_ada"][c], B.wring, ring, 48)

        @block.tensor
        def _(pe):
            project_pe(pe, nc, s, "m", B.wring, B.cond, lambda r: B.ps[:, r, :], ring, 48, 2)

        @block.vector
        def _(dve):
            ch = Chain(dve, s["chain"])
            project_out(dve, s, "m", lambda c, r: nc.vector.tensor_copy(B.mod[:, c, :], B.ps[:, r, 0:2]), ring, 48)
            dve.wait_ge(s["m_out"], 48)
            v2 = B.v2
            ch.link(nc.vector.tensor_tensor(B.mod, B.mod, bcast(v2("b_ada"), 2, 2), ALU.add))
            one = nc.vector.tensor_scalar
            ch.did(one(B.gains[:, 0, :], B.mod[:, 8:16, 0], 1.0, None, ALU.add))
            ch.did(one(B.gains[:, 1, :], B.mod[:, 8:16, 1], 1.0, None, ALU.add))
            ch.did(one(B.gains[:, 2, :], B.mod[:, 32:40, 0], 1.0, None, ALU.add))
            dve.wait_ge(s["chain"], ch.n)
            for j, name in enumerate(("mix_pre", "mix_pre", "ffn_pre")):
                ch.did(nc.vector.tensor_tensor(B.gains[:, j, :], B.gains[:, j, :], v2(name), ALU.mult))
            ch.did(nc.vector.tensor_tensor(B.gains[:, 3, :], B.mod[:, 16:24, 0], v2("mix_post"), ALU.mult))
            ch.did(nc.vector.tensor_tensor(B.gains[:, 4, :], B.mod[:, 40:48, 0], v2("ffn_post"), ALU.mult))
            dve.wait_ge(s["chain"], ch.n)


def norm_phase(nc, B, src, dst, gain, shift, add_to=None):
    ps, con = B.ps, B.con
    with phase(nc, NORM + "chain") as (block, s):
        s.update(std=B.std[:, 0:T], var=B.var[:, 0:T], rstd=B.rstd[:, 0:T])
        ms = ps[:, 0, 0:T]

        @block.scalar
        def _(act):
            norm_act(act, nc, s, src, B.sq2)

        @block.tensor
        def _(pe):
            norm_pe(pe, nc, s, B.sq2, ms, con("mean_d"), KD)

        @block.vector
        def _(dve):
            norm_dve(dve, nc, s, src, dst, ms, gain, KD)
            dve.wait_ge(s["h_normed"], 1)
            ch = Chain(dve, s["chain"])
            if add_to is not None:
                ch.link(nc.vector.tensor_tensor(add_to, add_to, dst, ALU.add))
            else:
                for k in range(KD):
                    ch.did(nc.vector.tensor_scalar(dst[:, k, :], dst[:, k, :], shift[:, k:k + 1], None, ALU.add))
                dve.wait_ge(s["chain"], ch.n)


def kv_phase(nc, B, I):
    ps = B.ps
    ring = 7
    with phase(nc, project_sems("kv", ring) + "gw g_mm g_out") as (block, s):

        @block.sync
        def _(sp):
            sp.dma_start(B.w_mg, I["w_mg"]).then_inc(s["gw"], 16)
            project_sp(sp, s, "kv", lambda c: I["w_kv"][c], B.wring, ring, CX)

        @block.tensor
        def _(pe):
            pe.wait_ge(s["gw"], 16)
            for t in range(NT2 // P):
                for k in range(KD):
                    mm = nc.tensor.matmul(ps[:, 7, 16 * t:16 * t + 16], B.hcat[:, k, t * P:(t + 1) * P], B.w_mg[:, k, :],
                                          start=(k == 0), stop=(k == KD - 1))
            mm.then_inc(s["g_mm"], 1)
            project_pe(pe, nc, s, "kv", B.wring, B.hcat, lambda r: ps[:, r, :], ring, CX, NT2)

        @block.scalar
        def _(act):
            project_out(act, s, "kv", lambda c, r: nc.scalar.copy(B.kv[:, c, :], ps[:, r, :]), ring, CX)

        @block.vector
        def _(dve):
            dve.wait_ge(s["g_mm"], 1)
            nc.vector.tensor_copy(B.mg, ps[:, 7, 0:64].rearrange("p (t g) -> p t g", g=16)).then_inc(s["g_out"], 1)
            dve.wait_ge(s["g_out"], 1)


def plain_project_phase(nc, B, wsrc, src, dst, ring, n, func):
    ps = B.ps
    with phase(nc, project_sems("q", ring)) as (block, s):

        @block.sync
        def _(sp):
            project_sp(sp, s, "q", wsrc, B.wring, ring, n)

        @block.tensor
        def _(pe):
            project_pe(pe, nc, s, "q", B.wring, src, lambda r: ps[:, r, :], ring, n, T)

        @block.scalar
        def _(act):
            project_out(act, s, "q", lambda c, r: nc.scalar.activation(dst[:, c, :], ps[:, r, 0:T], func), ring, n)


NAK, NAV, MLK, MLV = 0, 4, 8, 10
NAQ, MLQ, MLO = 0, 4, 6


def prepare2_phase(nc, B):
    ps, con, kv, q = B.ps, B.con, B.kv, B.q10
    with phase(nc, "v_turned v_copied q_scaled turned_mm rope chain tanh_in tanh exp_in exp ln_in ln") as (block, s):

        @block.tensor
        def _(pe):
            for j, c0 in enumerate((NAV, MLV)):
                for t in range(NT2 // P):
                    for c in range(4):
                        mm = nc.tensor.transpose(ps[:, 4 * j + t, c * P:(c + 1) * P], kv[:, c0 + c, t * P:(t + 1) * P], con("ident"))
            mm.then_inc(s["v_turned"], 1)
            pe.wait_ge(s["v_copied"], 8)
            pe.wait_ge(s["q_scaled"], 1)
            for j in range(4):
                x = q[:, MLQ + j, :] if j < 2 else kv[:, MLK + j - 2, 0:T]
                mm = nc.tensor.matmul(ps[:, j // 2, (j % 2) * T:(j % 2 + 1) * T], con("turn"), x, start=(j % 2 == 0),
                                      stop=True, skip_group_check=True)
            mm.then_inc(s["turned_mm"], 1)

        @block.scalar
        def _(act):
            act.wait_ge(s["tanh_in"], 1)
            nc.scalar.activation(B.mg, B.mg, ACT.Tanh, scale=1.0 / CAP).then_inc(s["tanh"], 1)
            act.wait_ge(s["exp_in"], 1)
            nc.scalar.activation(B.mge, B.mgn, ACT.Exp).then_inc(s["exp"], 1)
            act.wait_ge(s["ln_in"], 1)
            nc.scalar.activation(B.mgn, B.mge, ACT.Ln).then_inc(s["ln"], 1)

        @block.vector
        def _(dve):
            ch = Chain(dve, s["chain"])
            nc.vector.tensor_scalar(q[:, 0:6, :], q[:, 0:6, :], HD ** -0.5, None, ALU.mult).then_inc(s["q_scaled"], 1)
            nc.vector.tensor_tensor(B.mg, B.mg, bcast(B.v2("gates"), 1, 4), ALU.add).then_inc(s["tanh_in"], 1)
            dve.wait_ge(s["v_turned"], 1)
            for j, dst in enumerate((B.v_na, B.v_ml)):
                for t in range(NT2 // P):
                    nc.vector.tensor_copy(dst[:, t, :], ps[:, 4 * j + t, :]).then_inc(s["v_copied"], 1)
            dve.wait_ge(s["tanh"], 1)
            ch.link(nc.vector.tensor_scalar(B.mg, B.mg, CAP, None, ALU.mult))
            ch.link(nc.vector.tensor_scalar(B.mge, B.mg, -1.0, None, ALU.mult))
            nc.vector.tensor_tensor(B.mgn, B.mg, B.mge, ALU.min).then_inc(s["exp_in"], 1)
            dve.wait_ge(s["exp"], 1)
            nc.vector.tensor_scalar(B.mge, B.mge, 1.0, None, ALU.add).then_inc(s["ln_in"], 1)
            dve.wait_ge(s["ln"], 1)
            ch.link(nc.vector.tensor_scalar(B.mlf, B.mg, 0.0, None, ALU.min))
            ch.link(nc.vector.tensor_tensor(B.mlf, B.mlf, B.mgn, ALU.subtract))
            for h in range(ML_HEADS):
                up, fr = con("upto"), con("from")
                for dst, mask, t, col in ((B.lf_f0[:, h, :], up[:, 0, :], 0, 4 + h), (B.lf_f1[:, h, :], up[:, 1, P:T], 1, 4 + h),
                                          (B.lf_b0[:, h, :], fr[:, 0, 0:P], 0, 12 + h), (B.lf_b1[:, h, :], fr[:, 1, :], 1, 12 + h)):
                    ch.did(nc.vector.tensor_scalar(dst, mask, B.mlf[:, t, col:col + 1], None, ALU.mult))
            dve.wait_ge(s["turned_mm"], 1)
            for j in range(2):
                x = q[:, MLQ:MLQ + 2, :] if j == 0 else kv[:, MLK:MLK + 2, 0:T]
                ch.link(nc.vector.tensor_tensor(B.ropet[:, 0:2, :], ps[:, j, :].rearrange("p (c t) -> p c t", t=T),
                                                bcast(con("sin"), 1, 2), ALU.mult))
                ch.link(nc.vector.tensor_tensor(x, x, bcast(con("cos"), 1, 2), ALU.mult))
                ch.link(nc.vector.tensor_tensor(x, x, B.ropet[:, 0:2, :], ALU.add))


def neighbourhood(nc, B):
    units = []
    for h in range(NA_HEADS):
        lo = (h % 2) * HD
        for qc in range(TC):
            def scores(dst, h=h, lo=lo, qc=qc):
                return nc.tensor.matmul(dst, B.q10[lo:lo + HD, NAQ + h // 2, qc * P:(qc + 1) * P],
                                        B.kv[lo:lo + HD, NAK + h // 2, :], start=True, stop=True)

            units.append(dict(scores=scores, table=B.na_table[:, h * TC + qc, :], sink=None, row=lo,
                              values=[B.v_na[:, t, h * HD:(h + 1) * HD] for t in range(NT2 // P)],
                              out=B.b_na[lo:lo + HD, h // 2, qc * P:(qc + 1) * P]))
    attention_phase(nc, B, units, NT2)


def mlstm_phase(nc, B):
    ps, con, q, kv = B.ps, B.con, B.q10, B.kv
    units = [(h, qc, d) for h in range(ML_HEADS) for qc in range(TC) for d in range(2)]
    n = len(units)
    with phase(nc, "scores_ready max_ready exp_ready probs_ready turned probs_t_ready out_ready out_copied chain added") as (block, s):
        spread = {0: (B.lf_f0, B.lf_f1), 1: (B.lf_b0, B.lf_b1)}

        @block.tensor
        def _(pe):
            def scores(u):
                h, qc, d = units[u]
                lo = (h % 2) * HD
                if u >= 2:
                    pe.wait_ge(s["probs_ready"], u - 1)
                nc.tensor.matmul(ps[:, u % 2, :], q[lo:lo + HD, MLQ + h // 2, qc * P:(qc + 1) * P],
                                 kv[lo:lo + HD, MLK + h // 2, :], start=True, stop=True)
                dd = ps[:, 2 + u % 2, :]
                side = con("after") if d == 0 else con("before")
                lf = 4 + h if d == 0 else 12 + h
                li = h if d == 0 else 8 + h
                chunks = [c for c in range(TC) if (c <= qc if d == 0 else c >= qc)]
                for j, c in enumerate(chunks):
                    a = spread[d][c]
                    whole = (c == 0) == (d == 0)
                    lhs = a[:, h, qc * P:(qc + 1) * P] if whole else a[:, h, :]
                    nc.tensor.matmul(dd, lhs, side[:, c, :], start=(j == 0), stop=False, skip_group_check=True)
                for c in range(TC):
                    nc.tensor.matmul(dd[:, T:NT2], B.mlf[:, TC + c, lf:lf + 1].broadcast_to([P, P]), side[:, c, 0:T],
                                     start=False, stop=False, skip_group_check=True)
                for c in range(2 * TC):
                    mm = nc.tensor.matmul(dd[:, c * P:(c + 1) * P], B.mg[:, c, li:li + 1].broadcast_to([P, P]), con("ident"),
                                          start=False, stop=(c == 2 * TC - 1), skip_group_check=True)
                mm.then_inc(s["scores_ready"], 1)

            def turn(u):
                pe.wait_ge(s["probs_ready"], u + 1)
                if u >= 2:
                    pe.wait_ge(s["probs_t_ready"], u - 1)
                for j in range(4):
                    mm = nc.tensor.transpose(ps[:, 4 + u % 2, j * P:(j + 1) * P], B.prob[:, u % 2, j * P:(j + 1) * P], con("ident"))
                mm.then_inc(s["turned"], 1)

            def values(u):
                h, qc, d = units[u]
                pe.wait_ge(s["probs_t_ready"], u + 1)
                if d == 0 and u >= 4:
                    pe.wait_ge(s["out_copied"], u // 2 - 1)
                for j in range(4):
                    mm = nc.tensor.matmul(ps[:, 6 + (u // 2) % 2, 0:P], B.v_ml[:, j, h * P:(h + 1) * P],
                                          B.prob_t[:, u % 2, j * P:(j + 1) * P], start=(d == 0 and j == 0),
                                          stop=(d == 1 and j == 3))
                mm.then_inc(s["out_ready"], 1)

            scores(0)
            for u in range(n):
                if u + 1 < n:
                    scores(u + 1)
                turn(u)
                values(u)

        @block.scalar
        def _(act):
            for u in range(n + 1):
                if u < n:
                    act.wait_ge(s["max_ready"], u + 1)
                    nc.scalar.activation(B.stat[:, u % 2, 2:3], B.stat[:, u % 2, 0:1], ACT.Exp)
                    nc.scalar.activation(B.prob[:, u % 2, :], B.prob[:, u % 2, :], ACT.Exp,
                                         bias=B.stat[:, u % 2, 0:1]).then_inc(s["exp_ready"], 1)
                if u >= 1:
                    act.wait_ge(s["turned"], u)
                    if u >= 3:
                        act.wait_ge(s["out_ready"], u - 2)
                    nc.scalar.copy(B.prob_t[:, (u - 1) % 2, :], ps[:, 4 + (u - 1) % 2, :]).then_inc(s["probs_t_ready"], 1)

        @block.vector
        def _(dve):
            ch = Chain(dve, s["chain"])
            for u in range(n + 2):
                if u < n:
                    h, qc, d = units[u]
                    dve.wait_ge(s["scores_ready"], u + 1)
                    if u >= 2:
                        dve.wait_ge(s["turned"], u - 1)
                    dd = ps[:, 2 + u % 2, :]
                    mask = con("causal" if d == 0 else "anticausal")[:, qc, :]
                    ch.did(nc.vector.tensor_tensor(B.prob[:, u % 2, 0:T], dd[:, 0:T], mask, ALU.add))
                    ch.link(nc.vector.tensor_copy(B.prob[:, u % 2, T:NT2], dd[:, T:NT2]))
                    nc.vector.tensor_reduce(B.stat[:, u % 2, 0:1], B.prob[:, u % 2, :], AX, ALU.max,
                                            negate=True).then_inc(s["max_ready"], 1)
                if 1 <= u <= n:
                    w = u - 1
                    dve.wait_ge(s["exp_ready"], w + 1)
                    den = B.stat[:, w % 2, 1:2]
                    p = B.prob[:, w % 2, :]
                    ch.link(nc.vector.tensor_tensor(p, p, ps[:, w % 2, :], ALU.mult))
                    ch.link(nc.vector.tensor_reduce(den, p, AX, ALU.add))
                    ch.link(nc.vector.tensor_scalar(B.stat[:, w % 2, 3:4], den, -1.0, None, ALU.mult))
                    ch.link(nc.vector.tensor_tensor(den, den, B.stat[:, w % 2, 3:4], ALU.max))
                    ch.link(nc.vector.tensor_tensor(den, den, B.stat[:, w % 2, 2:3], ALU.max))
                    ch.link(nc.vector.reciprocal(B.stat[:, w % 2, 3:4], den))
                    nc.vector.tensor_scalar(p, p, B.stat[:, w % 2, 3:4], None, ALU.mult).then_inc(s["probs_ready"], 1)
                if u >= 2 and units[u - 2][2] == 1:
                    h, qc, _ = units[u - 2]
                    dve.wait_ge(s["out_ready"], u - 1)
                    nc.vector.tensor_copy(B.b_ml[:, h, qc * P:(qc + 1) * P],
                                          ps[:, 6 + ((u - 2) // 2) % 2, 0:P]).then_inc(s["out_copied"], 1)
            dve.wait_ge(s["out_copied"], n // 2)


def head_norm_phase(nc, B):
    ps, con = B.ps, B.con
    sq = B.sq2[:, 0:ML_HEADS, :]
    with phase(nc, "sq ms var std sig chain") as (block, s):

        @block.scalar
        def _(act):
            nc.scalar.activation(sq, B.b_ml, ACT.Square).then_inc(s["sq"], 1)
            nc.scalar.activation(B.q10[:, MLO:MLO + 4, :], B.q10[:, MLO:MLO + 4, :], ACT.Sigmoid).then_inc(s["sig"], 1)
            act.wait_ge(s["var"], 1)
            nc.scalar.activation(sq, sq, ACT.Sqrt).then_inc(s["std"], 1)

        @block.tensor
        def _(pe):
            pe.wait_ge(s["sq"], 1)
            for j in range(2):
                mm = nc.tensor.matmul(ps[:, j, :], con("mean_head"), sq[:, 2 * j:2 * j + 2, :], start=True, stop=True)
            mm.then_inc(s["ms"], 1)

        @block.vector
        def _(dve):
            ch = Chain(dve, s["chain"])
            dve.wait_ge(s["ms"], 1)
            nc.vector.tensor_scalar(sq, ps[:, 0:2, :].rearrange("p b (c t) -> p (b c) t", t=T), EPS, None,
                                    ALU.add).then_inc(s["var"], 1)
            dve.wait_ge(s["std"], 1)
            ch.link(nc.vector.reciprocal(sq, sq))
            dve.wait_ge(s["sig"], 1)
            ch.did(nc.vector.tensor_tensor(sq, sq, B.q10[:, MLO:MLO + 4, :], ALU.mult))
            dve.wait_ge(s["chain"], ch.n)
            for h in range(ML_HEADS):
                ch.did(nc.vector.scalar_tensor_tensor(B.b_ml[:, h, :], B.b_ml[:, h, :], B.v2("head")[:, h:h + 1], sq[:, h, :],
                                                      ALU.mult, ALU.mult))
            dve.wait_ge(s["chain"], ch.n)


NB = 2 * E


def router_phase(nc, B, I):
    ps, con = B.ps, B.con
    with phase(nc, "in logits h_turned h_copied max_ready exp_ready sel_ready counted chain listed") as (block, s):

        @block.sync
        def _(sp):
            sp.dma_start(B.w_r, I["w_router"]).then_inc(s["in"], 16)

        @block.tensor
        def _(pe):
            pe.wait_ge(s["in"], 16)
            for t in range(TC):
                for k in range(KD):
                    mm = nc.tensor.matmul(ps[:, 0, t * E:(t + 1) * E], B.h2[:, k, t * P:(t + 1) * P], B.w_r[:, k, :],
                                          start=(k == 0), stop=(k == KD - 1))
            mm.then_inc(s["logits"], 1)
            for t in range(TC):
                for k in range(KD):
                    mm = nc.tensor.transpose(ps[:, 2 + 2 * t + k // 4, (k % 4) * P:(k % 4 + 1) * P],
                                             B.h2[:, k, t * P:(t + 1) * P], con("ident"))
            mm.then_inc(s["h_turned"], 1)
            pe.wait_ge(s["sel_ready"], 1)
            for t in range(TC):
                for c in range(t + 1):
                    nc.tensor.matmul(ps[:, 1, t * E:(t + 1) * E], con("before")[:, c, t * P:(t + 1) * P], B.sel[:, c, :],
                                     start=(c == 0), stop=(c == t))
            for c in range(TC):
                mm = nc.tensor.matmul(ps[:, 1, TC * E:(TC + 1) * E], con("ones"), B.sel[:, c, :], start=(c == 0), stop=(c == TC - 1))
            mm.then_inc(s["counted"], 1)

        @block.scalar
        def _(act):
            act.wait_ge(s["max_ready"], 1)
            for t in range(TC):
                nc.scalar.activation(B.wtok[:, t, :], B.lg[:, t, :], ACT.Exp, bias=B.rmax[:, t:t + 1]).then_inc(s["exp_ready"], 1)
            act.wait_ge(s["h_turned"], 1)
            for t in range(TC):
                nc.scalar.copy(B.htok[:, t, :], ps[:, 2 + 2 * t:4 + 2 * t, :].rearrange("p b c -> p (b c)")).then_inc(s["h_copied"], 1)
            act.wait_ge(s["h_copied"], TC)

        @block.vector
        def _(dve):
            ch = Chain(dve, s["chain"])
            tt, ts, red = nc.vector.tensor_tensor, nc.vector.tensor_scalar, nc.vector.tensor_reduce
            dve.wait_ge(s["logits"], 1)
            ch.link(tt(B.lg, ps[:, 0, 0:TC * E].rearrange("p (t e) -> p t e", e=E), bcast(B.v2("b_router"), 1, TC), ALU.add))
            red(B.rmax, B.lg, AX, ALU.max, negate=True).then_inc(s["max_ready"], 1)
            for t in range(TC):
                other, this = bcast(B.lg[:, t, :], 1, E), bcast(B.lg[:, t, :], 2, E)
                ch.link(tt(B.cmp, other, this, ALU.is_equal))
                ch.link(tt(B.cmp, B.cmp, con("earlier"), ALU.mult))
                ch.link(tt(B.cmp2, other, this, ALU.is_gt))
                ch.link(tt(B.cmp, B.cmp, B.cmp2, ALU.add))
                ch.link(red(B.sel[:, t, :], B.cmp, AX, ALU.add))
            ts(B.sel, B.sel, TOPK - 0.5, None, ALU.is_lt).then_inc(s["sel_ready"], 1)
            dve.wait_ge(s["sel_ready"], 1)
            dve.wait_ge(s["exp_ready"], TC)
            ch.link(tt(B.wtok, B.wtok, B.sel, ALU.mult))
            ch.link(red(B.rsum, B.wtok, AX, ALU.add))
            ch.link(nc.vector.reciprocal(B.rsum, B.rsum))
            for t in range(TC):
                ch.did(ts(B.wtok[:, t, :], B.wtok[:, t, :], B.rsum[:, t:t + 1], None, ALU.mult))
            dve.wait_ge(s["counted"], 1)
            pos = ps[:, 1, 0:TC * E].rearrange("p (t e) -> p t e", e=E)
            for o in range(PER):
                part = B.slot[:, :, o:PER * E:PER]
                ch.link(ts(part, pos, 1.0 - o * SLOTS, None, ALU.add))
                ch.link(tt(part, part, B.sel, ALU.mult))
                ch.link(ts(part, part, -1.0, None, ALU.add))
            cnt = ps[:, 1, TC * E:(TC + 1) * E]
            ch.link(ts(B.nb[:, 0, :], cnt, 0.5, None, ALU.is_gt))
            for o in range(1, PER):
                ch.link(ts(B.nb[:, 1, :], cnt, o * SLOTS + 0.5, None, ALU.is_gt))
                ch.link(tt(B.nb[:, 0, :], B.nb[:, 0, :], B.nb[:, 1, :], ALU.add))
            ch.link(tt(B.cmp, bcast(B.nb[:, 0, :], 1, E), con("earlier"), ALU.mult))
            ch.link(red(B.nb[:, 1, :], B.cmp, AX, ALU.add))
            ch.link(tt(B.nb[:, 1, :], B.nb[:, 1, :], B.nb[:, 0, :], ALU.add))
            blocks = B.list[:, 0, PER:PER + NB]
            ch.link(nc.vector.memset(B.list, -1.0))
            ch.link(tt(B.listc, bcast(B.nb[:, 1, :], 1, NB), bcast(con("block_no"), 2, E), ALU.is_le))
            ch.link(red(blocks, B.listc, AX, ALU.add))
            ch.link(ts(blocks, blocks, E - 1.0, None, ALU.min))
            col = B.list[:, 1, PER:PER + NB]
            ch.link(ts(col, blocks, float(PER), None, ALU.mult))
            for o in range(1, PER):
                ch.link(tt(B.same, blocks, B.list[:, 0, PER - o:PER - o + NB], ALU.is_equal))
                ch.link(tt(col, col, B.same, ALU.add))
            ch.link(nc.vector.tensor_copy(B.list[:, 1, 0:1], B.nb[:, 1, E - 1:E]))
            ch.link(nc.vector.tensor_copy(B.listi, B.list))


def moe_phase(nc, B, I):
    ps, con = B.ps, B.con
    names = ("wg0 wg1 wl0 wl1 wd0 wd1 gate_half lin_half down_half g_ready sig_ready a_ready scattered0 scattered1 added0 added1 st_turned "
             "st_copied s_ready gathered hg_ready a_turned at_ready y_ready bias_in bias_spread t_read l_read g_read m_ready zeroed tick_ready")
    wsrc = {"g": I["w_gate2"], "l": I["w_lin2"], "d": I["w_down2"]}
    with phase(nc, names) as (block, s):
        G, L, Y, X, H, A, S_t = ps[:, 0, :], ps[:, 1, :], ps[:, 2, :], ps[:, 3:5, :], ps[:, 5, :], ps[:, 6, :], ps[:, 7, :]
        HALF = D // 2
        side = lambda half: slice(half * SLOTS, (half + 1) * SLOTS)

        def blocks(eng):
            return eng.value_load(B.listi[0:1, 1, 0:1], min_val=T * TOPK // SLOTS, max_val=NB - 1)

        def entry(eng, row, j, top):
            return eng.value_load(B.listi[0:1, row, bass.ds(j, 1)], min_val=0, max_val=top)

        @block.sync
        def _(sp):
            def weights(e, kind, half):
                src = wsrc[kind][e].rearrange("(k p) n -> p k n", p=P)[:, 4 * half:4 * half + 4, :]
                sp.dma_start(B.wexp[2 * "gld".index(kind) + half], src).then_inc(s[f"w{kind}{half}"], 16)

            total = blocks(sp)
            e = entry(sp, 0, PER, E - 1)
            sp.dma_start(B.brow, I["bias2"][bass.ds(e, 1), :]).then_inc(s["bias_in"], 16)
            for kind in "gld":
                for half in range(2):
                    weights(e, kind, half)
            with sp.Fori(1, total) as j:
                e = entry(sp, 0, j + PER, E - 1)
                sp.wait_ge(s["bias_spread"], j)
                sp.dma_start(B.brow, I["bias2"][bass.ds(e, 1), :]).then_inc(s["bias_in"], 16)
                for kind, used in (("g", "gate_half"), ("l", "lin_half"), ("d", "down_half")):
                    for half in range(2):
                        sp.wait_ge(s[used], 2 * j + (half - 1))
                        weights(e, kind, half)

        @block.gpsimd
        def _(pool):
            total = blocks(pool)
            nc.gpsimd.memset(B.tick, 0.0).then_inc(s["tick_ready"], 1)
            pool.wait_ge(s["tick_ready"], 1)
            pool.wait_ge(s["bias_in"], 16)
            nc.gpsimd.partition_broadcast(B.bias, B.brow).then_inc(s["bias_spread"], 1)
            with pool.Fori(1, total) as j:
                pool.wait_ge(s["bias_in"], 16 * j + 16)
                pool.wait_ge(s["y_ready"], j)
                nc.gpsimd.tensor_tensor(B.tick[:, 1:2], B.tick[:, 0:1], B.tick[:, 0:1], ALU.add)
                nc.gpsimd.partition_broadcast(B.bias, B.brow).then_inc(s["bias_spread"], 1)

        @block.tensor
        def _(pe):
            total = blocks(pe)

            def gather():
                for k in range(KD):
                    for t in range(TC):
                        mm = nc.tensor.matmul(H[:, k * SLOTS:(k + 1) * SLOTS], B.htok[:, t, k * P:(k + 1) * P],
                                              B.S[:, t, 0:SLOTS], start=(t == 0), stop=(t == TC - 1))
                mm.then_inc(s["gathered"], 1)

            def wide(j, kind, lhs, dst, done):
                for part in range(2):
                    pe.wait_ge(s[f"w{kind}{part}"], 16 * j + 16)
                    for k in range(4 * part, 4 * part + 4):
                        for half in range(2):
                            mm = nc.tensor.matmul(dst[side(half), :], lhs(k),
                                                  B.wexp[2 * "gld".index(kind) + part][:, k % 4, half * HALF:(half + 1) * HALF],
                                                  start=(k == 0), stop=(k == KD - 1), skip_group_check=True)
                    mm.then_inc(s[done], 1)

            def scatter(t):
                for half in range(2):
                    mm = nc.tensor.matmul(X[:, half, :], B.ST[side(half), t, :], B.y[side(half), :], start=True, stop=True)
                mm.then_inc(s[f"scattered{t}"], 1)

            def block_turn(j, first):
                pe.wait_ge(s["hg_ready"], j + 1)
                if not first:
                    pe.wait_ge(s["g_read"], j)
                wide(j, "g", lambda k: B.hg[:, k, :], G, "gate_half")
                if not first:
                    pe.wait_ge(s["st_copied"], j)
                for t in range(TC):
                    mm = nc.tensor.transpose(S_t[:, t * P:(t + 1) * P], B.S[:, t, :], con("ident"))
                mm.then_inc(s["st_turned"], 1)
                if not first:
                    pe.wait_ge(s["y_ready"], j)
                    scatter(0)
                    pe.wait_ge(s["l_read"], j)
                wide(j, "l", lambda k: B.hg[:, k, :], L, "lin_half")
                if not first:
                    pe.wait_ge(s["added0"], j)
                    scatter(1)
                pe.wait_ge(s["s_ready"], j + 2)
                gather()
                pe.wait_ge(s["a_ready"], j + 1)
                for k in range(4):
                    mm = nc.tensor.transpose(A[:, k * P:(k + 1) * P], B.a[:, k * P:(k + 1) * P], con("ident"))
                mm.then_inc(s["a_turned"], 1)
                pe.wait_ge(s["at_ready"], j + 1)
                wide(j, "d", lambda k: B.aT[:, k % 4, side(k // 4)], Y, "down_half")

            pe.wait_ge(s["s_ready"], 1)
            gather()
            block_turn(0, True)
            with pe.Fori(1, total) as j:
                block_turn(j, False)
            pe.wait_ge(s["y_ready"], total)
            scatter(0)
            pe.wait_ge(s["added0"], total)
            scatter(1)

        @block.scalar
        def _(act):
            total = blocks(act)

            def gathered_copy(n):
                act.wait_ge(s["gathered"], n + 1)
                nc.scalar.copy(B.hg, H.rearrange("p (k t) -> p k t", t=SLOTS)).then_inc(s["hg_ready"], 1)

            def block_turn(j, first):
                act.wait_ge(s["g_ready"], j + 1)
                nc.scalar.activation(B.sg, B.g, ACT.Sigmoid, scale=ALPHA).then_inc(s["sig_ready"], 1)
                act.wait_ge(s["st_turned"], j + 1)
                if not first:
                    act.wait_ge(s["scattered1"], j)
                nc.scalar.copy(B.ST, S_t[:, 0:T].rearrange("p (a b) -> p a b", b=P)).then_inc(s["st_copied"], 1)
                gathered_copy(j + 1)
                act.wait_ge(s["a_turned"], j + 1)
                nc.scalar.copy(B.aT, A.rearrange("p (k t) -> p k t", t=P)).then_inc(s["at_ready"], 1)

            gathered_copy(0)
            block_turn(0, True)
            with act.Fori(1, total) as j:
                block_turn(j, False)

        @block.vector
        def _(dve):
            total = blocks(dve)
            tt, ts, stt = nc.vector.tensor_tensor, nc.vector.tensor_scalar, nc.vector.scalar_tensor_tensor

            def one_hot(j):
                col = entry(dve, 1, j + PER, PER * E - 1)
                for t in range(TC):
                    last = ts(B.S[:, t, :], con("slots"), B.slot[:, t, bass.ds(col, 1)], None, ALU.is_equal)
                last.then_inc(s["s_ready"], 1)

            def biased(dst, bank, n):
                for half in range(2):
                    last = tt(dst[side(half), :], bank[side(half), :],
                              B.bias[side(half), n * D + half * HALF:n * D + (half + 1) * HALF], ALU.add)
                return last

            def add(t, n, e):
                dve.wait_ge(s[f"scattered{t}"], n)
                stt(B.acc[:, t, :], X.rearrange("p b c -> p (b c)"), B.wtok[:, t, bass.ds(e, 1)], B.acc[:, t, :], ALU.mult, ALU.add).then_inc(s[f"added{t}"], 1)

            def block_turn(j, first):
                e = None if first else entry(dve, 0, j + (PER - 1), E - 1)
                dve.wait_ge(s["bias_spread"], j + 1)
                dve.wait_ge(s["gate_half"], 2 * j + 2)
                biased(B.g, G, 0).then_inc(s["g_read"], 1)
                dve.wait_ge(s["g_read"], j + 1)
                ts(B.g, B.g, LIMIT, None, ALU.min).then_inc(s["g_ready"], 1)
                dve.wait_ge(s["st_turned"], j + 1)
                one_hot(j + 1)
                if not first:
                    add(0, j, e)
                dve.wait_ge(s["sig_ready"], j + 1)
                tt(B.g, B.g, B.sg, ALU.mult).then_inc(s["t_read"], 1)
                dve.wait_ge(s["lin_half"], 2 * j + 2)
                biased(B.l, L, 1).then_inc(s["l_read"], 1)
                dve.wait_ge(s["l_read"], j + 1)
                ts(B.l, B.l, LIMIT, -LIMIT, ALU.min, ALU.max).then_inc(s["m_ready"], 1)
                dve.wait_ge(s["m_ready"], j + 1)
                dve.wait_ge(s["t_read"], j + 1)
                stt(B.a, B.l, 1.0, B.g, ALU.add, ALU.mult).then_inc(s["a_ready"], 1)
                if not first:
                    add(1, j, e)
                dve.wait_ge(s["down_half"], 2 * j + 2)
                biased(B.y, Y, 2).then_inc(s["y_ready"], 1)

            nc.vector.memset(B.acc, 0.0).then_inc(s["zeroed"], 1)
            dve.wait_ge(s["zeroed"], 1)
            one_hot(0)
            block_turn(0, True)
            with dve.Fori(1, total) as j:
                block_turn(j, False)
            e = entry(dve, 0, total + (PER - 1), E - 1)
            add(0, total, e)
            add(1, total, e)


def turn_back_phase(nc, B):
    ps = B.ps
    with phase(nc, "turned copied") as (block, s):

        @block.tensor
        def _(pe):
            for k in range(KD):
                for t in range(TC):
                    mm = nc.tensor.transpose(ps[:, k // 2, (k % 2) * T + t * P:(k % 2) * T + (t + 1) * P],
                                             B.acc[:, t, k * P:(k + 1) * P], B.con("ident"))
            mm.then_inc(s["turned"], 1)

        @block.vector
        def _(dve):
            dve.wait_ge(s["turned"], 1)
            nc.vector.tensor_copy(B.h2, ps[:, 0:4, :].rearrange("p b (c t) -> p (b c) t", t=T)).then_inc(s["copied"], 1)
            dve.wait_ge(s["copied"], 1)


def second_block_program(nc, B, I, out):
    B.stage = "second"
    mod = lambda c: B.mod[:, c:c + KD, 0]
    with ExitStack() as outer:
        (B.vec2, B.cond, B.mod, B.gains, B.h2) = alloc(
            nc, outer, B, vec2=(P, NVEC2), cond=(P, KD, 2), mod=(P, 48, 2), gains=(P, 5, KD), h2=(P, KD, T))
        B.v2 = lambda name: B.vec2[:, VEC2[name][0]:VEC2[name][0] + VEC2[name][1]]
        B.sq2 = B.sq
        with ExitStack() as ctx:
            (B.hcat, B.kv, B.q10, B.na_table, B.w_mg, B.mg, B.mge, B.mgn, B.mlf, B.lf_f0, B.lf_f1, B.lf_b0, B.lf_b1,
             B.v_na, B.v_ml, B.prob, B.prob_t, B.stat) = alloc(
                nc, ctx, B, hcat=(P, KD, NT2), kv=(P, CX, NT2), q10=(P, LX, T), na_table=(P, NA_HEADS * TC, T),
                w_mg=(P, KD, 16), mg=(P, 4, 16), mge=(P, 4, 16), mgn=(P, 4, 16), mlf=(P, 4, 16), lf_f0=(P, 4, T),
                lf_f1=(P, 4, P), lf_b0=(P, 4, P), lf_b1=(P, 4, T), v_na=(P, 4, 512), v_ml=(P, 4, 512),
                prob=(P, 2, 512), prob_t=(P, 2, 512), stat=(P, 2, 4))
            halves = B.kv[:, NAV:NAV + 4, :].rearrange("p c (b t) -> p (c b) t", t=T)
            B.b_na, B.b_ml = halves[:, 0:4, :], halves[:, 4:8, :]
            B.ctx = B.h2
            B.ropet = B.prob_t.rearrange("p a (b t) -> p (a b) t", t=T)
            B.mtmp = B.ropet
            load2_phase(nc, B, I)
            ada_phase(nc, B, I)
            norm_phase(nc, B, B.x, B.hcat[:, :, 0:T], B.gains[:, 0, :], B.mod[:, 0:8, 0])
            norm_phase(nc, B, B.ctx, B.hcat[:, :, T:NT2], B.gains[:, 1, :], B.mod[:, 0:8, 1])
            kv_phase(nc, B, I)
            plain_project_phase(nc, B, lambda c: I["w_q2"][c], B.hcat[:, :, 0:T], B.q10, 5, LX, ACT.Copy)
            prepare2_phase(nc, B)
            neighbourhood(nc, B)
            plain_project_phase(nc, B, lambda c: I["w_g2"][c], B.hcat[:, :, 0:T], B.na_table, 4, G2, ACT.Sigmoid)
            mlstm_phase(nc, B)
            head_norm_phase(nc, B)
            merge_phase(nc, B, I["w_branch2"], [B.b_na, B.b_ml], 4, B.na_table, 2)
            out_phase(nc, B, lambda c: I["w_out2"][c], B.h2, False)
            norm_phase(nc, B, B.h2, B.h2, B.gains[:, 3, :], None, add_to=B.x)
        norm_phase(nc, B, B.x, B.h2, B.gains[:, 2, :], mod(24))
        with ExitStack() as ctx:
            (B.w_r, B.lg, B.rmax, B.rsum, B.sel, B.wtok, B.slot, B.nb, B.same, B.list, B.htok, B.acc) = alloc(
                nc, ctx, B, w_r=(P, KD, E), lg=(P, TC, E), rmax=(P, TC), rsum=(P, TC), sel=(P, TC, E),
                wtok=(P, TC, E), slot=(P, TC, PER * E), nb=(P, 2, E), same=(P, NB),
                list=(P, 2, PER + NB), htok=(P, TC, D),
                acc=(P, TC, D))
            B.listi = ctx.enter_context(nc.sbuf_tensor("listi", [P, 2, PER + NB], I32))[:, :, :]
            with ExitStack() as small:
                (B.cmp, B.cmp2, B.listc) = alloc(
                    nc, small, B, cmp=(P, E, E), cmp2=(P, E, E), listc=(P, NB, E))
                router_phase(nc, B, I)
            (B.wmore, B.S, B.ST, B.y, B.aT, B.hg, B.tick) = alloc(
                nc, ctx, B, wmore=(P, 4, 4, D), S=(P, TC, P), ST=(P, TC, P), y=(P, D // 2), aT=(P, 4, P), hg=(P, KD, SLOTS),
                tick=(P, 2))
            spent = B.con_all[:, B.con_kept:]
            B.bias, B.brow = spent[:, 0:3 * D], spent[0:1, 3 * D:6 * D]
            B.wexp = [B.wring[:, 0:4], B.wring[:, 4:8]] + [B.wmore[:, i] for i in range(4)]
            rows = B.sq.rearrange("p (h k) t -> p h (k t)", h=4)
            B.g, B.sg, B.l, B.a = [rows[:, i] for i in range(4)]
            moe_phase(nc, B, I)
            turn_back_phase(nc, B)
            norm_phase(nc, B, B.h2, B.h2, B.gains[:, 4, :], None, add_to=B.x)
        with phase(nc, "stored") as (block, s):
            @block.sync
            def _(sp):
                sp.dma_start(out, B.x).then_inc(s["stored"], 16)
                sp.wait_ge(s["stored"], 16)



def build(nc, I, out, stop=None):
    PHASES.clear()
    _, at = _constants()
    with ExitStack() as ctx:
        B = Bufs()
        width = I["const"].shape[1]
        (B.x, B.con_all, B.sq, B.var, B.std, B.rstd, B.wring) = alloc(
            nc, ctx, B, x=(P, KD, T), con_all=(P, width), sq=(P, KD, T), var=(P, 512), std=(P, 512), rstd=(P, 512),
            wring=(P, 8, D))
        B.wg, B.wu, B.wd, B.ring4, B.wb = B.wring[:, 0:2], B.wring[:, 2:4], B.wring[:, 4:6], B.wring[:, 0:4], B.wring
        B.ps = ctx.enter_context(nc.psum_tensor("ps", [P, 8, 512], F32))[:, :, :]
        B.d_line = nc.dram_tensor("line_scratch", (P, 4, 512), F32, kind="Internal").ap()

        def con(name):
            n, shape = at[name]
            size = int(np.prod(shape[1:]))
            a = B.con_all[:, n:n + size]
            if len(shape) == 3:
                a = a.rearrange("p (a b) -> p a b", b=shape[2])
            return a

        B.con = con
        B.con_kept = at["ones"][0]
        first_block_program(nc, B, I)
        if stop == "first":
            with phase(nc, "stored") as (block, s):
                @block.sync
                def _(sp):
                    sp.dma_start(out, B.x).then_inc(s["stored"], 16)
                    sp.wait_ge(s["stored"], 16)
            return
        second_block_program(nc, B, I, out)


def _chunk_rows(w):
    *lead, d, f = w.shape
    w = w.reshape(*lead, d // P, P, f // P, P)
    n = len(lead)
    return np.ascontiguousarray(w.transpose(*range(n), n + 2, n + 1, n, n + 3)).reshape(*lead, f // P, P, d)


def _cols(v):
    return v.reshape(-1, P).T


def _rep(v):
    return np.tile(v.reshape(1, -1), (P, 1))


def layout(a):
    I = {}
    I["const"] = _constants()[0]
    I["x"] = a["x"][0].T.reshape(KD, P, T).transpose(1, 0, 2)
    I["rel_bias"] = a["rel_bias"]
    for f in ("ffn1", "ffn2"):
        I[f + "_wg"] = _chunk_rows(a[f + "_w_gate"])
        I[f + "_wu"] = _chunk_rows(a[f + "_w_up"])
        I[f + "_wd"] = a[f + "_w_down"].reshape(DEPTH, FC, P, D)
    w = a["w_in"]
    zc = ZC * P
    I["w_z"] = _chunk_rows(w[:, :, :zc])
    I["w_ff"] = w[:, :, zc:zc + 4].reshape(DEPTH, KD, P, 4).transpose(0, 2, 1, 3)
    I["w_g"] = _chunk_rows(w[:, :, zc + 4:])
    I["w_branch"] = np.stack([a[n].reshape(DEPTH, 2, P, D) for n in ("conf_w_out", "sc_w_out", "swa_w_o", "fox_w_o")],
                             1).reshape(DEPTH, 8, P, D).transpose(0, 2, 1, 3)
    I["w_out"] = _chunk_rows(a["w_out"])
    rows = []
    for l in range(DEPTH):
        rows.append(np.concatenate([
            _cols(a["ffn1_norm"][l]), _cols(a["mix_norm"][l]), _cols(a["ffn2_norm"][l]),
            a["conf_dw"][l].T[:P], a["conf_dw"][l].T[P:], _cols(a["conf_dw_b"][l]), _cols(a["conf_ln_g"][l]),
            _cols(a["conf_ln_b"][l]), a["sc_conv"][l].T[:P], a["sc_conv"][l].T[P:],
            *[np.tile(a[n][l], 2)[:, None] for n in ("swa_q_norm", "swa_k_norm", "fox_q_norm", "fox_k_norm")],
            _rep(a["b_forget"][l]), _rep(a["swa_sink"][l])], 1))
    I["vec"] = np.stack(rows)
    kv_cols = 4 * P + 4 * P + 2 * P + 4 * P
    w = a["w_in_2"][0]
    I["w_kv"] = _chunk_rows(w[:, :kv_cols])
    I["w_mg"] = w[:, kv_cols:kv_cols + 16].reshape(KD, P, 16).transpose(1, 0, 2)
    I["w_q2"] = _chunk_rows(w[:, kv_cols + 16:kv_cols + 16 + LX * P])
    I["w_g2"] = _chunk_rows(w[:, kv_cols + 16 + LX * P:])
    I["w_ada"] = _chunk_rows(a["w_ada_2"][0])
    I["ctx"] = a["ctx_2"][0].T.reshape(KD, P, T).transpose(1, 0, 2)
    rpb = np.zeros((GRID_W, NA_HEADS, 2 * ROWS - 1, P), np.float32)
    rpb[:, :, :, GRID_W - WIN_W:GRID_W + WIN_W - 1] = a["rpb_2"][0][:, WIN_H - ROWS:WIN_H + ROWS - 1]
    I["rpb"] = rpb
    I["w_branch2"] = np.concatenate([a["w_branch_na_2"][0].reshape(4, P, D), a["w_branch_ml_2"][0].reshape(4, P, D)]).transpose(1, 0, 2)
    I["w_out2"] = _chunk_rows(a["w_out_2"][0])
    I["w_router"] = a["w_router_2"][0].reshape(KD, P, E).transpose(1, 0, 2)
    I["w_gate2"], I["w_lin2"], I["w_down2"] = a["w_gate_2"][0], a["w_lin_2"][0], a["w_down_2"][0]
    I["bias2"] = np.concatenate([a["b_gate_2"][0], a["b_lin_2"][0], a["b_down_2"][0]], 1)
    I["vec2"] = np.concatenate([
        _cols(a["c_2"][0]), _cols(a["c_ctx_2"]), _cols(a["b_ada_2"][0]), _cols(a["g_mix_pre_2"][0]), _cols(a["g_mix_post_2"][0]),
        _cols(a["g_ffn_pre_2"][0]), _cols(a["g_ffn_post_2"][0]), _rep(a["b_mlstm_gates_2"][0]), _cols(a["g_mlstm_head_2"][0]),
        _rep(a["b_router_2"][0])], 1)
    return {k: np.ascontiguousarray(v) for k, v in I.items()}


def kernel(**inputs):
    import concourse.bacc as _bacc
    from concourse.bass_utils import run_bass_kernel_spmd as _run

    arrays = layout({k: np.asarray(v) for k, v in inputs.items()})
    nc = _bacc.Bacc("TRN2", target_bir_lowering=False, num_devices=1)
    I = {k: nc.dram_tensor(f"in_{k}", v.shape, F32, kind="ExternalInput").ap() for k, v in arrays.items()}
    out = nc.dram_tensor("out", (P, KD, T), F32, kind="ExternalOutput").ap()
    build(nc, I, out, stop=STOP)
    r = _run(nc, [{f"in_{k}": v for k, v in arrays.items()}], core_ids=[0])
    o = r.results[0]["out"]
    return np.ascontiguousarray(o.transpose(2, 1, 0).reshape(1, T, D))


STOP = None
```

```python
from contextlib import ExitStack, contextmanager

import numpy as np
import concourse.bass as bass
from concourse import mybir

F32 = mybir.dt.float32
F32R = mybir.dt.float32r
I32 = mybir.dt.int32
ALU = mybir.AluOpType
ACT = mybir.ActivationFunctionType
AX = mybir.AxisListType.X

P = 128
D = 1024
KD = D // P
T = 256
TC = T // P
DEPTH = 2
FF = 2816
FC = FF // P
ZC = 20
GC = 32
HD = 64
CONV_K = 31
SC_K = 3
WINDOW = 128
N_BUCKETS = 32
EPS = 1e-6
NEG = -1e30

GRID_W = 64
ROWS = T // GRID_W
NA_HEADS = 8
WIN_H = 8
WIN_W = 16
ML_HEADS = 4
CAP = 15.0
CX = 14
LX = 10
G2 = 16
E = 32
TOPK = 4
SLOTS = 64
PER = T // SLOTS
ALPHA = 1.702
LIMIT = 7.0
NT2 = 2 * T


def _constants():
    parts, at = {}, {}

    def put(name, a):
        full = np.zeros((P, int(np.prod(a.shape[1:]))), np.float32)
        full[:a.shape[0]] = a.reshape(a.shape[0], -1)
        parts[name] = (full, a.shape)

    i = np.arange(P)
    u = np.arange(T).reshape(TC, P).T[:, :, None]
    s = np.arange(T)[None, None, :]
    put("ident", np.eye(P, dtype=np.float32))
    put("mean_d", np.full((P, P), 1.0 / D))
    put("slots", np.tile(np.arange(SLOTS, dtype=np.float32), (P, 2)))
    put("ones", np.ones((P, P)))
    put("mean_conv", np.full((P, P), 1.0 / 256))
    put("mean_head", np.full((P, P), 1.0 / P))
    put("zeros", np.zeros((P, 512)))
    heads = np.zeros((P, 7, 14))
    for c in range(7):
        heads[:HD, c, 2 * c] = heads[HD:, c, 2 * c + 1] = 1.0 / HD
    put("head_mean", heads)
    spread = np.zeros((14, 7, P))
    for c in range(7):
        spread[2 * c, c, :HD] = spread[2 * c + 1, c, HD:] = 1.0
    put("head_spread", spread)
    one = np.ones((P, TC, T))
    put("after", np.concatenate([(u > s), one], 2))
    put("before", np.concatenate([(u < s), one], 2))
    put("upto", (u <= s))
    put("from", (u >= s))
    put("causal", np.where(s <= u, 0.0, NEG))
    put("anticausal", np.where(s >= u, 0.0, NEG))
    dist = i[:, None] + P - np.arange(2 * P)[None, :]
    own = np.where((dist >= 0) & (dist < WINDOW), 0.0, NEG)
    first = np.full((P, T), NEG)
    first[:, :P] = own[:, P:]
    put("window", np.stack([first, own], 1))
    d = 255 - np.arange(2 * T - 1)
    dd = np.clip(d, 0, WINDOW - 1)
    half = N_BUCKETS // 2
    dm = np.maximum(dd, 1).astype(np.float32)
    large = half + (np.log(dm / np.float32(half)) / np.float32(np.log(P / half)) * np.float32(N_BUCKETS - half)).astype(np.int32)
    bucket = np.where(dd < half, dd, np.minimum(large, N_BUCKETS - 1))
    line = (bucket[None, :] == np.arange(N_BUCKETS)[:, None]).astype(np.float32)
    put("bucket", np.concatenate([line, np.zeros((N_BUCKETS, 1))], 1))
    cs = np.clip(np.arange(GRID_W) - WIN_W // 2, 0, GRID_W - WIN_W)[i % GRID_W][:, None]
    kc = np.arange(GRID_W)[None, :]
    put("na_mask", np.tile(np.where((kc >= cs) & (kc < cs + WIN_W), 0.0, NEG), (1, ROWS)))
    n_freq = HD // 4
    inv = np.float32(10000.0) ** (-np.arange(n_freq, dtype=np.float32) / n_freq)
    t = np.arange(T)
    ang = np.zeros((P, T), np.float32)
    turn = np.zeros((P, P))
    for p in range(P):
        pos = t // GRID_W if (p % HD) < HD // 2 else t % GRID_W
        ang[p] = pos.astype(np.float32) * inv[p % n_freq]
        if p % (2 * n_freq) < n_freq:
            turn[p + n_freq, p] = -1.0
        else:
            turn[p - n_freq, p] = 1.0
    put("cos", np.cos(ang))
    put("sin", np.sin(ang))
    put("turn", turn)
    j = np.arange(E)
    put("earlier", np.tile((j[None, :] < j[:, None]).astype(np.float32), (P, 1, 1)))
    put("block_no", np.tile(np.arange(2 * E, dtype=np.float32), (P, 1)))
    n = 0
    for name, (full, shape) in parts.items():
        at[name] = (n, shape)
        n += full.shape[1]
    return np.ascontiguousarray(np.concatenate([f for f, _ in parts.values()], 1).astype(np.float32)), at


VEC = {}
_n = 0
for _name, _w in (("ffn1", 8), ("mix", 8), ("ffn2", 8), ("dw", 2 * CONV_K), ("dw_b", 2), ("ln_g", 2), ("ln_b", 2),
                  ("sc", 2 * SC_K), ("swa_q", 1), ("swa_k", 1), ("fox_q", 1), ("fox_k", 1), ("b_forget", 4), ("sink", 4)):
    VEC[_name] = (_n, _w)
    _n += _w
NVEC = _n
VEC2 = {}
_n = 0
for _name, _w in (("c", 8), ("c_ctx", 8), ("b_ada", 48), ("mix_pre", 8), ("mix_post", 8), ("ffn_pre", 8), ("ffn_post", 8),
                  ("gates", 16), ("head", 4), ("b_router", 32)):
    VEC2[_name] = (_n, _w)
    _n += _w
NVEC2 = _n


PHASES = []


@contextmanager
def phase(nc, names):
    PHASES.append(len(PHASES))
    sems = {n: nc.alloc_semaphore(f"{n}_phase{len(PHASES)}") for n in names.split()}
    with nc.Block() as block:
        yield block, dict(sems)
    nc.clear_and_free_semaphores(list(sems.values()))
    nc.all_engine_barrier()


class Chain:

    def __init__(self, eng, sem):
        self.eng, self.sem, self.n = eng, sem, 0

    def did(self, ins):
        ins.then_inc(self.sem, 1)
        self.n += 1
        return self.n

    def link(self, ins):
        self.did(ins)
        self.eng.wait_ge(self.sem, self.n)


NORM = "sq_ready ms_ready var_ready std_ready h_normed norm_chain "


def norm_act(act, nc, s, x, sq):
    nc.scalar.activation(sq, x, ACT.Square).then_inc(s["sq_ready"], 1)
    act.wait_ge(s["var_ready"], 1)
    nc.scalar.activation(s["std"], s["var"], ACT.Sqrt).then_inc(s["std_ready"], 1)


def norm_pe(pe, nc, s, sq, ms, mean, n):
    pe.wait_ge(s["sq_ready"], 1)
    for k in range(n):
        mm = nc.tensor.matmul(ms, mean, sq[:, k, :], start=(k == 0), stop=(k == n - 1))
    mm.then_inc(s["ms_ready"], 1)


def norm_dve(dve, nc, s, x, h, ms, gain, n):
    dve.wait_ge(s["ms_ready"], 1)
    nc.vector.tensor_scalar(s["var"], ms, EPS, None, ALU.add).then_inc(s["var_ready"], 1)
    dve.wait_ge(s["std_ready"], 1)
    nc.vector.reciprocal(s["rstd"], s["std"]).then_inc(s["norm_chain"], 1)
    dve.wait_ge(s["norm_chain"], 1)
    for k in range(n):
        last = nc.vector.scalar_tensor_tensor(h[:, k, :], x[:, k, :], gain[:, k:k + 1], s["rstd"], ALU.mult, ALU.mult)
    last.then_inc(s["h_normed"], 1)


def product(nc, out, w_hi, w_lo, x_hi, x_lo, start, stop):
    nc.tensor.matmul(out, w_hi, x_hi, start=start, stop=False, skip_group_check=True)
    nc.tensor.matmul(out, w_hi, x_lo, start=False, stop=False, skip_group_check=True)
    return nc.tensor.matmul(out, w_lo, x_hi, start=False, stop=stop, skip_group_check=True)


def split_dve(dve, nc, x, hi, lo, hi_done, lo_done, n):
    nc.vector.tensor_copy(hi, x).then_inc(hi_done, 1)
    dve.wait_ge(hi_done, n)
    nc.vector.tensor_tensor(lo, x, hi.bitcast(F32), ALU.subtract).then_inc(lo_done, 1)


SPLIT = "h_hi_done h_lo_done "


def split_h(dve, nc, s, B):
    dve.wait_ge(s["h_normed"], 1)
    split_dve(dve, nc, B.sq, B.h_hi, B.h_lo, s["h_hi_done"], s["h_lo_done"], 1)


def wait(eng, sem, value):
    if not isinstance(value, int) or value > 0:
        eng.wait_ge(sem, value)


def turns(eng, n, unroll, body):
    rounds = n // unroll
    for r in range(unroll):
        body(r, r, n, 0)
    if rounds > 2:
        with eng.Fori(1, rounds - 1) as i:
            for r in range(unroll):
                body(i * unroll + r, r, None, i)
    if rounds > 1:
        for r in range(unroll):
            body((rounds - 1) * unroll + r, r, n, rounds - 1)


AHEAD = 2


def project_sems(tag, ring):
    return " ".join(f"{tag}_w{r}" for r in range(ring)) + f" {tag}_hi {tag}_lo {tag}_mm {tag}_out "


def project_sp(sp, s, tag, wsrc, raw, ring, n):
    def load(c, r, end, i):
        wait(sp, s[f"{tag}_lo"], c - ring + 1)
        sp.dma_start(raw[:, r], wsrc(c)).then_inc(s[f"{tag}_w{r}"], 16)

    turns(sp, n, ring, load)


def project_pe(pe, nc, s, tag, B, x_hi, x_lo, bank, ring, n, tokens):
    def chunk(c, r, end, i):
        pe.wait_ge(s[f"{tag}_lo"], c + 1)
        wait(pe, s[f"{tag}_out"], c - ring + 1)
        for k in range(KD):
            w = slice(k * P, (k + 1) * P)
            mm = product(nc, bank(r)[:, 0:tokens], B.w_hi[:, r, w], B.w_lo[:, r, w], x_hi[:, k, :], x_lo[:, k, :],
                         k == 0, k == KD - 1)
        mm.then_inc(s[f"{tag}_mm"], 1)

    turns(pe, n, ring, chunk)


def project_act(act, nc, s, tag, B, ring, n, move=None):
    def upper(c, r, i):
        act.wait_ge(s[f"{tag}_w{r % ring}"], (i + r // ring) * 16 + 16)
        wait(act, s[f"{tag}_mm"], c - ring + 1)
        nc.scalar.copy(B.w_hi[:, r % ring], B.raw[:, r % ring]).then_inc(s[f"{tag}_hi"], 1)

    def turn(c, r, end, i):
        if end is None or c + AHEAD < end:
            upper(c + AHEAD, r + AHEAD, i)
        if move is not None:
            act.wait_ge(s[f"{tag}_mm"], c + 1)
            move(c, r).then_inc(s[f"{tag}_out"], 1)

    for c in range(AHEAD):
        upper(c, c, 0)
    turns(act, n, ring, turn)


def lower_half(dve, nc, s, tag, B, c, slot):
    dve.wait_ge(s[f"{tag}_hi"], c + 1)
    nc.vector.tensor_tensor(B.w_lo[:, slot], B.raw[:, slot], B.w_hi[:, slot].bitcast(F32),
                            ALU.subtract).then_inc(s[f"{tag}_lo"], 1)


def project_dve(dve, nc, s, tag, B, ring, n, move=None):
    lower = lambda c, r: lower_half(dve, nc, s, tag, B, c, r % ring)

    def turn(c, r, end, i):
        if end is None or c + AHEAD < end:
            lower(c + AHEAD, r + AHEAD)
        if move is not None:
            dve.wait_ge(s[f"{tag}_mm"], c + 1)
            move(c, r).then_inc(s[f"{tag}_out"], 1)

    for c in range(AHEAD):
        lower(c, c)
    turns(dve, n, ring, turn)


def ffn_phase(nc, B, l, wg, wu, wd, gain):
    with ExitStack() as ctx:
        (raw, sil, hid) = alloc(nc, ctx, B, raw=(P, 6, D), sil=(P, 2, T), hid=(P, 2, T))
        (hi, lo, hid_hi, hid_lo) = alloc(nc, ctx, B, F32R, hi=(P, 6, D), lo=(P, 6, D), hid_hi=(P, 2, T), hid_lo=(P, 2, T))
        ffn_program(nc, B, l, dict(g=wg, u=wu, d=wd), gain, raw, hi, lo, sil, hid, hid_hi, hid_lo)


def ffn_program(nc, B, l, src, gain, raw, hi, lo, sil, hid, hid_hi, hid_lo):
    x, ps, con = B.x, B.ps, B.con
    acc = ps[:, 0:4, :].rearrange("p b (c t) -> p (b c) t", t=T)
    gu = [ps[:, 4 + a, :].rearrange("p (w t) -> p w t", t=T) for a in range(2)]
    ms = ps[:, 6, 0:T]
    slot = {"g": 0, "u": 2, "d": 4}
    names = " ".join(f"w{k}{a}" for k in "gud" for a in range(2)) + " " + " ".join(f"{k}_{h}" for k in "gud" for h in ("hi", "lo"))
    with phase(nc, NORM + SPLIT + names + " gu_done silu_done hid_mul hid_hi_done hidden_ready down_done x_done") as (block, s):
        s.update(std=B.std[:, 0:T], var=B.var[:, 0:T], rstd=B.rstd[:, 0:T])

        @block.sync
        def _(sp):
            def load(c, a, end, i):
                for k in "gud":
                    wait(sp, s[f"{k}_lo"], c - 1)
                    sp.dma_start(raw[:, slot[k] + a], src[k][l, c]).then_inc(s[f"w{k}{a}"], 16)

            turns(sp, FC, 2, load)

        @block.tensor
        def _(pe):
            for b in range(4):
                nc.tensor.matmul(ps[:, b, :], con("zeros")[:, 0:P], con("zeros"), start=True, stop=False,
                                 skip_group_check=True)
            norm_pe(pe, nc, s, B.sq, ms, con("mean_d"), KD)
            pe.wait_ge(s["h_lo_done"], 1)

            def gate_up(c, a):
                wait(pe, s["hidden_ready"], c - 1)
                for j, kind in enumerate("gu"):
                    pe.wait_ge(s[f"{kind}_lo"], c + 1)
                    for k in range(KD):
                        w = slice(k * P, (k + 1) * P)
                        mm = product(nc, gu[a][:, j, :], hi[:, slot[kind] + a, w], lo[:, slot[kind] + a, w],
                                     B.h_hi[:, k, :], B.h_lo[:, k, :], k == 0, k == KD - 1)
                mm.then_inc(s["gu_done"], 1)

            def down(c, a):
                pe.wait_ge(s["hidden_ready"], c + 1)
                pe.wait_ge(s["d_lo"], c + 1)
                for k in range(KD):
                    w = slice(k * P, (k + 1) * P)
                    mm = product(nc, acc[:, k, :], hi[:, slot["d"] + a, w], lo[:, slot["d"] + a, w],
                                 hid_hi[:, a, :], hid_lo[:, a, :], False, False)
                mm.then_inc(s["down_done"], 1)

            gate_up(0, 0)
            gate_up(1, 1)
            down(0, 0)
            with pe.Fori(1, FC // 2) as i:
                gate_up(2 * i, 0)
                down(2 * i - 1, 1)
                gate_up(2 * i + 1, 1)
                down(2 * i, 0)
            down(FC - 1, 1)

        @block.scalar
        def _(act):
            def upper(kind, c, a, i):
                act.wait_ge(s[f"w{kind}{a % 2}"], (i + a // 2) * 16 + 16)
                if kind == "d":
                    wait(act, s["down_done"], c - 1)
                else:
                    wait(act, s["gu_done"], c - 1)
                nc.scalar.copy(hi[:, slot[kind] + a % 2], raw[:, slot[kind] + a % 2]).then_inc(s[f"{kind}_hi"], 1)

            def turn(c, a, end, i):
                if end is None or c + 1 < end:
                    upper("g", c + 1, a + 1, i)
                    upper("u", c + 1, a + 1, i)
                upper("d", c, a, i)
                act.wait_ge(s["gu_done"], c + 1)
                wait(act, s["hid_mul"], c - 1)
                nc.scalar.activation(sil[:, a, :], gu[a][:, 0, :], ACT.Silu).then_inc(s["silu_done"], 1)

            norm_act(act, nc, s, x, B.sq)
            upper("g", 0, 0, 0)
            upper("u", 0, 0, 0)
            turns(act, FC, 2, turn)

        @block.vector
        def _(dve):
            def lower(kind, c, a):
                dve.wait_ge(s[f"{kind}_hi"], c + 1)
                j = slot[kind] + a % 2
                nc.vector.tensor_tensor(lo[:, j], raw[:, j], hi[:, j].bitcast(F32), ALU.subtract).then_inc(s[f"{kind}_lo"], 1)

            def turn(c, a, end, i):
                if end is None or c + 1 < end:
                    lower("g", c + 1, a + 1)
                    lower("u", c + 1, a + 1)
                lower("d", c, a)
                dve.wait_ge(s["silu_done"], c + 1)
                nc.vector.tensor_tensor(hid[:, a, :], sil[:, a, :], gu[a][:, 1, :], ALU.mult).then_inc(s["hid_mul"], 1)
                dve.wait_ge(s["hid_mul"], c + 1)
                wait(dve, s["down_done"], c - 1)
                split_dve(dve, nc, hid[:, a, :], hid_hi[:, a, :], hid_lo[:, a, :], s["hid_hi_done"], s["hidden_ready"], c + 1)

            norm_dve(dve, nc, s, x, B.sq, ms, gain, KD)
            split_h(dve, nc, s, B)
            lower("g", 0, 0)
            lower("u", 0, 0)
            turns(dve, FC, 2, turn)
            dve.wait_ge(s["down_done"], FC)
            for b in range(4):
                nc.vector.scalar_tensor_tensor(x[:, 2 * b:2 * b + 2, :], acc[:, 2 * b:2 * b + 2, :], 0.5,
                                               x[:, 2 * b:2 * b + 2, :], ALU.mult, ALU.add).then_inc(s["x_done"], 1)
            dve.wait_ge(s["x_done"], 4)


def z_phase(nc, B, l, w_z, gain):
    ps, con = B.ps, B.con
    ring = 4
    with phase(nc, NORM + SPLIT + project_sems("z", ring) + "ff_w ff_mm ff_out") as (block, s):
        s.update(std=B.std[:, 0:T], var=B.var[:, 0:T], rstd=B.rstd[:, 0:T])

        @block.sync
        def _(sp):
            sp.dma_start(B.w_ff, B.d_wff[l]).then_inc(s["ff_w"], 16)
            project_sp(sp, s, "z", lambda c: w_z[l, c], B.raw, ring, ZC)

        @block.tensor
        def _(pe):
            norm_pe(pe, nc, s, B.sq, ps[:, 6, 0:T], con("mean_d"), KD)
            pe.wait_ge(s["h_normed"], 1)
            pe.wait_ge(s["ff_w"], 16)
            for c in range(TC):
                for k in range(KD):
                    mm = nc.tensor.matmul(ps[:, 7, 4 * c:4 * c + 4], B.sq[:, k, c * P:(c + 1) * P],
                                          B.w_ff[:, k, :], start=(k == 0), stop=(k == KD - 1))
            mm.then_inc(s["ff_mm"], 1)
            pe.wait_ge(s["h_lo_done"], 1)
            project_pe(pe, nc, s, "z", B, B.h_hi, B.h_lo, lambda r: ps[:, r, :], ring, ZC, T)

        @block.scalar
        def _(act):
            norm_act(act, nc, s, B.x, B.sq)
            project_act(act, nc, s, "z", B, ring, ZC, lambda c, r: nc.scalar.copy(B.z[:, c, :], ps[:, r, 0:T]))

        @block.vector
        def _(dve):
            norm_dve(dve, nc, s, B.x, B.sq, ps[:, 6, 0:T], gain, KD)
            split_h(dve, nc, s, B)
            project_dve(dve, nc, s, "z", B, ring, ZC)
            dve.wait_ge(s["ff_mm"], 1)
            nc.vector.tensor_copy(B.ff, ps[:, 7, 0:8]).then_inc(s["ff_out"], 1)
            dve.wait_ge(s["ff_out"], 1)


CA, CB, SB, SC, SX, AQ, AK, AV, FQ, FK, FV = 0, 2, 4, 6, 8, 10, 12, 13, 14, 16, 18


def branch_phase(nc, B, l, w_g):
    ps, con, z, vec = B.ps, B.con, B.z, B.vec
    ring = 4
    v = lambda name, j=0, n=1: vec[:, VEC[name][0] + j:VEC[name][0] + j + n]
    with phase(nc, project_sems("g", ring) + "qk_sq qk_ms qk_var qk_std qk_rstd qk_spread v_turned v_copied sig "
               "ff_in ff_exp ff_in2 ff_ln conv_done conv_sq cen_in mean cen var std ln_in silu chain done") as (block, s):
        msq = ps[0:14, 6, 0:T]

        @block.sync
        def _(sp):
            project_sp(sp, s, "g", lambda c: w_g[l, c], B.raw, ring, GC)

        @block.tensor
        def _(pe):
            pe.wait_ge(s["qk_sq"], 2)
            for c in range(7):
                mm = nc.tensor.matmul(msq, con("head_mean")[:, c, :], B.qksq[:, c, :], start=(c == 0), stop=(c == 6))
            mm.then_inc(s["qk_ms"], 1)
            for j, c in enumerate((AV, FV, FV + 1)):
                for t in range(TC):
                    n = j * TC + t
                    mm = nc.tensor.transpose(ps[:, 4 + n // 4, (n % 4) * P:(n % 4 + 1) * P],
                                             z[:, c, t * P:(t + 1) * P], con("ident"))
            mm.then_inc(s["v_turned"], 1)
            pe.wait_ge(s["qk_rstd"], 1)
            for c in range(7):
                mm = nc.tensor.matmul(ps[:, c // 2, (c % 2) * T:(c % 2 + 1) * T], con("head_spread")[0:14, c, :],
                                      B.hrstd[0:14, :], start=(c % 2 == 0), stop=True, skip_group_check=True)
            mm.then_inc(s["qk_spread"], 1)
            pe.wait_ge(s["done"], 1)
            project_pe(pe, nc, s, "g", B, B.h_hi, B.h_lo, lambda r: ps[:, r, :], ring, GC, T)
            pe.wait_ge(s["conv_done"], 1)
            for c in range(2):
                mm = nc.tensor.matmul(ps[:, 4, 0:T], con("mean_conv"), B.u[:, c, :], start=(c == 0), stop=(c == 1))
            mm.then_inc(s["mean"], 1)
            pe.wait_ge(s["conv_sq"], 1)
            for c in range(2):
                mm = nc.tensor.matmul(ps[:, 5, 0:T], con("mean_conv"), B.sq[:, c, :], start=(c == 0), stop=(c == 1))
            mm.then_inc(s["var"], 1)

        @block.scalar
        def _(act):
            nc.scalar.activation(B.qksq[:, 0:3, :], z[:, AQ:AQ + 3, :], ACT.Square).then_inc(s["qk_sq"], 1)
            nc.scalar.activation(B.qksq[:, 3:7, :], z[:, FQ:FQ + 4, :], ACT.Square).then_inc(s["qk_sq"], 1)
            nc.scalar.activation(B.u, z[:, CB:CB + 2, :], ACT.Sigmoid).then_inc(s["sig"], 1)
            act.wait_ge(s["qk_var"], 1)
            nc.scalar.activation(B.hstd[0:14, :], B.hvar[0:14, :], ACT.Sqrt).then_inc(s["qk_std"], 1)
            act.wait_ge(s["ff_in"], 1)
            nc.scalar.activation(B.ffe, B.ffn_, ACT.Exp).then_inc(s["ff_exp"], 1)
            act.wait_ge(s["ff_in2"], 1)
            nc.scalar.activation(B.ffn_, B.ffe, ACT.Ln).then_inc(s["ff_ln"], 1)
            project_act(act, nc, s, "g", B, ring, GC,
                        lambda c, r: nc.scalar.activation(B.gates[:, c, :], ps[:, r, 0:T], ACT.Sigmoid))
            act.wait_ge(s["cen"], 1)
            nc.scalar.activation(B.sq[:, 0:2, :], B.u, ACT.Square).then_inc(s["conv_sq"], 1)
            act.wait_ge(s["cen_in"], 1)
            nc.scalar.activation(B.std[:, 0:T], B.var[:, 0:T], ACT.Sqrt).then_inc(s["std"], 1)
            act.wait_ge(s["ln_in"], 1)
            nc.scalar.activation(B.b_conf, B.u, ACT.Silu).then_inc(s["silu"], 1)
            act.wait_ge(s["silu"], 1)

        @block.vector
        def _(dve):
            ch = Chain(dve, s["chain"])
            dve.wait_ge(s["qk_ms"], 1)
            nc.vector.tensor_scalar(B.hvar[0:14, :], msq, EPS, None, ALU.add).then_inc(s["qk_var"], 1)
            for t in range(TC):
                ch.did(nc.vector.tensor_tensor(B.ff[:, 4 * t:4 * t + 4], B.ff[:, 4 * t:4 * t + 4], v("b_forget", 0, 4), ALU.add))
            dve.wait_ge(s["chain"], ch.n)
            ch.link(nc.vector.tensor_scalar(B.ffe, B.ff, -1.0, None, ALU.mult))
            nc.vector.tensor_tensor(B.ffn_, B.ff, B.ffe, ALU.min).then_inc(s["ff_in"], 1)
            dve.wait_ge(s["qk_std"], 1)
            nc.vector.reciprocal(B.hrstd[0:14, :], B.hstd[0:14, :]).then_inc(s["qk_rstd"], 1)
            dve.wait_ge(s["ff_exp"], 1)
            ch.link(nc.vector.tensor_scalar(B.ffe, B.ffe, 1.0, None, ALU.add))
            nc.vector.tensor_scalar(B.ff, B.ff, 0.0, None, ALU.min).then_inc(s["ff_in2"], 1)
            dve.wait_ge(s["v_turned"], 1)
            for j in range(3):
                for t in range(TC):
                    n = j * TC + t
                    last = nc.vector.tensor_copy(B.vtok[:, t, j * P:(j + 1) * P],
                                                 ps[:, 4 + n // 4, (n % 4) * P:(n % 4 + 1) * P])
            last.then_inc(s["v_copied"], 1)
            for j, name in ((0, "swa_q"), (1, "fox_q")):
                ch.link(nc.vector.tensor_scalar(B.qgain[:, j:j + 1], v(name), HD ** -0.5, None, ALU.mult))
            dve.wait_ge(s["qk_spread"], 1)
            for c, (zc, g) in enumerate(((AQ, B.qgain[:, 0:1]), (AQ + 1, B.qgain[:, 0:1]), (AK, v("swa_k")),
                                         (FQ, B.qgain[:, 1:2]), (FQ + 1, B.qgain[:, 1:2]), (FK, v("fox_k")),
                                         (FK + 1, v("fox_k")))):
                ch.did(nc.vector.scalar_tensor_tensor(z[:, zc, :], z[:, zc, :], g, ps[:, c // 2, (c % 2) * T:(c % 2 + 1) * T],
                                                      ALU.mult, ALU.mult))
            dve.wait_ge(s["chain"], ch.n)
            for g in range(2):
                for half in range(2):
                    last = nc.vector.tensor_copy(B.kdup[half * HD:(half + 1) * HD, g, :], z[g * HD:(g + 1) * HD, AK, :])
            last.then_inc(s["done"], 1)
            dve.wait_ge(s["ff_ln"], 1)
            ch.link(nc.vector.tensor_tensor(B.ff, B.ff, B.ffn_, ALU.subtract))
            for h in range(4):
                ch.did(nc.vector.tensor_scalar(B.lfa0[:, h, :], con("upto")[:, 0, :], B.ff[:, h:h + 1], None, ALU.mult))
                ch.did(nc.vector.tensor_scalar(B.lfa1[:, h, :], con("upto")[:, 1, P:T], B.ff[:, 4 + h:5 + h], None, ALU.mult))
            pad = CONV_K - 1
            for c in range(2):
                ch.did(nc.vector.memset(B.upad[:, c, 0:pad], 0.0))
            ch.did(nc.vector.tensor_tensor(B.upad[:, :, pad:], z[:, SC:SC + 2, :], z[:, SX:SX + 2, :], ALU.mult))
            dve.wait_ge(s["chain"], ch.n)
            for j in range(SC_K):
                for c in range(2):
                    w = v("sc", c * SC_K + j)
                    x_in = B.upad[:, c, pad - SC_K + 1 + j:pad - SC_K + 1 + j + T]
                    if j == 0:
                        ch.did(nc.vector.tensor_scalar(B.b_sc[:, c, :], x_in, w, None, ALU.mult))
                    else:
                        dve.wait_ge(s["chain"], ch.n - 1)
                        ch.did(nc.vector.scalar_tensor_tensor(B.b_sc[:, c, :], x_in, w, B.b_sc[:, c, :], ALU.mult, ALU.add))
            dve.wait_ge(s["chain"], ch.n)
            ch.did(nc.vector.tensor_tensor(B.b_sc, B.b_sc, z[:, SB:SB + 2, :], ALU.mult))
            dve.wait_ge(s["sig"], 1)
            ch.link(nc.vector.tensor_tensor(B.upad[:, :, pad:], z[:, CA:CA + 2, :], B.u, ALU.mult))
            for j in range(CONV_K):
                lower_half(dve, nc, s, "g", B, j, j % ring)
                for c in range(2):
                    w = v("dw", c * CONV_K + j)
                    x_in = B.upad[:, c, j:j + T]
                    if j == 0:
                        ch.did(nc.vector.tensor_scalar(B.u[:, c, :], x_in, w, v("dw_b", c), ALU.mult, ALU.add))
                    else:
                        dve.wait_ge(s["chain"], ch.n - 1)
                        ch.did(nc.vector.scalar_tensor_tensor(B.u[:, c, :], x_in, w, B.u[:, c, :], ALU.mult, ALU.add))
            for j in range(CONV_K, GC):
                lower_half(dve, nc, s, "g", B, j, j % ring)
            dve.wait_ge(s["chain"], ch.n)
            dve.sem_inc(s["conv_done"], 1)
            dve.wait_ge(s["mean"], 1)
            for c in range(2):
                ch.did(nc.vector.tensor_tensor(B.u[:, c, :], B.u[:, c, :], ps[:, 4, 0:T], ALU.subtract))
            dve.wait_ge(s["chain"], ch.n)
            dve.sem_inc(s["cen"], 1)
            dve.wait_ge(s["var"], 1)
            nc.vector.tensor_scalar(B.var[:, 0:T], ps[:, 5, 0:T], EPS, None, ALU.add).then_inc(s["cen_in"], 1)
            dve.wait_ge(s["std"], 1)
            ch.link(nc.vector.reciprocal(B.rstd[:, 0:T], B.std[:, 0:T]))
            for c in range(2):
                ch.did(nc.vector.scalar_tensor_tensor(B.u[:, c, :], B.u[:, c, :], v("ln_g", c), B.rstd[:, 0:T],
                                                      ALU.mult, ALU.mult))
            dve.wait_ge(s["chain"], ch.n)
            for c in range(2):
                ch.did(nc.vector.tensor_scalar(B.u[:, c, :], B.u[:, c, :], v("ln_b", c), None, ALU.add))
            dve.wait_ge(s["chain"], ch.n)
            dve.sem_inc(s["ln_in"], 1)


DEPTH_A = 3


def attention_phase(nc, B, units, width, prefetch=None):
    ps, con = B.ps, B.con
    n = len(units)
    with phase(nc, "scores_ready max_ready exp_ready probs_ready turned probs_t_ready out_ready out_copied chain prefetched") as (block, s):

        @block.sync
        def _(sp):
            if prefetch is not None:
                sp.dma_start(*prefetch).then_inc(s["prefetched"], 16)
                sp.wait_ge(s["prefetched"], 16)

        @block.tensor
        def _(pe):
            def scores(u):
                if u >= DEPTH_A:
                    pe.wait_ge(s["max_ready"], u - DEPTH_A + 1)
                units[u]["scores"](ps[:, u % DEPTH_A, 0:width]).then_inc(s["scores_ready"], 1)

            def turn(u):
                pe.wait_ge(s["probs_ready"], u + 1)
                if u >= 2:
                    pe.wait_ge(s["probs_t_ready"], u - 1)
                for j in range(width // P):
                    mm = nc.tensor.transpose(ps[:, 3 + u % 2, j * P:(j + 1) * P], B.prob[:, u % DEPTH_A, j * P:(j + 1) * P],
                                             con("ident"))
                mm.then_inc(s["turned"], 1)

            def values(u):
                pe.wait_ge(s["probs_t_ready"], u + 1)
                if u >= 2:
                    pe.wait_ge(s["out_copied"], u - 1)
                v = units[u]["values"]
                lo = units[u]["row"]
                for j, vj in enumerate(v):
                    mm = nc.tensor.matmul(ps[lo:lo + HD, 5 + u % 2, 0:P], vj, B.prob_t[:, u % 2, j * P:(j + 1) * P],
                                          start=(j == 0), stop=(j == len(v) - 1))
                mm.then_inc(s["out_ready"], 1)

            scores(0)
            scores(1)
            for u in range(n + 1):
                if u + 2 < n:
                    scores(u + 2)
                if u < n:
                    turn(u)
                if u >= 1:
                    values(u - 1)

        @block.scalar
        def _(act):
            def turned_copy(u):
                act.wait_ge(s["turned"], u + 1)
                if u >= 2:
                    act.wait_ge(s["out_ready"], u - 1)
                nc.scalar.copy(B.prob_t[:, u % 2, 0:width], ps[:, 3 + u % 2, 0:width]).then_inc(s["probs_t_ready"], 1)

            for u in range(n + 1):
                if u < n:
                    act.wait_ge(s["max_ready"], u + 1)
                    if units[u]["sink"] is not None:
                        nc.scalar.activation(B.stat[:, u % DEPTH_A, 2:3], units[u]["sink"], ACT.Exp, bias=B.stat[:, u % DEPTH_A, 0:1])
                    nc.scalar.activation(B.prob[:, u % DEPTH_A, 0:width], B.prob[:, u % DEPTH_A, 0:width], ACT.Exp,
                                         bias=B.stat[:, u % DEPTH_A, 0:1], accum_out=B.stat[:, u % DEPTH_A, 1:2]).then_inc(s["exp_ready"], 1)
                if u >= 1:
                    turned_copy(u - 1)

        @block.vector
        def _(dve):
            ch = Chain(dve, s["chain"])

            def masked_max(u):
                dve.wait_ge(s["scores_ready"], u + 1)
                if u >= DEPTH_A:
                    dve.wait_ge(s["turned"], u - DEPTH_A + 1)
                table = units[u]["table"]
                m = table.shape[1]
                ch.did(nc.vector.tensor_tensor(B.prob[:, u % DEPTH_A, 0:m], ps[:, u % DEPTH_A, 0:m], table, ALU.add))
                if m < width:
                    ch.did(nc.vector.tensor_copy(B.prob[:, u % DEPTH_A, m:width], ps[:, u % DEPTH_A, m:width]))
                dve.wait_ge(s["chain"], ch.n)
                nm = B.stat[:, u % DEPTH_A, 0:1]
                red = nc.vector.tensor_reduce(nm, B.prob[:, u % DEPTH_A, 0:width], AX, ALU.max, negate=True)
                if units[u]["sink"] is not None:
                    ch.link(red)
                    red = nc.vector.tensor_tensor(nm, nm, units[u]["minus_sink"], ALU.min)
                red.then_inc(s["max_ready"], 1)

            def norm(u):
                dve.wait_ge(s["exp_ready"], u + 1)
                den = B.stat[:, u % DEPTH_A, 1:2]
                if units[u]["sink"] is not None:
                    ch.link(nc.vector.tensor_tensor(den, den, B.stat[:, u % DEPTH_A, 2:3], ALU.add))
                ch.link(nc.vector.reciprocal(B.stat[:, u % DEPTH_A, 3:4], den))
                nc.vector.tensor_scalar(B.prob[:, u % DEPTH_A, 0:width], B.prob[:, u % DEPTH_A, 0:width], B.stat[:, u % DEPTH_A, 3:4], None,
                                        ALU.mult).then_inc(s["probs_ready"], 1)

            def out(u):
                dve.wait_ge(s["out_ready"], u + 1)
                lo = units[u]["row"]
                nc.vector.tensor_copy(units[u]["out"], ps[lo:lo + HD, 5 + u % 2, 0:P]).then_inc(s["out_copied"], 1)

            for u in range(n + 3):
                if u < n:
                    masked_max(u)
                if 1 <= u <= n:
                    norm(u - 1)
                if u >= 3:
                    out(u - 3)
            dve.wait_ge(s["out_copied"], n)


def first_attention(nc, B, prefetch):
    ps, con, z = B.ps, B.con, B.z
    units = []
    for h in range(4):
        lo = (h % 2) * HD
        for qc in range(TC):
            def swa(dst, h=h, lo=lo, qc=qc):
                return nc.tensor.matmul(dst, z[lo:lo + HD, AQ + h // 2, qc * P:(qc + 1) * P], B.kdup[lo:lo + HD, h // 2, :],
                                        start=True, stop=True)

            units.append(dict(scores=swa, table=B.swa_table[:, h * TC + qc, :], sink=B.vec[:, VEC["sink"][0] + h:VEC["sink"][0] + h + 1],
                              minus_sink=B.nsink[:, h:h + 1], row=lo,
                              values=[B.vtok[:, t, (h // 2) * HD:(h // 2 + 1) * HD] for t in range(TC)],
                              out=B.b_swa[lo:lo + HD, h // 2, qc * P:(qc + 1) * P]))
    for h in range(4):
        lo = (h % 2) * HD
        for qc in range(TC):
            def fox(dst, h=h, lo=lo, qc=qc):
                nc.tensor.matmul(dst, z[lo:lo + HD, FQ + h // 2, qc * P:(qc + 1) * P], z[lo:lo + HD, FK + h // 2, :],
                                 start=True, stop=False)
                mm = nc.tensor.matmul(dst, B.lfa0[:, h, qc * P:(qc + 1) * P], con("after")[:, 0, 0:T], start=False, stop=(qc == 0))
                if qc == 1:
                    mm = nc.tensor.matmul(dst, B.lfa1[:, h, :], con("after")[:, 1, 0:T], start=False, stop=True)
                return mm

            units.append(dict(scores=fox, table=con("causal")[:, qc, :], sink=None, row=lo,
                              values=[B.vtok[:, t, P + h * HD:P + (h + 1) * HD] for t in range(TC)],
                              out=B.b_fox[lo:lo + HD, h // 2, qc * P:(qc + 1) * P]))
    attention_phase(nc, B, units, T, prefetch)


def merge_phase(nc, B, acts, per, gates, n_branch):
    ps = B.ps
    with phase(nc, SPLIT + "prod merged chain") as (block, s):
        nb2 = n_branch // 2

        @block.tensor
        def _(pe):
            for c in range(KD):
                if c >= 2:
                    pe.wait_ge(s["merged"], c - 1)
                for b in range(n_branch):
                    bank = ps[:, (c % 2) * 2 + b // 2, (b % 2) * T:(b % 2 + 1) * T]
                    for k in range(per):
                        mm = nc.tensor.matmul(bank, B.wb[:, b * per + k, c * P:(c + 1) * P], acts[b][:, k, :],
                                              start=(k == 0), stop=(k == per - 1), skip_group_check=True)
                mm.then_inc(s["prod"], 1)

        @block.vector
        def _(dve):
            ch = Chain(dve, s["chain"])
            for c in range(KD):
                dve.wait_ge(s["prod"], c + 1)
                for b in range(nb2):
                    bank = ps[:, (c % 2) * 2 + b, :].rearrange("p (b t) -> p b t", t=T)
                    g = gates[:, 2 * b * KD + c:2 * b * KD + c + KD + 1:KD, :]
                    ch.did(nc.vector.tensor_tensor(B.mtmp[:, 2 * b:2 * b + 2, :], bank, g, ALU.mult))
                dve.wait_ge(s["chain"], ch.n)
                if nb2 == 2:
                    ch.link(nc.vector.tensor_tensor(B.mtmp[:, 0:2, :], B.mtmp[:, 0:2, :], B.mtmp[:, 2:4, :], ALU.add))
                nc.vector.tensor_tensor(B.sq[:, c, :], B.mtmp[:, 0, :], B.mtmp[:, 1, :], ALU.add).then_inc(s["merged"], 1)
                dve.wait_ge(s["merged"], c + 1)
                split_dve(dve, nc, B.sq[:, c, :], B.h_hi[:, c, 0:T], B.h_lo[:, c, 0:T], s["h_hi_done"], s["h_lo_done"], c + 1)
            dve.wait_ge(s["h_lo_done"], KD)


def out_phase(nc, B, wsrc, dst, add, ring=4):
    ps = B.ps
    with phase(nc, project_sems("o", ring)) as (block, s):

        @block.sync
        def _(sp):
            project_sp(sp, s, "o", wsrc, B.raw, ring, KD)

        @block.tensor
        def _(pe):
            pe_src = (B.h_hi[:, :, 0:T], B.h_lo[:, :, 0:T])
            project_pe(pe, nc, s, "o", B, *pe_src, lambda r: ps[:, r, :], ring, KD, T)

        @block.scalar
        def _(act):
            project_act(act, nc, s, "o", B, ring, KD)

        @block.vector
        def _(dve):
            def move(c, r):
                if add:
                    return nc.vector.tensor_tensor(dst[:, c, :], dst[:, c, :], ps[:, r, 0:T], ALU.add)
                return nc.vector.tensor_copy(dst[:, c, :], ps[:, r, 0:T])

            project_dve(dve, nc, s, "o", B, ring, KD, move)
            dve.wait_ge(s["o_out"], KD)


class Bufs:

    stage = "whole"


def alloc(nc, ctx, B, dtype=F32, **spec):
    made = []
    for name, shape in spec.items():
        t = ctx.enter_context(nc.sbuf_tensor(f"{name}_{B.stage}{len(PHASES)}", list(shape), dtype))
        made.append(t[tuple(slice(None) for _ in shape)])
    return made


def split_ring(nc, ctx, B, ring):
    (B.raw,) = alloc(nc, ctx, B, raw=(P, ring, D))
    B.w_hi, B.w_lo = alloc(nc, ctx, B, F32R, w_hi=(P, ring, D), w_lo=(P, ring, D))


def first_block_program(nc, B, I):
    B.stage = "first"
    with ExitStack() as ctx:
        (B.vec, B.nsink, B.swa_table) = alloc(nc, ctx, B, vec=(P, NVEC), nsink=(P, 4), swa_table=(P, 4 * TC, T))
        B.h_hi, B.h_lo = alloc(nc, ctx, B, F32R, h_hi=(P, KD, T), h_lo=(P, KD, T))
        with ExitStack() as small:
            (B.relb, B.line) = alloc(nc, small, B, relb=(N_BUCKETS, 4), line=(P, 4, 512))
            swa_table_phase(nc, B, I)
        with nc.Fori(0, DEPTH) as l:
            layer_vec_phase(nc, B, I, l)
            v = lambda name: B.vec[:, VEC[name][0]:VEC[name][0] + VEC[name][1]]
            ffn_phase(nc, B, l, I["ffn1_wg"], I["ffn1_wu"], I["ffn1_wd"], v("ffn1"))
            mixer(nc, B, I, l, v("mix"))
            ffn_phase(nc, B, l, I["ffn2_wg"], I["ffn2_wu"], I["ffn2_wd"], v("ffn2"))


def mixer(nc, B, I, l, gain):
    with ExitStack() as ctx:
        (B.w_ff, B.z, B.ff, B.ffe, B.ffn_, B.vtok, B.qgain, B.kdup, B.lfa0, B.lfa1, B.u, B.b_sc, B.gates,
         B.pp, B.stat) = alloc(
            nc, ctx, B, w_ff=(P, KD, 4),
            z=(P, ZC, T), ff=(P, 8), ffe=(P, 8), ffn_=(P, 8),
            vtok=(P, TC, 384), qgain=(P, 2), kdup=(P, 2, T), lfa0=(P, 4, T), lfa1=(P, 4, P),
            u=(P, 2, T), b_sc=(P, 2, T), gates=(P, GC, T),
            pp=(P, 2048), stat=(P, DEPTH_A, 4))
        B.qksq = B.pp[:, 0:7 * T].rearrange("p (c t) -> p c t", t=T)
        B.prob = B.pp[:, 0:DEPTH_A * T].rearrange("p (a t) -> p a t", t=T)
        B.prob_t = B.pp[:, DEPTH_A * T:(DEPTH_A + 2) * T].rearrange("p (a t) -> p a t", t=T)
        B.mtmp = B.pp[:, 1024:2048].rearrange("p (c t) -> p c t", t=T)
        padded = CONV_K - 1 + T
        B.upad = B.pp[:, 0:2 * padded].rearrange("p (c t) -> p c t", t=padded)
        B.hvar, B.hstd, B.hrstd = B.var[:, T:], B.std[:, T:], B.rstd[:, T:]
        B.b_conf = B.u
        B.d_wff = I["w_ff"]
        with ExitStack() as ring:
            split_ring(nc, ring, B, 4)
            z_phase(nc, B, l, I["w_z"], gain)
            branch_phase(nc, B, l, I["w_g"])
        with ExitStack() as whole:
            (B.wb, B.b_swa, B.b_fox) = alloc(nc, whole, B, wb=(P, 8, D), b_swa=(P, 2, T), b_fox=(P, 2, T))
            first_attention(nc, B, (B.wb, I["w_branch"][l]))
            merge_phase(nc, B, [B.b_conf, B.b_sc, B.b_swa, B.b_fox], 2, B.gates, 4)
    with ExitStack() as ring:
        split_ring(nc, ring, B, 4)
        out_phase(nc, B, lambda c: I["w_out"][l, c], B.x, True)


def swa_table_phase(nc, B, I):
    line = B.line
    ps, con = B.ps, B.con
    with phase(nc, "loaded relb_in line_mm line_ready line_out table_in masked") as (block, s):

        @block.sync
        def _(sp):
            sp.dma_start(B.con_all, I["const"]).then_inc(s["loaded"], 16)
            sp.dma_start(B.x, I["x"]).then_inc(s["loaded"], 16)
            sp.dma_start(B.relb, I["rel_bias"]).then_inc(s["relb_in"], 16)
            sp.wait_ge(s["line_ready"], 1)
            sp.dma_start(B.d_line, line).then_inc(s["line_out"], 16)
            sp.wait_ge(s["line_out"], 16)
            for h in range(4):
                for qc in range(TC):
                    skew = bass.AP(tensor=B.d_line.tensor, offset=h * 512 + P - 1 + (0 if qc else P), ap=[[4 * 512 - 1, P], [1, T]])
                    sp.dma_start(B.swa_table[:, h * TC + qc, :], skew).then_inc(s["table_in"], 16)
            sp.wait_ge(s["loaded"], 32)

        @block.tensor
        def _(pe):
            pe.wait_ge(s["loaded"], 32)
            pe.wait_ge(s["relb_in"], 16)
            for h in range(4):
                mm = nc.tensor.matmul(ps[:, h, :], B.relb[:, h:h + 1].broadcast_to([N_BUCKETS, P]), con("bucket")[0:N_BUCKETS, :],
                                      start=True, stop=True)
            mm.then_inc(s["line_mm"], 1)

        @block.vector
        def _(dve):
            dve.wait_ge(s["line_mm"], 1)
            nc.vector.tensor_copy(line, ps[:, 0:4, :]).then_inc(s["line_ready"], 1)
            dve.wait_ge(s["table_in"], 16 * 4 * TC)
            for h in range(4):
                nc.vector.tensor_tensor(B.swa_table[:, h * TC:(h + 1) * TC, :], B.swa_table[:, h * TC:(h + 1) * TC, :],
                                        con("window"), ALU.add).then_inc(s["masked"], 1)
            dve.wait_ge(s["masked"], 4)


def layer_vec_phase(nc, B, I, l):
    with phase(nc, "vec_in nsink_ready") as (block, s):

        @block.sync
        def _(sp):
            sp.dma_start(B.vec, I["vec"][l]).then_inc(s["vec_in"], 16)

        @block.vector
        def _(dve):
            dve.wait_ge(s["vec_in"], 16)
            nc.vector.tensor_scalar(B.nsink, B.vec[:, VEC["sink"][0]:VEC["sink"][0] + 4], -1.0, None,
                                    ALU.mult).then_inc(s["nsink_ready"], 1)
            dve.wait_ge(s["nsink_ready"], 1)


def bcast(a, axis, n):
    a = a.unsqueeze(axis)
    shape = list(a.shape)
    shape[axis] = n
    return a.broadcast_to(shape)


def load2_phase(nc, B, I):
    v2 = B.v2
    with phase(nc, "in silu") as (block, s):

        @block.sync
        def _(sp):
            sp.dma_start(B.vec2, I["vec2"]).then_inc(s["in"], 16)
            sp.dma_start(B.ctx, I["ctx"]).then_inc(s["in"], 16)
            sp.wait_ge(s["in"], 32)

        @block.scalar
        def _(act):
            act.wait_ge(s["in"], 32)
            for j, name in enumerate(("c", "c_ctx")):
                nc.scalar.activation(B.cond[:, :, j], v2(name), ACT.Silu).then_inc(s["silu"], 1)
            act.wait_ge(s["silu"], 2)


def ada_phase(nc, B, I):
    ring, n = 4, 48
    with phase(nc, " ".join(f"w{r}" for r in range(ring)) + " mm mod_out chain") as (block, s):

        @block.sync
        def _(sp):
            def load(c, r, end, i):
                wait(sp, s["mm"], c - ring + 1)
                sp.dma_start(B.wada[:, r], I["w_ada"][c]).then_inc(s[f"w{r}"], 16)

            turns(sp, n, ring, load)

        @block.tensor
        def _(pe):
            def chunk(c, r, end, i):
                pe.wait_ge(s[f"w{r}"], i * 16 + 16)
                wait(pe, s["mod_out"], c - ring + 1)
                for k in range(KD):
                    mm = nc.tensor.matmul(B.ps[:, r, 0:2], B.wada[:, r, k * P:(k + 1) * P], B.cond[:, k, :],
                                          start=(k == 0), stop=(k == KD - 1))
                mm.then_inc(s["mm"], 1)

            turns(pe, n, ring, chunk)

        @block.vector
        def _(dve):
            def empty(c, r, end, i):
                dve.wait_ge(s["mm"], c + 1)
                nc.vector.tensor_copy(B.mod[:, c, :], B.ps[:, r, 0:2]).then_inc(s["mod_out"], 1)

            ch = Chain(dve, s["chain"])
            turns(dve, n, ring, empty)
            dve.wait_ge(s["mod_out"], n)
            v2 = B.v2
            ch.link(nc.vector.tensor_tensor(B.mod, B.mod, bcast(v2("b_ada"), 2, 2), ALU.add))
            one = nc.vector.tensor_scalar
            ch.did(one(B.gains[:, 0, :], B.mod[:, 8:16, 0], 1.0, None, ALU.add))
            ch.did(one(B.gains[:, 1, :], B.mod[:, 8:16, 1], 1.0, None, ALU.add))
            ch.did(one(B.gains[:, 2, :], B.mod[:, 32:40, 0], 1.0, None, ALU.add))
            dve.wait_ge(s["chain"], ch.n)
            for j, name in enumerate(("mix_pre", "mix_pre", "ffn_pre")):
                ch.did(nc.vector.tensor_tensor(B.gains[:, j, :], B.gains[:, j, :], v2(name), ALU.mult))
            ch.did(nc.vector.tensor_tensor(B.gains[:, 3, :], B.mod[:, 16:24, 0], v2("mix_post"), ALU.mult))
            ch.did(nc.vector.tensor_tensor(B.gains[:, 4, :], B.mod[:, 40:48, 0], v2("ffn_post"), ALU.mult))
            dve.wait_ge(s["chain"], ch.n)


def norm_phase(nc, B, src, dst, gain, shift, add_to=None, halves=None):
    ps, con = B.ps, B.con
    with phase(nc, NORM + SPLIT + "chain") as (block, s):
        s.update(std=B.std[:, 0:T], var=B.var[:, 0:T], rstd=B.rstd[:, 0:T])
        ms = ps[:, 0, 0:T]

        @block.scalar
        def _(act):
            norm_act(act, nc, s, src, B.sq2)

        @block.tensor
        def _(pe):
            norm_pe(pe, nc, s, B.sq2, ms, con("mean_d"), KD)

        @block.vector
        def _(dve):
            norm_dve(dve, nc, s, src, dst, ms, gain, KD)
            dve.wait_ge(s["h_normed"], 1)
            ch = Chain(dve, s["chain"])
            if add_to is not None:
                ch.link(nc.vector.tensor_tensor(add_to, add_to, dst, ALU.add))
            else:
                for k in range(KD):
                    ch.did(nc.vector.tensor_scalar(dst[:, k, :], dst[:, k, :], shift[:, k:k + 1], None, ALU.add))
                dve.wait_ge(s["chain"], ch.n)
                if halves is not None:
                    split_dve(dve, nc, dst, *halves, s["h_hi_done"], s["h_lo_done"], 1)
                    dve.wait_ge(s["h_lo_done"], 1)


def kv_phase(nc, B, I):
    ps = B.ps
    ring = 2
    with phase(nc, project_sems("kv", ring) + "gw gw_hi gw_lo g_mm g_out") as (block, s):

        @block.sync
        def _(sp):
            sp.dma_start(B.w_mg, I["w_mg"]).then_inc(s["gw"], 16)
            project_sp(sp, s, "kv", lambda c: I["w_kv"][c], B.raw, ring, CX)

        @block.tensor
        def _(pe):
            pe.wait_ge(s["gw_lo"], 1)
            for t in range(NT2 // P):
                for k in range(KD):
                    tok = slice(t * P, (t + 1) * P)
                    mm = product(nc, ps[:, 7, 16 * t:16 * t + 16], B.h_hi[:, k, tok], B.h_lo[:, k, tok], B.w_mg_hi[:, k, :],
                                 B.w_mg_lo[:, k, :], k == 0, k == KD - 1)
            mm.then_inc(s["g_mm"], 1)
            project_pe(pe, nc, s, "kv", B, B.h_hi, B.h_lo, lambda r: ps[:, r, :], ring, CX, NT2)

        @block.scalar
        def _(act):
            project_act(act, nc, s, "kv", B, ring, CX, lambda c, r: nc.scalar.copy(B.kv[:, c, :], ps[:, r, :]))

        @block.vector
        def _(dve):
            dve.wait_ge(s["gw"], 16)
            split_dve(dve, nc, B.w_mg, B.w_mg_hi, B.w_mg_lo, s["gw_hi"], s["gw_lo"], 1)
            project_dve(dve, nc, s, "kv", B, ring, CX)
            dve.wait_ge(s["g_mm"], 1)
            nc.vector.tensor_copy(B.mg, ps[:, 7, 0:64].rearrange("p (t g) -> p t g", g=16)).then_inc(s["g_out"], 1)
            dve.wait_ge(s["g_out"], 1)


def plain_project_phase(nc, B, wsrc, dst, ring, n, func):
    ps = B.ps
    with phase(nc, project_sems("q", ring)) as (block, s):

        @block.sync
        def _(sp):
            project_sp(sp, s, "q", wsrc, B.raw, ring, n)

        @block.tensor
        def _(pe):
            project_pe(pe, nc, s, "q", B, B.h_hi[:, :, 0:T], B.h_lo[:, :, 0:T], lambda r: ps[:, r, :], ring, n, T)

        @block.scalar
        def _(act):
            project_act(act, nc, s, "q", B, ring, n, lambda c, r: nc.scalar.activation(dst[:, c, :], ps[:, r, 0:T], func))

        @block.vector
        def _(dve):
            project_dve(dve, nc, s, "q", B, ring, n)


NAK, NAV, MLK, MLV = 0, 4, 8, 10
NAQ, MLQ, MLO = 0, 4, 6


def prepare2_phase(nc, B, I):
    ps, con, kv, q = B.ps, B.con, B.kv, B.q10
    with phase(nc, "v_turned v_copied q_scaled turned_mm rope chain tanh_in tanh exp_in exp ln_in ln table_in masked") as (block, s):

        @block.sync
        def _(sp):
            rows_kept = 2 * ROWS - 1
            copy = NA_HEADS * rows_kept * P
            for h in range(NA_HEADS):
                for qc in range(TC):
                    for r2 in range(P // GRID_W):
                        r = qc * (P // GRID_W) + r2
                        first = (h * rows_kept + ROWS - 1 - r) * P + GRID_W - 1
                        skew = bass.AP(tensor=I["rpb"].tensor, offset=first, ap=[[copy - 1, GRID_W], [P, ROWS], [1, GRID_W]])
                        dst = B.na_table[r2 * GRID_W:(r2 + 1) * GRID_W, h * TC + qc, :].rearrange("p (r c) -> p r c", c=GRID_W)
                        sp.dma_start(dst, skew).then_inc(s["table_in"], 16)

        @block.tensor
        def _(pe):
            for j, c0 in enumerate((NAV, MLV)):
                for t in range(NT2 // P):
                    for c in range(4):
                        mm = nc.tensor.transpose(ps[:, 4 * j + t, c * P:(c + 1) * P], kv[:, c0 + c, t * P:(t + 1) * P], con("ident"))
            mm.then_inc(s["v_turned"], 1)
            pe.wait_ge(s["v_copied"], 8)
            pe.wait_ge(s["q_scaled"], 1)
            for j in range(4):
                x = q[:, MLQ + j, :] if j < 2 else kv[:, MLK + j - 2, 0:T]
                mm = nc.tensor.matmul(ps[:, j // 2, (j % 2) * T:(j % 2 + 1) * T], con("turn"), x, start=(j % 2 == 0),
                                      stop=True, skip_group_check=True)
            mm.then_inc(s["turned_mm"], 1)

        @block.scalar
        def _(act):
            act.wait_ge(s["tanh_in"], 1)
            nc.scalar.activation(B.mg, B.mg, ACT.Tanh, scale=1.0 / CAP).then_inc(s["tanh"], 1)
            act.wait_ge(s["exp_in"], 1)
            nc.scalar.activation(B.mge, B.mgn, ACT.Exp).then_inc(s["exp"], 1)
            act.wait_ge(s["ln_in"], 1)
            nc.scalar.activation(B.mgn, B.mge, ACT.Ln).then_inc(s["ln"], 1)

        @block.vector
        def _(dve):
            ch = Chain(dve, s["chain"])
            nc.vector.tensor_scalar(q[:, 0:6, :], q[:, 0:6, :], HD ** -0.5, None, ALU.mult).then_inc(s["q_scaled"], 1)
            nc.vector.tensor_tensor(B.mg, B.mg, bcast(B.v2("gates"), 1, 4), ALU.add).then_inc(s["tanh_in"], 1)
            dve.wait_ge(s["v_turned"], 1)
            for j, dst in enumerate((B.v_na, B.v_ml)):
                for t in range(NT2 // P):
                    nc.vector.tensor_copy(dst[:, t, :], ps[:, 4 * j + t, :]).then_inc(s["v_copied"], 1)
            dve.wait_ge(s["tanh"], 1)
            ch.link(nc.vector.tensor_scalar(B.mg, B.mg, CAP, None, ALU.mult))
            ch.link(nc.vector.tensor_scalar(B.mge, B.mg, -1.0, None, ALU.mult))
            nc.vector.tensor_tensor(B.mgn, B.mg, B.mge, ALU.min).then_inc(s["exp_in"], 1)
            dve.wait_ge(s["exp"], 1)
            nc.vector.tensor_scalar(B.mge, B.mge, 1.0, None, ALU.add).then_inc(s["ln_in"], 1)
            dve.wait_ge(s["ln"], 1)
            ch.link(nc.vector.tensor_scalar(B.mlf, B.mg, 0.0, None, ALU.min))
            ch.link(nc.vector.tensor_tensor(B.mlf, B.mlf, B.mgn, ALU.subtract))
            for h in range(ML_HEADS):
                up, fr = con("upto"), con("from")
                for dst, mask, t, col in ((B.lf_f0[:, h, :], up[:, 0, :], 0, 4 + h), (B.lf_f1[:, h, :], up[:, 1, P:T], 1, 4 + h),
                                          (B.lf_b0[:, h, :], fr[:, 0, 0:P], 0, 12 + h), (B.lf_b1[:, h, :], fr[:, 1, :], 1, 12 + h)):
                    ch.did(nc.vector.tensor_scalar(dst, mask, B.mlf[:, t, col:col + 1], None, ALU.mult))
            dve.wait_ge(s["turned_mm"], 1)
            for j in range(2):
                x = q[:, MLQ:MLQ + 2, :] if j == 0 else kv[:, MLK:MLK + 2, 0:T]
                ch.link(nc.vector.tensor_tensor(B.ropet[:, 0:2, :], ps[:, j, :].rearrange("p (c t) -> p c t", t=T),
                                                bcast(con("sin"), 1, 2), ALU.mult))
                ch.link(nc.vector.tensor_tensor(x, x, bcast(con("cos"), 1, 2), ALU.mult))
                ch.link(nc.vector.tensor_tensor(x, x, B.ropet[:, 0:2, :], ALU.add))
            dve.wait_ge(s["table_in"], 16 * NA_HEADS * TC * (P // GRID_W))
            mask = bcast(con("na_mask"), 1, NA_HEADS * TC)
            nc.vector.tensor_tensor(B.na_table, B.na_table, mask, ALU.add).then_inc(s["masked"], 1)
            dve.wait_ge(s["masked"], 1)


def neighbourhood(nc, B):
    units = []
    for h in range(NA_HEADS):
        lo = (h % 2) * HD
        for qc in range(TC):
            def scores(dst, h=h, lo=lo, qc=qc):
                return nc.tensor.matmul(dst, B.q10[lo:lo + HD, NAQ + h // 2, qc * P:(qc + 1) * P],
                                        B.kv[lo:lo + HD, NAK + h // 2, :], start=True, stop=True)

            units.append(dict(scores=scores, table=B.na_table[:, h * TC + qc, :], sink=None, row=lo,
                              values=[B.v_na[:, t, h * HD:(h + 1) * HD] for t in range(NT2 // P)],
                              out=B.b_na[lo:lo + HD, h // 2, qc * P:(qc + 1) * P]))
    attention_phase(nc, B, units, NT2)


def mlstm_phase(nc, B, prefetch):
    ps, con, q, kv = B.ps, B.con, B.q10, B.kv
    units = [(h, qc, d) for h in range(ML_HEADS) for qc in range(TC) for d in range(2)]
    n = len(units)
    with phase(nc, "scores_ready max_ready exp_ready probs_ready turned probs_t_ready out_ready out_copied chain added prefetched") as (block, s):

        @block.sync
        def _(sp):
            sp.dma_start(*prefetch).then_inc(s["prefetched"], 16)
            sp.wait_ge(s["prefetched"], 16)

        spread = {0: (B.lf_f0, B.lf_f1), 1: (B.lf_b0, B.lf_b1)}

        @block.tensor
        def _(pe):
            def scores(u):
                h, qc, d = units[u]
                lo = (h % 2) * HD
                if u >= 2:
                    pe.wait_ge(s["probs_ready"], u - 1)
                nc.tensor.matmul(ps[:, u % 2, :], q[lo:lo + HD, MLQ + h // 2, qc * P:(qc + 1) * P],
                                 kv[lo:lo + HD, MLK + h // 2, :], start=True, stop=True)
                dd = ps[:, 2 + u % 2, :]
                side = con("after") if d == 0 else con("before")
                lf = 4 + h if d == 0 else 12 + h
                li = h if d == 0 else 8 + h
                chunks = [c for c in range(TC) if (c <= qc if d == 0 else c >= qc)]
                for j, c in enumerate(chunks):
                    a = spread[d][c]
                    whole = (c == 0) == (d == 0)
                    lhs = a[:, h, qc * P:(qc + 1) * P] if whole else a[:, h, :]
                    nc.tensor.matmul(dd, lhs, side[:, c, :], start=(j == 0), stop=False, skip_group_check=True)
                for c in range(TC):
                    nc.tensor.matmul(dd[:, T:NT2], B.mlf[:, TC + c, lf:lf + 1].broadcast_to([P, P]), side[:, c, 0:T],
                                     start=False, stop=False, skip_group_check=True)
                for c in range(2 * TC):
                    mm = nc.tensor.matmul(dd[:, c * P:(c + 1) * P], B.mg[:, c, li:li + 1].broadcast_to([P, P]), con("ident"),
                                          start=False, stop=(c == 2 * TC - 1), skip_group_check=True)
                mm.then_inc(s["scores_ready"], 1)

            def turn(u):
                pe.wait_ge(s["probs_ready"], u + 1)
                if u >= 2:
                    pe.wait_ge(s["probs_t_ready"], u - 1)
                for j in range(4):
                    mm = nc.tensor.transpose(ps[:, 4 + u % 2, j * P:(j + 1) * P], B.prob[:, u % 2, j * P:(j + 1) * P], con("ident"))
                mm.then_inc(s["turned"], 1)

            def values(u):
                h, qc, d = units[u]
                pe.wait_ge(s["probs_t_ready"], u + 1)
                if d == 0 and u >= 4:
                    pe.wait_ge(s["out_copied"], u // 2 - 1)
                for j in range(4):
                    mm = nc.tensor.matmul(ps[:, 6 + (u // 2) % 2, 0:P], B.v_ml[:, j, h * P:(h + 1) * P],
                                          B.prob_t[:, u % 2, j * P:(j + 1) * P], start=(d == 0 and j == 0),
                                          stop=(d == 1 and j == 3))
                mm.then_inc(s["out_ready"], 1)

            scores(0)
            for u in range(n + 1):
                if u + 1 < n:
                    scores(u + 1)
                if u < n:
                    turn(u)
                if u >= 1:
                    values(u - 1)

        @block.scalar
        def _(act):
            for u in range(n + 1):
                if u >= 1:
                    act.wait_ge(s["turned"], u)
                    if u >= 3:
                        act.wait_ge(s["out_ready"], u - 2)
                    nc.scalar.copy(B.prob_t[:, (u - 1) % 2, :], ps[:, 4 + (u - 1) % 2, :]).then_inc(s["probs_t_ready"], 1)
                if u < n:
                    act.wait_ge(s["max_ready"], u + 1)
                    nc.scalar.activation(B.stat[:, u % 2, 2:3], B.stat[:, u % 2, 0:1], ACT.Exp)
                    nc.scalar.activation(B.prob[:, u % 2, :], B.prob[:, u % 2, :], ACT.Exp,
                                         bias=B.stat[:, u % 2, 0:1]).then_inc(s["exp_ready"], 1)

        @block.vector
        def _(dve):
            ch = Chain(dve, s["chain"])
            for u in range(n + 2):
                if u < n:
                    h, qc, d = units[u]
                    dve.wait_ge(s["scores_ready"], u + 1)
                    if u >= 2:
                        dve.wait_ge(s["turned"], u - 1)
                    dd = ps[:, 2 + u % 2, :]
                    mask = con("causal" if d == 0 else "anticausal")[:, qc, :]
                    ch.did(nc.vector.tensor_tensor(B.prob[:, u % 2, 0:T], dd[:, 0:T], mask, ALU.add))
                    ch.link(nc.vector.tensor_copy(B.prob[:, u % 2, T:NT2], dd[:, T:NT2]))
                    nc.vector.tensor_reduce(B.stat[:, u % 2, 0:1], B.prob[:, u % 2, :], AX, ALU.max,
                                            negate=True).then_inc(s["max_ready"], 1)
                    dve.wait_ge(s["exp_ready"], u + 1)
                    den, minus = B.stat[:, u % 2, 1:2], B.stat[:, u % 2, 3:4]
                    p = B.prob[:, u % 2, :]
                    ch.link(nc.vector.tensor_tensor(p, p, ps[:, u % 2, :], ALU.mult))
                    ch.link(nc.vector.tensor_reduce(den, p, AX, ALU.add))
                    ch.link(nc.vector.tensor_scalar(minus, den, -1.0, None, ALU.mult))
                    ch.link(nc.vector.tensor_tensor(den, den, minus, ALU.max))
                    ch.link(nc.vector.tensor_tensor(den, den, B.stat[:, u % 2, 2:3], ALU.max))
                    ch.link(nc.vector.reciprocal(minus, den))
                    nc.vector.tensor_scalar(p, p, minus, None, ALU.mult).then_inc(s["probs_ready"], 1)
                if u >= 2 and units[u - 2][2] == 1:
                    h, qc, _ = units[u - 2]
                    dve.wait_ge(s["out_ready"], u - 1)
                    nc.vector.tensor_copy(B.b_ml[:, h, qc * P:(qc + 1) * P],
                                          ps[:, 6 + ((u - 2) // 2) % 2, 0:P]).then_inc(s["out_copied"], 1)
            dve.wait_ge(s["out_copied"], n // 2)


def head_norm_phase(nc, B):
    ps, con = B.ps, B.con
    sq = B.sq2[:, 0:ML_HEADS, :]
    with phase(nc, "sq ms var std sig chain") as (block, s):

        @block.scalar
        def _(act):
            nc.scalar.activation(sq, B.b_ml, ACT.Square).then_inc(s["sq"], 1)
            nc.scalar.activation(B.q10[:, MLO:MLO + 4, :], B.q10[:, MLO:MLO + 4, :], ACT.Sigmoid).then_inc(s["sig"], 1)
            act.wait_ge(s["var"], 1)
            nc.scalar.activation(sq, sq, ACT.Sqrt).then_inc(s["std"], 1)

        @block.tensor
        def _(pe):
            pe.wait_ge(s["sq"], 1)
            for j in range(2):
                mm = nc.tensor.matmul(ps[:, j, :], con("mean_head"), sq[:, 2 * j:2 * j + 2, :], start=True, stop=True)
            mm.then_inc(s["ms"], 1)

        @block.vector
        def _(dve):
            ch = Chain(dve, s["chain"])
            dve.wait_ge(s["ms"], 1)
            nc.vector.tensor_scalar(sq, ps[:, 0:2, :].rearrange("p b (c t) -> p (b c) t", t=T), EPS, None,
                                    ALU.add).then_inc(s["var"], 1)
            dve.wait_ge(s["std"], 1)
            ch.link(nc.vector.reciprocal(sq, sq))
            dve.wait_ge(s["sig"], 1)
            ch.did(nc.vector.tensor_tensor(sq, sq, B.q10[:, MLO:MLO + 4, :], ALU.mult))
            dve.wait_ge(s["chain"], ch.n)
            for h in range(ML_HEADS):
                ch.did(nc.vector.scalar_tensor_tensor(B.b_ml[:, h, :], B.b_ml[:, h, :], B.v2("head")[:, h:h + 1], sq[:, h, :],
                                                      ALU.mult, ALU.mult))
            dve.wait_ge(s["chain"], ch.n)


NB = 2 * E


def router_phase(nc, B, I):
    ps, con = B.ps, B.con
    with phase(nc, "in logits h_turned h_copied max_ready exp_ready sel_ready counted chain listed") as (block, s):

        @block.sync
        def _(sp):
            sp.dma_start(B.w_r, I["w_router"]).then_inc(s["in"], 16)

        @block.tensor
        def _(pe):
            pe.wait_ge(s["in"], 16)
            for t in range(TC):
                for k in range(KD):
                    mm = nc.tensor.matmul(ps[:, 0, t * E:(t + 1) * E], B.h2[:, k, t * P:(t + 1) * P], B.w_r[:, k, :],
                                          start=(k == 0), stop=(k == KD - 1))
            mm.then_inc(s["logits"], 1)
            for t in range(TC):
                for k in range(KD):
                    mm = nc.tensor.transpose(ps[:, 2 + 2 * t + k // 4, (k % 4) * P:(k % 4 + 1) * P],
                                             B.h2[:, k, t * P:(t + 1) * P], con("ident"))
            mm.then_inc(s["h_turned"], 1)
            pe.wait_ge(s["sel_ready"], 1)
            for t in range(TC):
                for c in range(t + 1):
                    nc.tensor.matmul(ps[:, 1, t * E:(t + 1) * E], con("before")[:, c, t * P:(t + 1) * P], B.sel[:, c, :],
                                     start=(c == 0), stop=(c == t))
            for c in range(TC):
                mm = nc.tensor.matmul(ps[:, 1, TC * E:(TC + 1) * E], con("ones"), B.sel[:, c, :], start=(c == 0), stop=(c == TC - 1))
            mm.then_inc(s["counted"], 1)

        @block.scalar
        def _(act):
            act.wait_ge(s["max_ready"], 1)
            for t in range(TC):
                nc.scalar.activation(B.wtok[:, t, :], B.lg[:, t, :], ACT.Exp, bias=B.rmax[:, t:t + 1]).then_inc(s["exp_ready"], 1)
            act.wait_ge(s["h_turned"], 1)
            for t in range(TC):
                nc.scalar.copy(B.htok[:, t, :], ps[:, 2 + 2 * t:4 + 2 * t, :].rearrange("p b c -> p (b c)")).then_inc(s["h_copied"], 1)
            act.wait_ge(s["h_copied"], TC)

        @block.vector
        def _(dve):
            ch = Chain(dve, s["chain"])
            tt, ts, red = nc.vector.tensor_tensor, nc.vector.tensor_scalar, nc.vector.tensor_reduce
            dve.wait_ge(s["logits"], 1)
            ch.link(tt(B.lg, ps[:, 0, 0:TC * E].rearrange("p (t e) -> p t e", e=E), bcast(B.v2("b_router"), 1, TC), ALU.add))
            red(B.rmax, B.lg, AX, ALU.max, negate=True).then_inc(s["max_ready"], 1)
            for t in range(TC):
                other, this = bcast(B.lg[:, t, :], 1, E), bcast(B.lg[:, t, :], 2, E)
                ch.link(tt(B.cmp, other, this, ALU.is_equal))
                ch.link(tt(B.cmp, B.cmp, con("earlier"), ALU.mult))
                ch.link(tt(B.cmp2, other, this, ALU.is_gt))
                ch.link(tt(B.cmp, B.cmp, B.cmp2, ALU.add))
                ch.link(red(B.sel[:, t, :], B.cmp, AX, ALU.add))
            ts(B.sel, B.sel, TOPK - 0.5, None, ALU.is_lt).then_inc(s["sel_ready"], 1)
            dve.wait_ge(s["sel_ready"], 1)
            dve.wait_ge(s["exp_ready"], TC)
            ch.link(tt(B.wtok, B.wtok, B.sel, ALU.mult))
            ch.link(red(B.rsum, B.wtok, AX, ALU.add))
            ch.link(nc.vector.reciprocal(B.rsum, B.rsum))
            for t in range(TC):
                ch.did(ts(B.wtok[:, t, :], B.wtok[:, t, :], B.rsum[:, t:t + 1], None, ALU.mult))
            dve.wait_ge(s["counted"], 1)
            pos = ps[:, 1, 0:TC * E].rearrange("p (t e) -> p t e", e=E)
            for o in range(PER):
                part = B.slot[:, :, o:PER * E:PER]
                ch.link(ts(part, pos, 1.0 - o * SLOTS, None, ALU.add))
                ch.link(tt(part, part, B.sel, ALU.mult))
                ch.link(ts(part, part, -1.0, None, ALU.add))
            cnt = ps[:, 1, TC * E:(TC + 1) * E]
            ch.link(ts(B.nb[:, 0, :], cnt, 0.5, None, ALU.is_gt))
            for o in range(1, PER):
                ch.link(ts(B.nb[:, 1, :], cnt, o * SLOTS + 0.5, None, ALU.is_gt))
                ch.link(tt(B.nb[:, 0, :], B.nb[:, 0, :], B.nb[:, 1, :], ALU.add))
            ch.link(tt(B.cmp, bcast(B.nb[:, 0, :], 1, E), con("earlier"), ALU.mult))
            ch.link(red(B.nb[:, 1, :], B.cmp, AX, ALU.add))
            ch.link(tt(B.nb[:, 1, :], B.nb[:, 1, :], B.nb[:, 0, :], ALU.add))
            blocks = B.list[:, 0, PER:PER + NB]
            ch.link(nc.vector.memset(B.list, -1.0))
            ch.link(tt(B.listc, bcast(B.nb[:, 1, :], 1, NB), bcast(con("block_no"), 2, E), ALU.is_le))
            ch.link(red(blocks, B.listc, AX, ALU.add))
            ch.link(ts(blocks, blocks, E - 1.0, None, ALU.min))
            col = B.list[:, 1, PER:PER + NB]
            ch.link(ts(col, blocks, float(PER), None, ALU.mult))
            for o in range(1, PER):
                ch.link(tt(B.same, blocks, B.list[:, 0, PER - o:PER - o + NB], ALU.is_equal))
                ch.link(tt(col, col, B.same, ALU.add))
            ch.link(nc.vector.tensor_copy(B.list[:, 1, 0:1], B.nb[:, 1, E - 1:E]))
            ch.link(nc.vector.tensor_copy(B.listi, B.list))


def moe_phase(nc, B, I):
    ps, con = B.ps, B.con
    names = ("wg0 wg1 wl0 wl1 wd0 wd1 gate_half lin_half down_half g_ready sig_ready a_ready scattered0 scattered1 added0 added1 st_turned "
             "st_copied s_ready gathered hg_ready a_turned at_ready y_ready bias_in bias_spread t_read l_read g_read m_ready zeroed tick_ready")
    wsrc = {"g": I["w_gate2"], "l": I["w_lin2"], "d": I["w_down2"]}
    with phase(nc, names) as (block, s):
        G, L, Y, X, H, A, S_t = ps[:, 0, :], ps[:, 1, :], ps[:, 2, :], ps[:, 3:5, :], ps[:, 5, :], ps[:, 6, :], ps[:, 7, :]
        HALF = D // 2
        side = lambda half: slice(half * SLOTS, (half + 1) * SLOTS)

        def blocks(eng):
            return eng.value_load(B.listi[0:1, 1, 0:1], min_val=T * TOPK // SLOTS, max_val=NB - 1)

        def entry(eng, row, j, top):
            return eng.value_load(B.listi[0:1, row, bass.ds(j, 1)], min_val=0, max_val=top)

        @block.sync
        def _(sp):
            def weights(e, kind, half):
                src = wsrc[kind][e].rearrange("(k p) n -> p k n", p=P)[:, 4 * half:4 * half + 4, :]
                sp.dma_start(B.wexp[2 * "gld".index(kind) + half], src).then_inc(s[f"w{kind}{half}"], 16)

            total = blocks(sp)
            e = entry(sp, 0, PER, E - 1)
            sp.dma_start(B.brow, I["bias2"][bass.ds(e, 1), :]).then_inc(s["bias_in"], 16)
            for kind in "gld":
                for half in range(2):
                    weights(e, kind, half)
            with sp.Fori(1, total) as j:
                e = entry(sp, 0, j + PER, E - 1)
                sp.wait_ge(s["bias_spread"], j)
                sp.dma_start(B.brow, I["bias2"][bass.ds(e, 1), :]).then_inc(s["bias_in"], 16)
                for kind, used in (("g", "gate_half"), ("l", "lin_half"), ("d", "down_half")):
                    for half in range(2):
                        sp.wait_ge(s[used], 2 * j + (half - 1))
                        weights(e, kind, half)

        @block.gpsimd
        def _(pool):
            total = blocks(pool)
            nc.gpsimd.memset(B.tick, 0.0).then_inc(s["tick_ready"], 1)
            pool.wait_ge(s["tick_ready"], 1)
            pool.wait_ge(s["bias_in"], 16)
            nc.gpsimd.partition_broadcast(B.bias, B.brow).then_inc(s["bias_spread"], 1)
            with pool.Fori(1, total) as j:
                pool.wait_ge(s["bias_in"], 16 * j + 16)
                pool.wait_ge(s["y_ready"], j)
                nc.gpsimd.tensor_tensor(B.tick[:, 1:2], B.tick[:, 0:1], B.tick[:, 0:1], ALU.add)
                nc.gpsimd.partition_broadcast(B.bias, B.brow).then_inc(s["bias_spread"], 1)

        @block.tensor
        def _(pe):
            total = blocks(pe)

            def gather():
                for k in range(KD):
                    for t in range(TC):
                        mm = nc.tensor.matmul(H[:, k * SLOTS:(k + 1) * SLOTS], B.htok[:, t, k * P:(k + 1) * P],
                                              B.S[:, t, 0:SLOTS], start=(t == 0), stop=(t == TC - 1))
                mm.then_inc(s["gathered"], 1)

            def wide(j, kind, lhs, dst, done):
                for part in range(2):
                    pe.wait_ge(s[f"w{kind}{part}"], 16 * j + 16)
                    for k in range(4 * part, 4 * part + 4):
                        for half in range(2):
                            mm = nc.tensor.matmul(dst[side(half), :], lhs(k),
                                                  B.wexp[2 * "gld".index(kind) + part][:, k % 4, half * HALF:(half + 1) * HALF],
                                                  start=(k == 0), stop=(k == KD - 1), skip_group_check=True)
                    mm.then_inc(s[done], 1)

            def scatter(t):
                for half in range(2):
                    mm = nc.tensor.matmul(X[:, half, :], B.ST[side(half), t, :], B.y[side(half), :], start=True, stop=True)
                mm.then_inc(s[f"scattered{t}"], 1)

            def block_turn(j, first):
                pe.wait_ge(s["hg_ready"], j + 1)
                if not first:
                    pe.wait_ge(s["g_read"], j)
                wide(j, "g", lambda k: B.hg[:, k, :], G, "gate_half")
                if not first:
                    pe.wait_ge(s["st_copied"], j)
                for t in range(TC):
                    mm = nc.tensor.transpose(S_t[:, t * P:(t + 1) * P], B.S[:, t, :], con("ident"))
                mm.then_inc(s["st_turned"], 1)
                if not first:
                    pe.wait_ge(s["y_ready"], j)
                    scatter(0)
                    pe.wait_ge(s["l_read"], j)
                wide(j, "l", lambda k: B.hg[:, k, :], L, "lin_half")
                if not first:
                    pe.wait_ge(s["added0"], j)
                    scatter(1)
                pe.wait_ge(s["s_ready"], j + 2)
                gather()
                pe.wait_ge(s["a_ready"], j + 1)
                for k in range(4):
                    mm = nc.tensor.transpose(A[:, k * P:(k + 1) * P], B.a[:, k * P:(k + 1) * P], con("ident"))
                mm.then_inc(s["a_turned"], 1)
                pe.wait_ge(s["at_ready"], j + 1)
                wide(j, "d", lambda k: B.aT[:, k % 4, side(k // 4)], Y, "down_half")

            pe.wait_ge(s["s_ready"], 1)
            gather()
            block_turn(0, True)
            with pe.Fori(1, total) as j:
                block_turn(j, False)
            pe.wait_ge(s["y_ready"], total)
            scatter(0)
            pe.wait_ge(s["added0"], total)
            scatter(1)

        @block.scalar
        def _(act):
            total = blocks(act)

            def gathered_copy(n):
                act.wait_ge(s["gathered"], n + 1)
                nc.scalar.copy(B.hg, H.rearrange("p (k t) -> p k t", t=SLOTS)).then_inc(s["hg_ready"], 1)

            def block_turn(j, first):
                act.wait_ge(s["g_ready"], j + 1)
                nc.scalar.activation(B.sg, B.g, ACT.Sigmoid, scale=ALPHA).then_inc(s["sig_ready"], 1)
                act.wait_ge(s["st_turned"], j + 1)
                if not first:
                    act.wait_ge(s["scattered1"], j)
                nc.scalar.copy(B.ST, S_t[:, 0:T].rearrange("p (a b) -> p a b", b=P)).then_inc(s["st_copied"], 1)
                gathered_copy(j + 1)
                act.wait_ge(s["a_turned"], j + 1)
                nc.scalar.copy(B.aT, A.rearrange("p (k t) -> p k t", t=P)).then_inc(s["at_ready"], 1)

            gathered_copy(0)
            block_turn(0, True)
            with act.Fori(1, total) as j:
                block_turn(j, False)

        @block.vector
        def _(dve):
            total = blocks(dve)
            tt, ts, stt = nc.vector.tensor_tensor, nc.vector.tensor_scalar, nc.vector.scalar_tensor_tensor

            def one_hot(j):
                col = entry(dve, 1, j + PER, PER * E - 1)
                for t in range(TC):
                    last = ts(B.S[:, t, :], con("slots"), B.slot[:, t, bass.ds(col, 1)], None, ALU.is_equal)
                last.then_inc(s["s_ready"], 1)

            def biased(dst, bank, n):
                for half in range(2):
                    last = tt(dst[side(half), :], bank[side(half), :],
                              B.bias[side(half), n * D + half * HALF:n * D + (half + 1) * HALF], ALU.add)
                return last

            def add(t, n, e):
                dve.wait_ge(s[f"scattered{t}"], n)
                stt(B.acc[:, t, :], X.rearrange("p b c -> p (b c)"), B.wtok[:, t, bass.ds(e, 1)], B.acc[:, t, :], ALU.mult, ALU.add).then_inc(s[f"added{t}"], 1)

            def block_turn(j, first):
                e = None if first else entry(dve, 0, j + (PER - 1), E - 1)
                dve.wait_ge(s["bias_spread"], j + 1)
                dve.wait_ge(s["gate_half"], 2 * j + 2)
                biased(B.g, G, 0).then_inc(s["g_read"], 1)
                dve.wait_ge(s["g_read"], j + 1)
                ts(B.g, B.g, LIMIT, None, ALU.min).then_inc(s["g_ready"], 1)
                dve.wait_ge(s["st_turned"], j + 1)
                one_hot(j + 1)
                if not first:
                    add(0, j, e)
                dve.wait_ge(s["sig_ready"], j + 1)
                tt(B.g, B.g, B.sg, ALU.mult).then_inc(s["t_read"], 1)
                dve.wait_ge(s["lin_half"], 2 * j + 2)
                biased(B.l, L, 1).then_inc(s["l_read"], 1)
                dve.wait_ge(s["l_read"], j + 1)
                ts(B.l, B.l, LIMIT, -LIMIT, ALU.min, ALU.max).then_inc(s["m_ready"], 1)
                dve.wait_ge(s["m_ready"], j + 1)
                dve.wait_ge(s["t_read"], j + 1)
                stt(B.a, B.l, 1.0, B.g, ALU.add, ALU.mult).then_inc(s["a_ready"], 1)
                if not first:
                    add(1, j, e)
                dve.wait_ge(s["down_half"], 2 * j + 2)
                biased(B.y, Y, 2).then_inc(s["y_ready"], 1)

            nc.vector.memset(B.acc, 0.0).then_inc(s["zeroed"], 1)
            dve.wait_ge(s["zeroed"], 1)
            one_hot(0)
            block_turn(0, True)
            with dve.Fori(1, total) as j:
                block_turn(j, False)
            e = entry(dve, 0, total + (PER - 1), E - 1)
            add(0, total, e)
            add(1, total, e)


def turn_back_phase(nc, B):
    ps = B.ps
    with phase(nc, "turned copied") as (block, s):

        @block.tensor
        def _(pe):
            for k in range(KD):
                for t in range(TC):
                    mm = nc.tensor.transpose(ps[:, k // 2, (k % 2) * T + t * P:(k % 2) * T + (t + 1) * P],
                                             B.acc[:, t, k * P:(k + 1) * P], B.con("ident"))
            mm.then_inc(s["turned"], 1)

        @block.vector
        def _(dve):
            dve.wait_ge(s["turned"], 1)
            nc.vector.tensor_copy(B.h2, ps[:, 0:4, :].rearrange("p b (c t) -> p (b c) t", t=T)).then_inc(s["copied"], 1)
            dve.wait_ge(s["copied"], 1)


def second_block_program(nc, B, I, out):
    B.stage = "second"
    mod = lambda c: B.mod[:, c:c + KD, 0]
    with ExitStack() as outer:
        (B.vec2, B.cond, B.mod, B.gains, B.h2) = alloc(
            nc, outer, B, vec2=(P, NVEC2), cond=(P, KD, 2), mod=(P, 48, 2), gains=(P, 5, KD), h2=(P, KD, T))
        B.v2 = lambda name: B.vec2[:, VEC2[name][0]:VEC2[name][0] + VEC2[name][1]]
        B.sq2 = B.sq
        B.ctx = B.h2
        load2_phase(nc, B, I)
        with ExitStack() as ctx:
            (B.wada,) = alloc(nc, ctx, B, wada=(P, 4, D))
            ada_phase(nc, B, I)
        with ExitStack() as ctx:
            (B.kv, B.q10, B.mg, B.mge, B.mgn, B.mlf, B.gates) = alloc(
                nc, ctx, B, kv=(P, CX, NT2), q10=(P, LX, T), mg=(P, 4, 16), mge=(P, 4, 16), mgn=(P, 4, 16), mlf=(P, 4, 16),
                gates=(P, G2, T))
            halves = B.kv[:, NAV:NAV + 4, :].rearrange("p c (b t) -> p (c b) t", t=T)
            B.b_na, B.b_ml = halves[:, 0:4, :], halves[:, 4:8, :]
            with ExitStack() as proj:
                (B.w_mg,) = alloc(nc, proj, B, w_mg=(P, KD, 16))
                B.h_hi, B.h_lo, B.w_mg_hi, B.w_mg_lo = alloc(
                    nc, proj, B, F32R, h_hi=(P, KD, NT2), h_lo=(P, KD, NT2), w_mg_hi=(P, KD, 16), w_mg_lo=(P, KD, 16))
                split_ring(nc, proj, B, 4)
                for src, tok, j in ((B.x, slice(0, T), 0), (B.ctx, slice(T, NT2), 1)):
                    norm_phase(nc, B, src, B.sq, B.gains[:, j, :], B.mod[:, 0:8, j], halves=(B.h_hi[:, :, tok], B.h_lo[:, :, tok]))
                kv_phase(nc, B, I)
                plain_project_phase(nc, B, lambda c: I["w_q2"][c], B.q10, 2, LX, ACT.Copy)
                plain_project_phase(nc, B, lambda c: I["w_g2"][c], B.gates, 4, G2, ACT.Sigmoid)
            with ExitStack() as branches:
                (B.prob, B.prob_t, B.stat) = alloc(
                    nc, branches, B, prob=(P, DEPTH_A, 512), prob_t=(P, 2, 512), stat=(P, DEPTH_A, 4))
                B.ropet = B.prob_t.rearrange("p a (b t) -> p (a b) t", t=T)
                B.mtmp = B.ropet
                B.h_hi, B.h_lo = alloc(nc, branches, B, F32R, m_hi=(P, KD, T), m_lo=(P, KD, T))
                with ExitStack() as ml:
                    (B.lf_f0, B.lf_f1, B.lf_b0, B.lf_b1, B.v_ml) = alloc(
                        nc, ml, B, lf_f0=(P, 4, T), lf_f1=(P, 4, P), lf_b0=(P, 4, P), lf_b1=(P, 4, T), v_ml=(P, 4, 512))
                    with ExitStack() as near:
                        (B.na_table, B.v_na) = alloc(nc, near, B, na_table=(P, NA_HEADS * TC, T), v_na=(P, 4, 512))
                        prepare2_phase(nc, B, I)
                        neighbourhood(nc, B)
                    (B.wb,) = alloc(nc, ml, B, wb=(P, 8, D))
                    mlstm_phase(nc, B, (B.wb, I["w_branch2"]))
                    head_norm_phase(nc, B)
                    merge_phase(nc, B, [B.b_na, B.b_ml], 4, B.gates, 2)
                split_ring(nc, branches, B, 4)
                out_phase(nc, B, lambda c: I["w_out2"][c], B.h2, False)
            norm_phase(nc, B, B.h2, B.h2, B.gains[:, 3, :], None, add_to=B.x)
        norm_phase(nc, B, B.x, B.h2, B.gains[:, 2, :], mod(24))
        with ExitStack() as ctx:
            (B.w_r, B.lg, B.rmax, B.rsum, B.sel, B.wtok, B.slot, B.nb, B.same, B.list, B.htok, B.acc) = alloc(
                nc, ctx, B, w_r=(P, KD, E), lg=(P, TC, E), rmax=(P, TC), rsum=(P, TC), sel=(P, TC, E),
                wtok=(P, TC, E), slot=(P, TC, PER * E), nb=(P, 2, E), same=(P, NB),
                list=(P, 2, PER + NB), htok=(P, TC, D),
                acc=(P, TC, D))
            B.listi = ctx.enter_context(nc.sbuf_tensor("listi", [P, 2, PER + NB], I32))[:, :, :]
            with ExitStack() as small:
                (B.cmp, B.cmp2, B.listc) = alloc(
                    nc, small, B, cmp=(P, E, E), cmp2=(P, E, E), listc=(P, NB, E))
                router_phase(nc, B, I)
            (B.wexp_all, B.S, B.ST, B.y, B.aT, B.hg, B.tick) = alloc(
                nc, ctx, B, wexp_all=(P, 6, 4, D), S=(P, TC, P), ST=(P, TC, P), y=(P, D // 2), aT=(P, 4, P), hg=(P, KD, SLOTS),
                tick=(P, 2))
            spent = B.con_all[:, B.con_kept:]
            B.bias, B.brow = spent[:, 0:3 * D], spent[0:1, 3 * D:6 * D]
            B.wexp = [B.wexp_all[:, i] for i in range(6)]
            rows = B.sq.rearrange("p (h k) t -> p h (k t)", h=4)
            B.g, B.sg, B.l, B.a = [rows[:, i] for i in range(4)]
            moe_phase(nc, B, I)
            turn_back_phase(nc, B)
            norm_phase(nc, B, B.h2, B.h2, B.gains[:, 4, :], None, add_to=B.x)
        with phase(nc, "stored") as (block, s):
            @block.sync
            def _(sp):
                sp.dma_start(out, B.x).then_inc(s["stored"], 16)
                sp.wait_ge(s["stored"], 16)



def build(nc, I, out, stop=None):
    PHASES.clear()
    _, at = _constants()
    with ExitStack() as ctx:
        B = Bufs()
        width = I["const"].shape[1]
        (B.x, B.con_all, B.sq, B.var, B.std, B.rstd) = alloc(
            nc, ctx, B, x=(P, KD, T), con_all=(P, width), sq=(P, KD, T), var=(P, 512), std=(P, 512), rstd=(P, 512))
        B.ps = ctx.enter_context(nc.psum_tensor("ps", [P, 8, 512], F32))[:, :, :]
        B.d_line = nc.dram_tensor("line_scratch", (P, 4, 512), F32, kind="Internal").ap()

        def con(name):
            n, shape = at[name]
            size = int(np.prod(shape[1:]))
            a = B.con_all[:, n:n + size]
            if len(shape) == 3:
                a = a.rearrange("p (a b) -> p a b", b=shape[2])
            return a

        B.con = con
        B.con_kept = at["ones"][0]
        first_block_program(nc, B, I)
        if stop == "first":
            with phase(nc, "stored") as (block, s):
                @block.sync
                def _(sp):
                    sp.dma_start(out, B.x).then_inc(s["stored"], 16)
                    sp.wait_ge(s["stored"], 16)
            return
        second_block_program(nc, B, I, out)


def _chunk_rows(w):
    *lead, d, f = w.shape
    w = w.reshape(*lead, d // P, P, f // P, P)
    n = len(lead)
    return np.ascontiguousarray(w.transpose(*range(n), n + 2, n + 1, n, n + 3)).reshape(*lead, f // P, P, d)


def _cols(v):
    return v.reshape(-1, P).T


def _rep(v):
    return np.tile(v.reshape(1, -1), (P, 1))


def layout(a):
    I = {}
    I["const"] = _constants()[0]
    I["x"] = a["x"][0].T.reshape(KD, P, T).transpose(1, 0, 2)
    I["rel_bias"] = a["rel_bias"]
    for f in ("ffn1", "ffn2"):
        I[f + "_wg"] = _chunk_rows(a[f + "_w_gate"])
        I[f + "_wu"] = _chunk_rows(a[f + "_w_up"])
        I[f + "_wd"] = a[f + "_w_down"].reshape(DEPTH, FC, P, D)
    w = a["w_in"]
    zc = ZC * P
    I["w_z"] = _chunk_rows(w[:, :, :zc])
    I["w_ff"] = w[:, :, zc:zc + 4].reshape(DEPTH, KD, P, 4).transpose(0, 2, 1, 3)
    I["w_g"] = _chunk_rows(w[:, :, zc + 4:])
    I["w_branch"] = np.stack([a[n].reshape(DEPTH, 2, P, D) for n in ("conf_w_out", "sc_w_out", "swa_w_o", "fox_w_o")],
                             1).reshape(DEPTH, 8, P, D).transpose(0, 2, 1, 3)
    I["w_out"] = _chunk_rows(a["w_out"])
    rows = []
    for l in range(DEPTH):
        rows.append(np.concatenate([
            _cols(a["ffn1_norm"][l]), _cols(a["mix_norm"][l]), _cols(a["ffn2_norm"][l]),
            a["conf_dw"][l].T[:P], a["conf_dw"][l].T[P:], _cols(a["conf_dw_b"][l]), _cols(a["conf_ln_g"][l]),
            _cols(a["conf_ln_b"][l]), a["sc_conv"][l].T[:P], a["sc_conv"][l].T[P:],
            *[np.tile(a[n][l], 2)[:, None] for n in ("swa_q_norm", "swa_k_norm", "fox_q_norm", "fox_k_norm")],
            _rep(a["b_forget"][l]), _rep(a["swa_sink"][l])], 1))
    I["vec"] = np.stack(rows)
    kv_cols = 4 * P + 4 * P + 2 * P + 4 * P
    w = a["w_in_2"][0]
    I["w_kv"] = _chunk_rows(w[:, :kv_cols])
    I["w_mg"] = w[:, kv_cols:kv_cols + 16].reshape(KD, P, 16).transpose(1, 0, 2)
    I["w_q2"] = _chunk_rows(w[:, kv_cols + 16:kv_cols + 16 + LX * P])
    I["w_g2"] = _chunk_rows(w[:, kv_cols + 16 + LX * P:])
    I["w_ada"] = _chunk_rows(a["w_ada_2"][0])
    I["ctx"] = a["ctx_2"][0].T.reshape(KD, P, T).transpose(1, 0, 2)
    rpb = np.zeros((GRID_W, NA_HEADS, 2 * ROWS - 1, P), np.float32)
    rpb[:, :, :, GRID_W - WIN_W:GRID_W + WIN_W - 1] = a["rpb_2"][0][:, WIN_H - ROWS:WIN_H + ROWS - 1]
    I["rpb"] = rpb
    I["w_branch2"] = np.concatenate([a["w_branch_na_2"][0].reshape(4, P, D), a["w_branch_ml_2"][0].reshape(4, P, D)]).transpose(1, 0, 2)
    I["w_out2"] = _chunk_rows(a["w_out_2"][0])
    I["w_router"] = a["w_router_2"][0].reshape(KD, P, E).transpose(1, 0, 2)
    I["w_gate2"], I["w_lin2"], I["w_down2"] = a["w_gate_2"][0], a["w_lin_2"][0], a["w_down_2"][0]
    I["bias2"] = np.concatenate([a["b_gate_2"][0], a["b_lin_2"][0], a["b_down_2"][0]], 1)
    I["vec2"] = np.concatenate([
        _cols(a["c_2"][0]), _cols(a["c_ctx_2"]), _cols(a["b_ada_2"][0]), _cols(a["g_mix_pre_2"][0]), _cols(a["g_mix_post_2"][0]),
        _cols(a["g_ffn_pre_2"][0]), _cols(a["g_ffn_post_2"][0]), _rep(a["b_mlstm_gates_2"][0]), _cols(a["g_mlstm_head_2"][0]),
        _rep(a["b_router_2"][0])], 1)
    return {k: np.ascontiguousarray(v) for k, v in I.items()}


def kernel(**inputs):
    import concourse.bacc as _bacc
    from concourse.bass_utils import run_bass_kernel_spmd as _run

    arrays = layout({k: np.asarray(v) for k, v in inputs.items()})
    nc = _bacc.Bacc("TRN2", target_bir_lowering=False, num_devices=1)
    I = {k: nc.dram_tensor(f"in_{k}", v.shape, F32, kind="ExternalInput").ap() for k, v in arrays.items()}
    out = nc.dram_tensor("out", (P, KD, T), F32, kind="ExternalOutput").ap()
    build(nc, I, out, stop=STOP)
    r = _run(nc, [{f"in_{k}": v for k, v in arrays.items()}], core_ids=[0])
    o = r.results[0]["out"]
    return np.ascontiguousarray(o.transpose(2, 1, 0).reshape(1, T, D))


STOP = None
```

```python
from contextlib import ExitStack, contextmanager

import numpy as np
import concourse.bass as bass
from concourse import mybir

F32 = mybir.dt.float32
F32R = mybir.dt.float32r
I32 = mybir.dt.int32
ALU = mybir.AluOpType
ACT = mybir.ActivationFunctionType
AX = mybir.AxisListType.X

P = 128
D = 1024
KD = D // P
T = 256
TC = T // P
DEPTH = 2
FF = 2816
FC = FF // P
ZC = 20
GC = 32
HD = 64
CONV_K = 31
SC_K = 3
WINDOW = 128
N_BUCKETS = 32
EPS = 1e-6
NEG = -1e30

GRID_W = 64
ROWS = T // GRID_W
NA_HEADS = 8
WIN_H = 8
WIN_W = 16
ML_HEADS = 4
CAP = 15.0
CX = 14
LX = 10
G2 = 16
E = 32
TOPK = 4
SLOTS = 64
PER = T // SLOTS
ALPHA = 1.702
LIMIT = 7.0
NT2 = 2 * T


def _constants():
    parts, at = {}, {}

    def put(name, a):
        full = np.zeros((P, int(np.prod(a.shape[1:]))), np.float32)
        full[:a.shape[0]] = a.reshape(a.shape[0], -1)
        parts[name] = (full, a.shape)

    i = np.arange(P)
    u = np.arange(T).reshape(TC, P).T[:, :, None]
    s = np.arange(T)[None, None, :]
    put("ident", np.eye(P, dtype=np.float32))
    put("mean_d", np.full((P, P), 1.0 / D))
    put("slots", np.tile(np.arange(SLOTS, dtype=np.float32), (P, 2)))
    put("ones", np.ones((P, P)))
    put("mean_conv", np.full((P, P), 1.0 / 256))
    put("mean_head", np.full((P, P), 1.0 / P))
    put("zeros", np.zeros((P, 512)))
    heads = np.zeros((P, 7, 14))
    for c in range(7):
        heads[:HD, c, 2 * c] = heads[HD:, c, 2 * c + 1] = 1.0 / HD
    put("head_mean", heads)
    spread = np.zeros((14, 7, P))
    for c in range(7):
        spread[2 * c, c, :HD] = spread[2 * c + 1, c, HD:] = 1.0
    put("head_spread", spread)
    one = np.ones((P, TC, T))
    put("after", np.concatenate([(u > s), one], 2))
    put("before", np.concatenate([(u < s), one], 2))
    put("upto", (u <= s))
    put("from", (u >= s))
    put("causal", np.where(s <= u, 0.0, NEG))
    put("anticausal", np.where(s >= u, 0.0, NEG))
    dist = i[:, None] + P - np.arange(2 * P)[None, :]
    own = np.where((dist >= 0) & (dist < WINDOW), 0.0, NEG)
    first = np.full((P, T), NEG)
    first[:, :P] = own[:, P:]
    put("window", np.stack([first, own], 1))
    d = 255 - np.arange(2 * T - 1)
    dd = np.clip(d, 0, WINDOW - 1)
    half = N_BUCKETS // 2
    dm = np.maximum(dd, 1).astype(np.float32)
    large = half + (np.log(dm / np.float32(half)) / np.float32(np.log(P / half)) * np.float32(N_BUCKETS - half)).astype(np.int32)
    bucket = np.where(dd < half, dd, np.minimum(large, N_BUCKETS - 1))
    line = (bucket[None, :] == np.arange(N_BUCKETS)[:, None]).astype(np.float32)
    put("bucket", np.concatenate([line, np.zeros((N_BUCKETS, 1))], 1))
    cs = np.clip(np.arange(GRID_W) - WIN_W // 2, 0, GRID_W - WIN_W)[i % GRID_W][:, None]
    kc = np.arange(GRID_W)[None, :]
    put("na_mask", np.tile(np.where((kc >= cs) & (kc < cs + WIN_W), 0.0, NEG), (1, ROWS)))
    n_freq = HD // 4
    inv = np.float32(10000.0) ** (-np.arange(n_freq, dtype=np.float32) / n_freq)
    t = np.arange(T)
    ang = np.zeros((P, T), np.float32)
    turn = np.zeros((P, P))
    for p in range(P):
        pos = t // GRID_W if (p % HD) < HD // 2 else t % GRID_W
        ang[p] = pos.astype(np.float32) * inv[p % n_freq]
        if p % (2 * n_freq) < n_freq:
            turn[p + n_freq, p] = -1.0
        else:
            turn[p - n_freq, p] = 1.0
    put("cos", np.cos(ang))
    put("sin", np.sin(ang))
    put("turn", turn)
    j = np.arange(E)
    put("earlier", np.tile((j[None, :] < j[:, None]).astype(np.float32), (P, 1, 1)))
    put("block_no", np.tile(np.arange(2 * E, dtype=np.float32), (P, 1)))
    n = 0
    for name, (full, shape) in parts.items():
        at[name] = (n, shape)
        n += full.shape[1]
    return np.ascontiguousarray(np.concatenate([f for f, _ in parts.values()], 1).astype(np.float32)), at


VEC = {}
_n = 0
for _name, _w in (("ffn1", 8), ("mix", 8), ("ffn2", 8), ("dw", 2 * CONV_K), ("dw_b", 2), ("ln_g", 2), ("ln_b", 2),
                  ("sc", 2 * SC_K), ("swa_q", 1), ("swa_k", 1), ("fox_q", 1), ("fox_k", 1), ("b_forget", 4), ("sink", 4)):
    VEC[_name] = (_n, _w)
    _n += _w
NVEC = _n
VEC2 = {}
_n = 0
for _name, _w in (("b_ada", 48), ("mix_pre", 8), ("mix_post", 8), ("ffn_pre", 8), ("ffn_post", 8),
                  ("gates", 16), ("head", 4), ("b_router", 32)):
    VEC2[_name] = (_n, _w)
    _n += _w
NVEC2 = _n


PHASES = []


@contextmanager
def phase(nc, names):
    PHASES.append(len(PHASES))
    sems = {n: nc.alloc_semaphore(f"{n}_phase{len(PHASES)}") for n in names.split()}
    with nc.Block() as block:
        yield block, dict(sems)
    nc.clear_and_free_semaphores(list(sems.values()))
    nc.all_engine_barrier()


class Chain:

    def __init__(self, eng, sem):
        self.eng, self.sem, self.n = eng, sem, 0

    def did(self, ins):
        ins.then_inc(self.sem, 1)
        self.n += 1
        return self.n

    def link(self, ins):
        self.did(ins)
        self.eng.wait_ge(self.sem, self.n)


NORM = "sq_ready ms_ready var_ready std_ready h_scaled h_normed norm_chain h_hi_done h_lo_done "


def norm_squares(act, nc, s, x, sq):
    for k in range(0, KD, 2):
        nc.scalar.activation(sq[:, k:k + 2, :], x[:, k:k + 2, :], ACT.Square).then_inc(s["sq_ready"], 1)


def norm_act(act, nc, s, x, sq, h=None, h_hi=None, between=None, squared=False):
    if not squared:
        norm_squares(act, nc, s, x, sq)
    if between is not None:
        between()
    act.wait_ge(s["var_ready"], 1)
    nc.scalar.activation(s["std"], s["var"], ACT.Sqrt).then_inc(s["std_ready"], 1)
    if h_hi is not None:
        for k in range(KD):
            act.wait_ge(s["h_normed"], k + 1)
            nc.scalar.copy(h_hi[:, k, :], h[:, k, :]).then_inc(s["h_hi_done"], 1)


def norm_pe(pe, nc, s, sq, ms, mean):
    for k in range(KD):
        if k % 2 == 0:
            pe.wait_ge(s["sq_ready"], k // 2 + 1)
        mm = nc.tensor.matmul(ms, mean, sq[:, k, :], start=(k == 0), stop=(k == KD - 1))
    mm.then_inc(s["ms_ready"], 1)


def norm_dve(dve, nc, s, x, h, ms, gain, shift=None, halves=None, between=None):
    if between is not None:
        between()
    dve.wait_ge(s["ms_ready"], 1)
    nc.vector.tensor_scalar(s["var"], ms, EPS, None, ALU.add).then_inc(s["var_ready"], 1)
    dve.wait_ge(s["std_ready"], 1)
    nc.vector.reciprocal(s["rstd"], s["std"]).then_inc(s["norm_chain"], 1)
    dve.wait_ge(s["norm_chain"], 1)
    for k in range(KD + 2):
        if k < KD:
            nc.vector.scalar_tensor_tensor(h[:, k, :], x[:, k, :], gain[:, k:k + 1], s["rstd"], ALU.mult, ALU.mult).then_inc(
                s["h_normed" if shift is None else "h_scaled"], 1)
        if shift is not None and 1 <= k <= KD:
            dve.wait_ge(s["h_scaled"], k)
            nc.vector.tensor_scalar(h[:, k - 1, :], h[:, k - 1, :], shift[:, k - 1:k], None, ALU.add).then_inc(s["h_normed"], 1)
        if halves is not None and k >= 2:
            dve.wait_ge(s["h_hi_done"], k - 1)
            nc.vector.tensor_tensor(halves[1][:, k - 2, :], h[:, k - 2, :], halves[0][:, k - 2, :].bitcast(F32),
                                    ALU.subtract).then_inc(s["h_lo_done"], 1)


def product(nc, out, w_hi, w_lo, x_hi, x_lo, start, stop):
    nc.tensor.matmul(out, w_hi, x_hi, start=start, stop=False, skip_group_check=True)
    nc.tensor.matmul(out, w_hi, x_lo, start=False, stop=False, skip_group_check=True)
    return nc.tensor.matmul(out, w_lo, x_hi, start=False, stop=stop, skip_group_check=True)


def split_dve(dve, nc, x, hi, lo, hi_done, lo_done, n):
    nc.vector.tensor_copy(hi, x).then_inc(hi_done, 1)
    dve.wait_ge(hi_done, n)
    nc.vector.tensor_tensor(lo, x, hi.bitcast(F32), ALU.subtract).then_inc(lo_done, 1)


def wait(eng, sem, value):
    if not isinstance(value, int) or value > 0:
        eng.wait_ge(sem, value)


def turns(eng, n, unroll, body):
    rounds = n // unroll
    for r in range(unroll):
        body(r, r, n, 0)
    if rounds > 2:
        with eng.Fori(1, rounds - 1) as i:
            for r in range(unroll):
                body(i * unroll + r, r, None, i)
    if rounds > 1:
        for r in range(unroll):
            body((rounds - 1) * unroll + r, r, n, rounds - 1)


AHEAD = 2


def project_sems(tag, ring):
    return " ".join(f"{tag}_w{r}" for r in range(ring)) + f" {tag}_hi {tag}_lo {tag}_mm {tag}_out "


def project_sp(sp, s, tag, wsrc, raw, ring, n):
    def load(c, r, end, i):
        wait(sp, s[f"{tag}_lo"], c - ring + 1)
        sp.dma_start(raw[:, r], wsrc(c)).then_inc(s[f"{tag}_w{r}"], 16)

    turns(sp, n, ring, load)


def project_pe(pe, nc, s, tag, B, x_hi, x_lo, bank, ring, n, tokens, x_ready=None):
    def chunk(c, r, end, i):
        pe.wait_ge(s[f"{tag}_lo"], c + 1)
        wait(pe, s[f"{tag}_out"], c - ring + 1)
        for k in range(KD):
            if x_ready is not None and isinstance(c, int) and c == 0:
                pe.wait_ge(x_ready, k + 1)
            w = slice(k * P, (k + 1) * P)
            mm = product(nc, bank(r)[:, 0:tokens], B.w_hi[:, r, w], B.w_lo[:, r, w], x_hi[:, k, :], x_lo[:, k, :],
                         k == 0, k == KD - 1)
        mm.then_inc(s[f"{tag}_mm"], 1)

    turns(pe, n, ring, chunk)


def upper_half(act, nc, s, tag, B, ring, c, r, i):
    act.wait_ge(s[f"{tag}_w{r % ring}"], (i + r // ring) * 16 + 16)
    wait(act, s[f"{tag}_mm"], c - ring + 1)
    nc.scalar.copy(B.w_hi[:, r % ring], B.raw[:, r % ring]).then_inc(s[f"{tag}_hi"], 1)


def project_act_start(act, nc, s, tag, B, ring):
    for c in range(AHEAD):
        upper_half(act, nc, s, tag, B, ring, c, c, 0)


def project_act(act, nc, s, tag, B, ring, n, move=None, started=False):
    if not started:
        project_act_start(act, nc, s, tag, B, ring)

    def turn(c, r, end, i):
        if end is None or c + AHEAD < end:
            upper_half(act, nc, s, tag, B, ring, c + AHEAD, r + AHEAD, i)
        if move is not None:
            act.wait_ge(s[f"{tag}_mm"], c + 1)
            move(c, r).then_inc(s[f"{tag}_out"], 1)

    turns(act, n, ring, turn)


def lower_half(dve, nc, s, tag, B, c, slot):
    dve.wait_ge(s[f"{tag}_hi"], c + 1)
    nc.vector.tensor_tensor(B.w_lo[:, slot], B.raw[:, slot], B.w_hi[:, slot].bitcast(F32),
                            ALU.subtract).then_inc(s[f"{tag}_lo"], 1)


def project_dve_start(dve, nc, s, tag, B):
    for c in range(AHEAD):
        lower_half(dve, nc, s, tag, B, c, c)


def project_dve(dve, nc, s, tag, B, ring, n, move=None, started=False):
    if not started:
        project_dve_start(dve, nc, s, tag, B)

    def turn(c, r, end, i):
        if end is None or c + AHEAD < end:
            lower_half(dve, nc, s, tag, B, c + AHEAD, (r + AHEAD) % ring)
        if move is not None:
            dve.wait_ge(s[f"{tag}_mm"], c + 1)
            move(c, r).then_inc(s[f"{tag}_out"], 1)

    turns(dve, n, ring, turn)


def ffn_phase(nc, B, I, l, which, wg, wu, wd, gain):
    with ExitStack() as ctx:
        (raw, sil, hid) = alloc(nc, ctx, B, raw=(P, 6, D), sil=(P, 2, T), hid=(P, 2, T))
        (hi, lo, hid_hi, hid_lo) = alloc(nc, ctx, B, F32R, hi=(P, 6, D), lo=(P, 6, D), hid_hi=(P, 2, T), hid_lo=(P, 2, T))
        (B.c_rows, B.wada, B.adaprod, B.adasum) = alloc(
            nc, ctx, B, c_rows=(P, 2, D), wada=(P, 2, D), adaprod=(P, D), adasum=(P, 2 * ADA_CTX + ADA_X, D // 8))
        ffn_program(nc, B, l, dict(g=wg, u=wu, d=wd), gain, raw, hi, lo, sil, hid, hid_hi, hid_lo, (I["w_ada"], which))


ADA = "c_in a_w0 a_w1 a_op "
ADA_CTX, ADA_X = 4, 8


def ada_pool(pool, nc, s, B, l, w_ada, which):
    quarters = 2 * DEPTH
    both = w_ada[0:quarters * ADA_CTX].rearrange("(l f i) p d -> l f i p d", f=2, i=ADA_CTX)
    alone = w_ada[quarters * ADA_CTX:].rearrange("(l f i) p d -> l f i p d", f=2, i=ADA_X)
    mod_both = B.mod[:, 0:quarters * ADA_CTX, :].rearrange("p (l f i) v -> p l f i v", f=2, i=ADA_CTX)
    mod_alone = B.mod[:, quarters * ADA_CTX:, :].rearrange("p (l f i) v -> p l f i v", f=2, i=ADA_X)

    pool.dma_start(B.c_rows, bass.AP(tensor=B.d_cond.tensor, offset=0, ap=[[0, P], [D, 2], [1, D]])).then_inc(s["c_in"], 16)
    pool.dma_start(B.wada[:, 0], both[l, which, 0]).then_inc(s["a_w0"], 16)
    pool.wait_ge(s["c_in"], 16)
    n = 0
    add = lambda out, x, width: nc.gpsimd.tensor_tensor(out, x[..., 0:width], x[..., width:2 * width], ALU.add)
    products = 0
    for i in range(ADA_CTX + ADA_X):
        a, nxt = i % 2, i + 1
        if n:
            pool.wait_ge(s["a_op"], n)
        if nxt < ADA_CTX + ADA_X:
            src = both[l, which, nxt] if nxt < ADA_CTX else alone[l, which, nxt - ADA_CTX]
            pool.dma_start(B.wada[:, 1 - a], src).then_inc(s[f"a_w{1 - a}"], 16)
        pool.wait_ge(s[f"a_w{a}"], 16 * (i // 2) + 16)
        for v in range(2 if i < ADA_CTX else 1):
            if v:
                pool.wait_ge(s["a_op"], n)
            nc.gpsimd.tensor_tensor(B.adaprod, B.wada[:, a], B.c_rows[:, v], ALU.mult).then_inc(s["a_op"], 1)
            n += 1
            for width in (D // 2, D // 4, D // 8):
                pool.wait_ge(s["a_op"], n)
                dst = B.adaprod[:, 0:width] if width > D // 8 else B.adasum[:, products, :]
                add(dst, B.adaprod, width).then_inc(s["a_op"], 1)
                n += 1
            products += 1
    width = D // 16
    while width > 1:
        pool.wait_ge(s["a_op"], n)
        add(B.adasum[:, :, 0:width], B.adasum, width).then_inc(s["a_op"], 1)
        n += 1
        width //= 2
    pool.wait_ge(s["a_op"], n)
    add(mod_both[:, l, which].unsqueeze(3), B.adasum[:, 0:2 * ADA_CTX, :].rearrange("p (i v) t -> p i v t", v=2), 1).then_inc(s["a_op"], 1)
    add(mod_alone[:, l, which, :, 0:1], B.adasum[:, 2 * ADA_CTX:, :], 1).then_inc(s["a_op"], 1)
    pool.wait_ge(s["a_op"], n + 2)


def ffn_program(nc, B, l, src, gain, raw, hi, lo, sil, hid, hid_hi, hid_lo, ada):
    x, ps, con = B.x, B.ps, B.con
    acc = ps[:, 0:4, :].rearrange("p b (c t) -> p (b c) t", t=T)
    gu = [ps[:, 4 + a, :].rearrange("p (w t) -> p w t", t=T) for a in range(2)]
    ms = ps[:, 6, 0:T]
    slot = {"g": 0, "u": 2, "d": 4}
    names = " ".join(f"w{k}{a}" for k in "gud" for a in range(2)) + " " + " ".join(f"{k}_{h}" for k in "gud" for h in ("hi", "lo"))
    with phase(nc, NORM + ADA + names + " gu_done silu_done hid_mul hid_hi_done hidden_ready down_done x_done") as (block, s):
        s.update(std=B.std[:, 0:T], var=B.var[:, 0:T], rstd=B.rstd[:, 0:T])

        @block.gpsimd
        def _(pool):
            ada_pool(pool, nc, s, B, l, *ada)

        @block.sync
        def _(sp):
            def load(c, a, end, i):
                for k in "gud":
                    wait(sp, s[f"{k}_lo"], c - 1)
                    sp.dma_start(raw[:, slot[k] + a], src[k][l, c]).then_inc(s[f"w{k}{a}"], 16)

            turns(sp, FC, 2, load)

        @block.tensor
        def _(pe):
            for b in range(4):
                nc.tensor.matmul(ps[:, b, :], con("zeros")[:, 0:P], con("zeros"), start=True, stop=False,
                                 skip_group_check=True)
            norm_pe(pe, nc, s, B.sq, ms, con("mean_d"))

            def gate_up(c, a):
                wait(pe, s["hidden_ready"], c - 1)
                for j, kind in enumerate("gu"):
                    pe.wait_ge(s[f"{kind}_lo"], c + 1)
                    for k in range(KD):
                        if kind == "g" and isinstance(c, int) and c == 0:
                            pe.wait_ge(s["h_lo_done"], k + 1)
                        w = slice(k * P, (k + 1) * P)
                        mm = product(nc, gu[a][:, j, :], hi[:, slot[kind] + a, w], lo[:, slot[kind] + a, w],
                                     B.h_hi[:, k, :], B.h_lo[:, k, :], k == 0, k == KD - 1)
                mm.then_inc(s["gu_done"], 1)

            def down(c, a):
                pe.wait_ge(s["hidden_ready"], c + 1)
                pe.wait_ge(s["d_lo"], c + 1)
                for k in range(KD):
                    w = slice(k * P, (k + 1) * P)
                    mm = product(nc, acc[:, k, :], hi[:, slot["d"] + a, w], lo[:, slot["d"] + a, w],
                                 hid_hi[:, a, :], hid_lo[:, a, :], False, False)
                mm.then_inc(s["down_done"], 1)

            gate_up(0, 0)
            gate_up(1, 1)
            down(0, 0)
            with pe.Fori(1, FC // 2) as i:
                gate_up(2 * i, 0)
                down(2 * i - 1, 1)
                gate_up(2 * i + 1, 1)
                down(2 * i, 0)
            down(FC - 1, 1)

        @block.scalar
        def _(act):
            def upper(kind, c, a, i):
                act.wait_ge(s[f"w{kind}{a % 2}"], (i + a // 2) * 16 + 16)
                if kind == "d":
                    wait(act, s["down_done"], c - 1)
                else:
                    wait(act, s["gu_done"], c - 1)
                nc.scalar.copy(hi[:, slot[kind] + a % 2], raw[:, slot[kind] + a % 2]).then_inc(s[f"{kind}_hi"], 1)

            def turn(c, a, end, i):
                if end is None or c + 1 < end:
                    upper("g", c + 1, a + 1, i)
                    upper("u", c + 1, a + 1, i)
                upper("d", c, a, i)
                act.wait_ge(s["gu_done"], c + 1)
                wait(act, s["hid_mul"], c - 1)
                nc.scalar.activation(sil[:, a, :], gu[a][:, 0, :], ACT.Silu).then_inc(s["silu_done"], 1)

            def first():
                upper("g", 0, 0, 0)
                upper("u", 0, 0, 0)

            norm_act(act, nc, s, x, B.sq, B.sq, B.h_hi, first)
            turns(act, FC, 2, turn)

        @block.vector
        def _(dve):
            def lower(kind, c, a):
                dve.wait_ge(s[f"{kind}_hi"], c + 1)
                j = slot[kind] + a % 2
                nc.vector.tensor_tensor(lo[:, j], raw[:, j], hi[:, j].bitcast(F32), ALU.subtract).then_inc(s[f"{kind}_lo"], 1)

            def turn(c, a, end, i):
                if end is None or c + 1 < end:
                    lower("g", c + 1, a + 1)
                    lower("u", c + 1, a + 1)
                lower("d", c, a)
                dve.wait_ge(s["silu_done"], c + 1)
                nc.vector.tensor_tensor(hid[:, a, :], sil[:, a, :], gu[a][:, 1, :], ALU.mult).then_inc(s["hid_mul"], 1)
                dve.wait_ge(s["hid_mul"], c + 1)
                wait(dve, s["down_done"], c - 1)
                split_dve(dve, nc, hid[:, a, :], hid_hi[:, a, :], hid_lo[:, a, :], s["hid_hi_done"], s["hidden_ready"], c + 1)

            def first():
                lower("g", 0, 0)
                lower("u", 0, 0)

            norm_dve(dve, nc, s, x, B.sq, ms, gain, halves=(B.h_hi, B.h_lo), between=first)
            turns(dve, FC, 2, turn)
            dve.wait_ge(s["down_done"], FC)
            for b in range(4):
                nc.vector.scalar_tensor_tensor(x[:, 2 * b:2 * b + 2, :], acc[:, 2 * b:2 * b + 2, :], 0.5,
                                               x[:, 2 * b:2 * b + 2, :], ALU.mult, ALU.add).then_inc(s["x_done"], 1)
            dve.wait_ge(s["x_done"], 4)


def z_phase(nc, B, l, w_z, gain):
    ps, con = B.ps, B.con
    ring = 4
    with phase(nc, NORM + project_sems("z", ring) + "ff_w ff_mm ff_out") as (block, s):
        s.update(std=B.std[:, 0:T], var=B.var[:, 0:T], rstd=B.rstd[:, 0:T])

        @block.sync
        def _(sp):
            sp.dma_start(B.w_ff, B.d_wff[l]).then_inc(s["ff_w"], 16)
            project_sp(sp, s, "z", lambda c: w_z[l, c], B.raw, ring, ZC)

        @block.tensor
        def _(pe):
            norm_pe(pe, nc, s, B.sq, ps[:, 6, 0:T], con("mean_d"))
            project_pe(pe, nc, s, "z", B, B.h_hi, B.h_lo, lambda r: ps[:, r, :], ring, ZC, T, s["h_lo_done"])
            pe.wait_ge(s["ff_w"], 16)
            for c in range(TC):
                for k in range(KD):
                    mm = nc.tensor.matmul(ps[:, 7, 4 * c:4 * c + 4], B.sq[:, k, c * P:(c + 1) * P],
                                          B.w_ff[:, k, :], start=(k == 0), stop=(k == KD - 1))
            mm.then_inc(s["ff_mm"], 1)

        @block.scalar
        def _(act):
            norm_act(act, nc, s, B.x, B.sq, B.sq, B.h_hi, lambda: project_act_start(act, nc, s, "z", B, ring))
            project_act(act, nc, s, "z", B, ring, ZC, lambda c, r: nc.scalar.copy(B.z[:, c, :], ps[:, r, 0:T]), started=True)

        @block.vector
        def _(dve):
            norm_dve(dve, nc, s, B.x, B.sq, ps[:, 6, 0:T], gain, halves=(B.h_hi, B.h_lo),
                     between=lambda: project_dve_start(dve, nc, s, "z", B))
            project_dve(dve, nc, s, "z", B, ring, ZC, started=True)
            dve.wait_ge(s["ff_mm"], 1)
            nc.vector.tensor_copy(B.ff, ps[:, 7, 0:8]).then_inc(s["ff_out"], 1)
            dve.wait_ge(s["ff_out"], 1)


CA, CB, SB, SC, SX, AQ, AK, AV, FQ, FK, FV = 0, 2, 4, 6, 8, 10, 12, 13, 14, 16, 18


def branch_phase(nc, B, l, w_g):
    ps, con, z, vec = B.ps, B.con, B.z, B.vec
    ring = 4
    v = lambda name, j=0, n=1: vec[:, VEC[name][0] + j:VEC[name][0] + j + n]
    with phase(nc, project_sems("g", ring) + "qk_sq qk_ms qk_var qk_std qk_rstd qk_spread v_turned v_copied sig "
               "ff_in ff_exp ff_in2 ff_ln conv_done conv_sq cen_in mean cen var std ln_in silu chain done") as (block, s):
        msq = ps[0:14, 6, 0:T]

        @block.sync
        def _(sp):
            project_sp(sp, s, "g", lambda c: w_g[l, c], B.raw, ring, GC)

        @block.tensor
        def _(pe):
            pe.wait_ge(s["qk_sq"], 2)
            for c in range(7):
                mm = nc.tensor.matmul(msq, con("head_mean")[:, c, :], B.qksq[:, c, :], start=(c == 0), stop=(c == 6))
            mm.then_inc(s["qk_ms"], 1)
            for j, c in enumerate((AV, FV, FV + 1)):
                for t in range(TC):
                    n = j * TC + t
                    mm = nc.tensor.transpose(ps[:, 4 + n // 4, (n % 4) * P:(n % 4 + 1) * P],
                                             z[:, c, t * P:(t + 1) * P], con("ident"))
            mm.then_inc(s["v_turned"], 1)
            pe.wait_ge(s["qk_rstd"], 1)
            pe.wait_ge(s["v_copied"], 1)
            for c in range(7):
                mm = nc.tensor.matmul(ps[:, 4 + c // 2, (c % 2) * T:(c % 2 + 1) * T], con("head_spread")[0:14, c, :],
                                      B.hrstd[0:14, :], start=(c % 2 == 0), stop=True, skip_group_check=True)
            mm.then_inc(s["qk_spread"], 1)
            project_pe(pe, nc, s, "g", B, B.h_hi, B.h_lo, lambda r: ps[:, r, :], ring, GC, T)
            pe.wait_ge(s["conv_done"], 1)
            for c in range(2):
                mm = nc.tensor.matmul(ps[:, 4, 0:T], con("mean_conv"), B.u[:, c, :], start=(c == 0), stop=(c == 1))
            mm.then_inc(s["mean"], 1)
            pe.wait_ge(s["conv_sq"], 1)
            for c in range(2):
                mm = nc.tensor.matmul(ps[:, 5, 0:T], con("mean_conv"), B.sq[:, c, :], start=(c == 0), stop=(c == 1))
            mm.then_inc(s["var"], 1)

        @block.scalar
        def _(act):
            nc.scalar.activation(B.qksq[:, 0:3, :], z[:, AQ:AQ + 3, :], ACT.Square).then_inc(s["qk_sq"], 1)
            nc.scalar.activation(B.qksq[:, 3:7, :], z[:, FQ:FQ + 4, :], ACT.Square).then_inc(s["qk_sq"], 1)
            nc.scalar.activation(B.u, z[:, CB:CB + 2, :], ACT.Sigmoid).then_inc(s["sig"], 1)
            project_act_start(act, nc, s, "g", B, ring)
            act.wait_ge(s["qk_var"], 1)
            nc.scalar.activation(B.hstd[0:14, :], B.hvar[0:14, :], ACT.Sqrt).then_inc(s["qk_std"], 1)
            act.wait_ge(s["ff_in"], 1)
            nc.scalar.activation(B.ffe, B.ffn_, ACT.Exp).then_inc(s["ff_exp"], 1)
            act.wait_ge(s["ff_in2"], 1)
            nc.scalar.activation(B.ffn_, B.ffe, ACT.Ln).then_inc(s["ff_ln"], 1)
            project_act(act, nc, s, "g", B, ring, GC,
                        lambda c, r: nc.scalar.activation(B.gates[:, c, :], ps[:, r, 0:T], ACT.Sigmoid), started=True)
            act.wait_ge(s["cen"], 1)
            nc.scalar.activation(B.sq[:, 0:2, :], B.u, ACT.Square).then_inc(s["conv_sq"], 1)
            act.wait_ge(s["cen_in"], 1)
            nc.scalar.activation(B.std[:, 0:T], B.var[:, 0:T], ACT.Sqrt).then_inc(s["std"], 1)
            act.wait_ge(s["ln_in"], 1)
            nc.scalar.activation(B.b_conf, B.u, ACT.Silu).then_inc(s["silu"], 1)
            act.wait_ge(s["silu"], 1)

        @block.vector
        def _(dve):
            ch = Chain(dve, s["chain"])
            dve.wait_ge(s["qk_ms"], 1)
            nc.vector.tensor_scalar(B.hvar[0:14, :], msq, EPS, None, ALU.add).then_inc(s["qk_var"], 1)
            for t in range(TC):
                ch.did(nc.vector.tensor_tensor(B.ff[:, 4 * t:4 * t + 4], B.ff[:, 4 * t:4 * t + 4], v("b_forget", 0, 4), ALU.add))
            dve.wait_ge(s["chain"], ch.n)
            ch.link(nc.vector.tensor_scalar(B.ffe, B.ff, -1.0, None, ALU.mult))
            nc.vector.tensor_tensor(B.ffn_, B.ff, B.ffe, ALU.min).then_inc(s["ff_in"], 1)
            project_dve_start(dve, nc, s, "g", B)
            dve.wait_ge(s["qk_std"], 1)
            nc.vector.reciprocal(B.hrstd[0:14, :], B.hstd[0:14, :]).then_inc(s["qk_rstd"], 1)
            dve.wait_ge(s["ff_exp"], 1)
            ch.link(nc.vector.tensor_scalar(B.ffe, B.ffe, 1.0, None, ALU.add))
            nc.vector.tensor_scalar(B.ff, B.ff, 0.0, None, ALU.min).then_inc(s["ff_in2"], 1)
            dve.wait_ge(s["v_turned"], 1)
            for j in range(3):
                for t in range(TC):
                    n = j * TC + t
                    last = nc.vector.tensor_copy(B.vtok[:, t, j * P:(j + 1) * P],
                                                 ps[:, 4 + n // 4, (n % 4) * P:(n % 4 + 1) * P])
            last.then_inc(s["v_copied"], 1)
            for j, name in ((0, "swa_q"), (1, "fox_q")):
                ch.link(nc.vector.tensor_scalar(B.qgain[:, j:j + 1], v(name), HD ** -0.5, None, ALU.mult))
            dve.wait_ge(s["qk_spread"], 1)
            for c, (zc, g) in enumerate(((AQ, B.qgain[:, 0:1]), (AQ + 1, B.qgain[:, 0:1]), (AK, v("swa_k")),
                                         (FQ, B.qgain[:, 1:2]), (FQ + 1, B.qgain[:, 1:2]), (FK, v("fox_k")),
                                         (FK + 1, v("fox_k")))):
                ch.did(nc.vector.scalar_tensor_tensor(z[:, zc, :], z[:, zc, :], g, ps[:, 4 + c // 2, (c % 2) * T:(c % 2 + 1) * T],
                                                      ALU.mult, ALU.mult))
            dve.wait_ge(s["chain"], ch.n)
            for g in range(2):
                for half in range(2):
                    last = nc.vector.tensor_copy(B.kdup[half * HD:(half + 1) * HD, g, :], z[g * HD:(g + 1) * HD, AK, :])
            last.then_inc(s["done"], 1)
            dve.wait_ge(s["done"], 1)
            for j in range(AHEAD, 2 * AHEAD):
                lower_half(dve, nc, s, "g", B, j, j % ring)
            dve.wait_ge(s["ff_ln"], 1)
            ch.link(nc.vector.tensor_tensor(B.ff, B.ff, B.ffn_, ALU.subtract))
            for h in range(4):
                ch.did(nc.vector.tensor_scalar(B.lfa0[:, h, :], con("upto")[:, 0, :], B.ff[:, h:h + 1], None, ALU.mult))
                ch.did(nc.vector.tensor_scalar(B.lfa1[:, h, :], con("upto")[:, 1, P:T], B.ff[:, 4 + h:5 + h], None, ALU.mult))
            pad = CONV_K - 1
            for c in range(2):
                ch.did(nc.vector.memset(B.upad[:, c, 0:pad], 0.0))
            ch.did(nc.vector.tensor_tensor(B.upad[:, :, pad:], z[:, SC:SC + 2, :], z[:, SX:SX + 2, :], ALU.mult))
            dve.wait_ge(s["chain"], ch.n)
            for j in range(SC_K):
                for c in range(2):
                    w = v("sc", c * SC_K + j)
                    x_in = B.upad[:, c, pad - SC_K + 1 + j:pad - SC_K + 1 + j + T]
                    if j == 0:
                        ch.did(nc.vector.tensor_scalar(B.b_sc[:, c, :], x_in, w, None, ALU.mult))
                    else:
                        dve.wait_ge(s["chain"], ch.n - 1)
                        ch.did(nc.vector.scalar_tensor_tensor(B.b_sc[:, c, :], x_in, w, B.b_sc[:, c, :], ALU.mult, ALU.add))
            dve.wait_ge(s["chain"], ch.n)
            ch.did(nc.vector.tensor_tensor(B.b_sc, B.b_sc, z[:, SB:SB + 2, :], ALU.mult))
            dve.wait_ge(s["sig"], 1)
            ch.link(nc.vector.tensor_tensor(B.upad[:, :, pad:], z[:, CA:CA + 2, :], B.u, ALU.mult))
            for j in range(CONV_K):
                if j + 2 * AHEAD < GC:
                    lower_half(dve, nc, s, "g", B, j + 2 * AHEAD, j % ring)
                for c in range(2):
                    w = v("dw", c * CONV_K + j)
                    x_in = B.upad[:, c, j:j + T]
                    if j == 0:
                        ch.did(nc.vector.tensor_scalar(B.u[:, c, :], x_in, w, v("dw_b", c), ALU.mult, ALU.add))
                    else:
                        dve.wait_ge(s["chain"], ch.n - 1)
                        ch.did(nc.vector.scalar_tensor_tensor(B.u[:, c, :], x_in, w, B.u[:, c, :], ALU.mult, ALU.add))
            for j in range(CONV_K + 2 * AHEAD, GC):
                lower_half(dve, nc, s, "g", B, j, j % ring)
            dve.wait_ge(s["chain"], ch.n)
            dve.sem_inc(s["conv_done"], 1)
            dve.wait_ge(s["mean"], 1)
            for c in range(2):
                ch.did(nc.vector.tensor_tensor(B.u[:, c, :], B.u[:, c, :], ps[:, 4, 0:T], ALU.subtract))
            dve.wait_ge(s["chain"], ch.n)
            dve.sem_inc(s["cen"], 1)
            dve.wait_ge(s["var"], 1)
            nc.vector.tensor_scalar(B.var[:, 0:T], ps[:, 5, 0:T], EPS, None, ALU.add).then_inc(s["cen_in"], 1)
            dve.wait_ge(s["std"], 1)
            ch.link(nc.vector.reciprocal(B.rstd[:, 0:T], B.std[:, 0:T]))
            for c in range(2):
                ch.did(nc.vector.scalar_tensor_tensor(B.u[:, c, :], B.u[:, c, :], v("ln_g", c), B.rstd[:, 0:T],
                                                      ALU.mult, ALU.mult))
            dve.wait_ge(s["chain"], ch.n)
            for c in range(2):
                ch.did(nc.vector.tensor_scalar(B.u[:, c, :], B.u[:, c, :], v("ln_b", c), None, ALU.add))
            dve.wait_ge(s["chain"], ch.n)
            dve.sem_inc(s["ln_in"], 1)


DEPTH_A = 3


def attention_phase(nc, B, units, width, prefetch=None):
    ps, con = B.ps, B.con
    n = len(units)
    with phase(nc, "scores_ready max_ready exp_ready probs_ready turned probs_t_ready out_ready out_copied chain prefetched") as (block, s):

        @block.sync
        def _(sp):
            if prefetch is not None:
                sp.dma_start(*prefetch).then_inc(s["prefetched"], 16)
                sp.wait_ge(s["prefetched"], 16)

        @block.tensor
        def _(pe):
            def scores(u):
                if u >= DEPTH_A:
                    pe.wait_ge(s["max_ready"], u - DEPTH_A + 1)
                units[u]["scores"](ps[:, u % DEPTH_A, 0:width]).then_inc(s["scores_ready"], 1)

            def turn(u):
                pe.wait_ge(s["probs_ready"], u + 1)
                if u >= 2:
                    pe.wait_ge(s["probs_t_ready"], u - 1)
                for j in range(width // P):
                    mm = nc.tensor.transpose(ps[:, 3 + u % 2, j * P:(j + 1) * P], B.prob[:, u % DEPTH_A, j * P:(j + 1) * P],
                                             con("ident"))
                mm.then_inc(s["turned"], 1)

            def values(u):
                pe.wait_ge(s["probs_t_ready"], u + 1)
                if u >= 2:
                    pe.wait_ge(s["out_copied"], u - 1)
                v = units[u]["values"]
                lo = units[u]["row"]
                for j, vj in enumerate(v):
                    mm = nc.tensor.matmul(ps[lo:lo + HD, 5 + u % 2, 0:P], vj, B.prob_t[:, u % 2, j * P:(j + 1) * P],
                                          start=(j == 0), stop=(j == len(v) - 1))
                mm.then_inc(s["out_ready"], 1)

            scores(0)
            scores(1)
            for u in range(n + 1):
                if u + 2 < n:
                    scores(u + 2)
                if u < n:
                    turn(u)
                if u >= 1:
                    values(u - 1)

        @block.scalar
        def _(act):
            def turned_copy(u):
                act.wait_ge(s["turned"], u + 1)
                if u >= 2:
                    act.wait_ge(s["out_ready"], u - 1)
                nc.scalar.copy(B.prob_t[:, u % 2, 0:width], ps[:, 3 + u % 2, 0:width]).then_inc(s["probs_t_ready"], 1)

            for u in range(n + 1):
                if u < n:
                    act.wait_ge(s["max_ready"], u + 1)
                    if units[u]["sink"] is not None:
                        nc.scalar.activation(B.stat[:, u % DEPTH_A, 2:3], units[u]["sink"], ACT.Exp, bias=B.stat[:, u % DEPTH_A, 0:1])
                    nc.scalar.activation(B.prob[:, u % DEPTH_A, 0:width], B.prob[:, u % DEPTH_A, 0:width], ACT.Exp,
                                         bias=B.stat[:, u % DEPTH_A, 0:1], accum_out=B.stat[:, u % DEPTH_A, 1:2]).then_inc(s["exp_ready"], 1)
                if u >= 1:
                    turned_copy(u - 1)

        @block.vector
        def _(dve):
            ch = Chain(dve, s["chain"])

            def masked_max(u):
                dve.wait_ge(s["scores_ready"], u + 1)
                if u >= DEPTH_A:
                    dve.wait_ge(s["turned"], u - DEPTH_A + 1)
                table = units[u]["table"]
                m = table.shape[1]
                ch.did(nc.vector.tensor_tensor(B.prob[:, u % DEPTH_A, 0:m], ps[:, u % DEPTH_A, 0:m], table, ALU.add))
                if m < width:
                    ch.did(nc.vector.tensor_copy(B.prob[:, u % DEPTH_A, m:width], ps[:, u % DEPTH_A, m:width]))
                dve.wait_ge(s["chain"], ch.n)
                nm = B.stat[:, u % DEPTH_A, 0:1]
                red = nc.vector.tensor_reduce(nm, B.prob[:, u % DEPTH_A, 0:width], AX, ALU.max, negate=True)
                if units[u]["sink"] is not None:
                    ch.link(red)
                    red = nc.vector.tensor_tensor(nm, nm, units[u]["minus_sink"], ALU.min)
                red.then_inc(s["max_ready"], 1)

            def norm(u):
                dve.wait_ge(s["exp_ready"], u + 1)
                den = B.stat[:, u % DEPTH_A, 1:2]
                if units[u]["sink"] is not None:
                    ch.link(nc.vector.tensor_tensor(den, den, B.stat[:, u % DEPTH_A, 2:3], ALU.add))
                ch.link(nc.vector.reciprocal(B.stat[:, u % DEPTH_A, 3:4], den))
                nc.vector.tensor_scalar(B.prob[:, u % DEPTH_A, 0:width], B.prob[:, u % DEPTH_A, 0:width], B.stat[:, u % DEPTH_A, 3:4], None,
                                        ALU.mult).then_inc(s["probs_ready"], 1)

            def out(u):
                dve.wait_ge(s["out_ready"], u + 1)
                lo = units[u]["row"]
                nc.vector.tensor_copy(units[u]["out"], ps[lo:lo + HD, 5 + u % 2, 0:P]).then_inc(s["out_copied"], 1)

            for u in range(n + 3):
                if u < n:
                    masked_max(u)
                if 1 <= u <= n:
                    norm(u - 1)
                if u >= 3:
                    out(u - 3)
            dve.wait_ge(s["out_copied"], n)


def first_attention(nc, B, prefetch):
    ps, con, z = B.ps, B.con, B.z
    units = []
    for h in range(4):
        lo = (h % 2) * HD
        for qc in range(TC):
            def swa(dst, h=h, lo=lo, qc=qc):
                return nc.tensor.matmul(dst, z[lo:lo + HD, AQ + h // 2, qc * P:(qc + 1) * P], B.kdup[lo:lo + HD, h // 2, :],
                                        start=True, stop=True)

            units.append(dict(scores=swa, table=B.swa_table[:, h * TC + qc, :], sink=B.vec[:, VEC["sink"][0] + h:VEC["sink"][0] + h + 1],
                              minus_sink=B.nsink[:, h:h + 1], row=lo,
                              values=[B.vtok[:, t, (h // 2) * HD:(h // 2 + 1) * HD] for t in range(TC)],
                              out=B.b_swa[lo:lo + HD, h // 2, qc * P:(qc + 1) * P]))
    for h in range(4):
        lo = (h % 2) * HD
        for qc in range(TC):
            def fox(dst, h=h, lo=lo, qc=qc):
                nc.tensor.matmul(dst, z[lo:lo + HD, FQ + h // 2, qc * P:(qc + 1) * P], z[lo:lo + HD, FK + h // 2, :],
                                 start=True, stop=False)
                mm = nc.tensor.matmul(dst, B.lfa0[:, h, qc * P:(qc + 1) * P], con("after")[:, 0, 0:T], start=False, stop=(qc == 0))
                if qc == 1:
                    mm = nc.tensor.matmul(dst, B.lfa1[:, h, :], con("after")[:, 1, 0:T], start=False, stop=True)
                return mm

            units.append(dict(scores=fox, table=con("causal")[:, qc, :], sink=None, row=lo,
                              values=[B.vtok[:, t, P + h * HD:P + (h + 1) * HD] for t in range(TC)],
                              out=B.b_fox[lo:lo + HD, h // 2, qc * P:(qc + 1) * P]))
    attention_phase(nc, B, units, T, prefetch)


def merge_phase(nc, B, acts, per, gates, n_branch):
    ps = B.ps
    with phase(nc, "h_hi_done h_lo_done prod merged chain") as (block, s):
        nb2 = n_branch // 2

        @block.tensor
        def _(pe):
            for c in range(KD):
                if c >= 2:
                    pe.wait_ge(s["merged"], c - 1)
                for b in range(n_branch):
                    bank = ps[:, (c % 2) * 2 + b // 2, (b % 2) * T:(b % 2 + 1) * T]
                    for k in range(per):
                        mm = nc.tensor.matmul(bank, B.wb[:, b * per + k, c * P:(c + 1) * P], acts[b][:, k, :],
                                              start=(k == 0), stop=(k == per - 1), skip_group_check=True)
                mm.then_inc(s["prod"], 1)

        @block.vector
        def _(dve):
            ch = Chain(dve, s["chain"])
            for c in range(KD):
                dve.wait_ge(s["prod"], c + 1)
                for b in range(nb2):
                    bank = ps[:, (c % 2) * 2 + b, :].rearrange("p (b t) -> p b t", t=T)
                    g = gates[:, 2 * b * KD + c:2 * b * KD + c + KD + 1:KD, :]
                    ch.did(nc.vector.tensor_tensor(B.mtmp[:, 2 * b:2 * b + 2, :], bank, g, ALU.mult))
                dve.wait_ge(s["chain"], ch.n)
                if nb2 == 2:
                    ch.link(nc.vector.tensor_tensor(B.mtmp[:, 0:2, :], B.mtmp[:, 0:2, :], B.mtmp[:, 2:4, :], ALU.add))
                nc.vector.tensor_tensor(B.sq[:, c, :], B.mtmp[:, 0, :], B.mtmp[:, 1, :], ALU.add).then_inc(s["merged"], 1)
                dve.wait_ge(s["merged"], c + 1)
                split_dve(dve, nc, B.sq[:, c, :], B.h_hi[:, c, 0:T], B.h_lo[:, c, 0:T], s["h_hi_done"], s["h_lo_done"], c + 1)
            dve.wait_ge(s["h_lo_done"], KD)


def out_phase(nc, B, wsrc, dst, add, ring=4):
    ps = B.ps
    with phase(nc, project_sems("o", ring)) as (block, s):

        @block.sync
        def _(sp):
            project_sp(sp, s, "o", wsrc, B.raw, ring, KD)

        @block.tensor
        def _(pe):
            pe_src = (B.h_hi[:, :, 0:T], B.h_lo[:, :, 0:T])
            project_pe(pe, nc, s, "o", B, *pe_src, lambda r: ps[:, r, :], ring, KD, T)

        @block.scalar
        def _(act):
            project_act(act, nc, s, "o", B, ring, KD)

        @block.vector
        def _(dve):
            def move(c, r):
                if add:
                    return nc.vector.tensor_tensor(dst[:, c, :], dst[:, c, :], ps[:, r, 0:T], ALU.add)
                return nc.vector.tensor_copy(dst[:, c, :], ps[:, r, 0:T])

            project_dve(dve, nc, s, "o", B, ring, KD, move)
            dve.wait_ge(s["o_out"], KD)


class Bufs:

    stage = "whole"


def alloc(nc, ctx, B, dtype=F32, **spec):
    made = []
    for name, shape in spec.items():
        t = ctx.enter_context(nc.sbuf_tensor(f"{name}_{B.stage}{len(PHASES)}", list(shape), dtype))
        made.append(t[tuple(slice(None) for _ in shape)])
    return made


def split_ring(nc, ctx, B, ring):
    (B.raw,) = alloc(nc, ctx, B, raw=(P, ring, D))
    B.w_hi, B.w_lo = alloc(nc, ctx, B, F32R, w_hi=(P, ring, D), w_lo=(P, ring, D))


def first_block_program(nc, B, I):
    B.stage = "first"
    with ExitStack() as ctx:
        (B.vec, B.nsink, B.swa_table) = alloc(nc, ctx, B, vec=(P, NVEC), nsink=(P, 4), swa_table=(P, 4 * TC, T))
        B.h_hi, B.h_lo = alloc(nc, ctx, B, F32R, h_hi=(P, KD, T), h_lo=(P, KD, T))
        with ExitStack() as small:
            (B.relb, B.line, B.c_row) = alloc(nc, small, B, relb=(N_BUCKETS, 4), line=(P, 4, 512), c_row=(1, 2 * D))
            swa_table_phase(nc, B, I)
        with nc.Fori(0, DEPTH) as l:
            layer_vec_phase(nc, B, I, l)
            v = lambda name: B.vec[:, VEC[name][0]:VEC[name][0] + VEC[name][1]]
            ffn_phase(nc, B, I, l, 0, I["ffn1_wg"], I["ffn1_wu"], I["ffn1_wd"], v("ffn1"))
            mixer(nc, B, I, l, v("mix"))
            ffn_phase(nc, B, I, l, 1, I["ffn2_wg"], I["ffn2_wu"], I["ffn2_wd"], v("ffn2"))


def mixer(nc, B, I, l, gain):
    with ExitStack() as ctx:
        (B.w_ff, B.z, B.ff, B.ffe, B.ffn_, B.vtok, B.qgain, B.kdup, B.lfa0, B.lfa1, B.u, B.b_sc, B.gates,
         B.pp, B.stat) = alloc(
            nc, ctx, B, w_ff=(P, KD, 4),
            z=(P, ZC, T), ff=(P, 8), ffe=(P, 8), ffn_=(P, 8),
            vtok=(P, TC, 384), qgain=(P, 2), kdup=(P, 2, T), lfa0=(P, 4, T), lfa1=(P, 4, P),
            u=(P, 2, T), b_sc=(P, 2, T), gates=(P, GC, T),
            pp=(P, 2048), stat=(P, DEPTH_A, 4))
        B.qksq = B.pp[:, 0:7 * T].rearrange("p (c t) -> p c t", t=T)
        B.prob = B.pp[:, 0:DEPTH_A * T].rearrange("p (a t) -> p a t", t=T)
        B.prob_t = B.pp[:, DEPTH_A * T:(DEPTH_A + 2) * T].rearrange("p (a t) -> p a t", t=T)
        B.mtmp = B.pp[:, 1024:2048].rearrange("p (c t) -> p c t", t=T)
        padded = CONV_K - 1 + T
        B.upad = B.pp[:, 0:2 * padded].rearrange("p (c t) -> p c t", t=padded)
        B.hvar, B.hstd, B.hrstd = B.var[:, T:], B.std[:, T:], B.rstd[:, T:]
        B.b_conf = B.u
        B.d_wff = I["w_ff"]
        with ExitStack() as ring:
            split_ring(nc, ring, B, 4)
            z_phase(nc, B, l, I["w_z"], gain)
            branch_phase(nc, B, l, I["w_g"])
        with ExitStack() as whole:
            (B.wb, B.b_swa, B.b_fox) = alloc(nc, whole, B, wb=(P, 8, D), b_swa=(P, 2, T), b_fox=(P, 2, T))
            first_attention(nc, B, (B.wb, I["w_branch"][l]))
            merge_phase(nc, B, [B.b_conf, B.b_sc, B.b_swa, B.b_fox], 2, B.gates, 4)
    with ExitStack() as ring:
        split_ring(nc, ring, B, 4)
        out_phase(nc, B, lambda c: I["w_out"][l, c], B.x, True)


def swa_table_phase(nc, B, I):
    line = B.line
    ps, con = B.ps, B.con
    with phase(nc, "loaded relb_in bias_consts_in line_mm line_ready line_out table_in masked c_in silu c_out") as (block, s):

        @block.sync
        def _(sp):
            first, last = B.con_tables
            sp.dma_start(B.relb, I["rel_bias"]).then_inc(s["relb_in"], 16)
            sp.dma_start(B.con_all[:, first:last], I["const"][:, first:last]).then_inc(s["bias_consts_in"], 16)
            sp.dma_start(B.c_row, I["c_row"]).then_inc(s["c_in"], 16)
            sp.wait_ge(s["line_ready"], 1)
            sp.dma_start(B.d_line, line).then_inc(s["line_out"], 16)
            sp.wait_ge(s["line_out"], 16)
            for h in range(4):
                for qc in range(TC):
                    skew = bass.AP(tensor=B.d_line.tensor, offset=h * 512 + P - 1 + (0 if qc else P), ap=[[4 * 512 - 1, P], [1, T]])
                    sp.dma_start(B.swa_table[:, h * TC + qc, :], skew).then_inc(s["table_in"], 16)
            sp.wait_ge(s["silu"], 1)
            sp.dma_start(B.d_cond, B.c_row).then_inc(s["c_out"], 16)
            sp.wait_ge(s["c_out"], 16)

        @block.scalar
        def _(act):
            first, last = B.con_tables
            nc.scalar.dma_start(B.x, I["x"]).then_inc(s["loaded"], 16)
            nc.scalar.dma_start(B.con_all[:, 0:first], I["const"][:, 0:first]).then_inc(s["loaded"], 16)
            nc.scalar.dma_start(B.con_all[:, last:], I["const"][:, last:]).then_inc(s["loaded"], 16)
            act.wait_ge(s["c_in"], 16)
            nc.scalar.activation(B.c_row, B.c_row, ACT.Silu).then_inc(s["silu"], 1)
            act.wait_ge(s["loaded"], 48)

        @block.tensor
        def _(pe):
            pe.wait_ge(s["bias_consts_in"], 16)
            pe.wait_ge(s["relb_in"], 16)
            for h in range(4):
                mm = nc.tensor.matmul(ps[:, h, :], B.relb[:, h:h + 1].broadcast_to([N_BUCKETS, P]), con("bucket")[0:N_BUCKETS, :],
                                      start=True, stop=True)
            mm.then_inc(s["line_mm"], 1)

        @block.vector
        def _(dve):
            dve.wait_ge(s["line_mm"], 1)
            nc.vector.tensor_copy(line, ps[:, 0:4, :]).then_inc(s["line_ready"], 1)
            dve.wait_ge(s["table_in"], 16 * 4 * TC)
            for h in range(4):
                nc.vector.tensor_tensor(B.swa_table[:, h * TC:(h + 1) * TC, :], B.swa_table[:, h * TC:(h + 1) * TC, :],
                                        con("window"), ALU.add).then_inc(s["masked"], 1)
            dve.wait_ge(s["masked"], 4)


def layer_vec_phase(nc, B, I, l):
    with phase(nc, "vec_in nsink_ready") as (block, s):

        @block.sync
        def _(sp):
            sp.dma_start(B.vec, I["vec"][l]).then_inc(s["vec_in"], 16)

        @block.vector
        def _(dve):
            dve.wait_ge(s["vec_in"], 16)
            nc.vector.tensor_scalar(B.nsink, B.vec[:, VEC["sink"][0]:VEC["sink"][0] + 4], -1.0, None,
                                    ALU.mult).then_inc(s["nsink_ready"], 1)
            dve.wait_ge(s["nsink_ready"], 1)


def bcast(a, axis, n):
    a = a.unsqueeze(axis)
    shape = list(a.shape)
    shape[axis] = n
    return a.broadcast_to(shape)


def load2_phase(nc, B, I):
    with phase(nc, "in chain") as (block, s):

        @block.sync
        def _(sp):
            sp.dma_start(B.vec2, I["vec2"]).then_inc(s["in"], 16)
            sp.dma_start(B.ctx, I["ctx"]).then_inc(s["in"], 16)

        @block.vector
        def _(dve):
            ch = Chain(dve, s["chain"])
            dve.wait_ge(s["in"], 32)
            x_mod, ctx_mod = B.mod[:, :, 0], B.mod[:, 0:16, 1]
            v2 = B.v2
            ch.did(nc.vector.tensor_tensor(x_mod, x_mod, v2("b_ada"), ALU.add))
            ch.link(nc.vector.tensor_tensor(ctx_mod, ctx_mod, v2("b_ada")[:, 0:16], ALU.add))
            one = nc.vector.tensor_scalar
            ch.did(one(B.gains[:, 0, :], B.mod[:, 8:16, 0], 1.0, None, ALU.add))
            ch.did(one(B.gains[:, 1, :], B.mod[:, 8:16, 1], 1.0, None, ALU.add))
            ch.did(one(B.gains[:, 2, :], B.mod[:, 32:40, 0], 1.0, None, ALU.add))
            dve.wait_ge(s["chain"], ch.n)
            for j, name in enumerate(("mix_pre", "mix_pre", "ffn_pre")):
                ch.did(nc.vector.tensor_tensor(B.gains[:, j, :], B.gains[:, j, :], v2(name), ALU.mult))
            ch.did(nc.vector.tensor_tensor(B.gains[:, 3, :], B.mod[:, 16:24, 0], v2("mix_post"), ALU.mult))
            ch.did(nc.vector.tensor_tensor(B.gains[:, 4, :], B.mod[:, 40:48, 0], v2("ffn_post"), ALU.mult))
            dve.wait_ge(s["chain"], ch.n)


def norm_phase(nc, B, src, dst, gain, shift, add_to=None, prefetch=None):
    ps, con = B.ps, B.con
    with phase(nc, NORM + "chain") as (block, s):
        s.update(std=B.std[:, 0:T], var=B.var[:, 0:T], rstd=B.rstd[:, 0:T])
        ms = ps[:, 0, 0:T]

        if prefetch is not None:
            @block.sync
            def _(sp):
                prefetch(sp)

        @block.scalar
        def _(act):
            norm_act(act, nc, s, src, B.sq)

        @block.tensor
        def _(pe):
            norm_pe(pe, nc, s, B.sq, ms, con("mean_d"))

        @block.vector
        def _(dve):
            norm_dve(dve, nc, s, src, dst, ms, gain, shift)
            dve.wait_ge(s["h_normed"], KD)
            if add_to is not None:
                Chain(dve, s["chain"]).link(nc.vector.tensor_tensor(add_to, add_to, dst, ALU.add))


def norm_pair_phase(nc, B):
    ps, con = B.ps, B.con
    with phase(nc, NORM + " ".join("c_" + name for name in NORM.split())) as (block, sems):
        both = []
        for j, (src, buf) in enumerate(((B.x, B.sq), (B.ctx, B.raw[:, 0:2].rearrange("p a (k t) -> p (a k) t", t=T)))):
            tok = slice(j * T, (j + 1) * T)
            s = {name: sems["c_" * j + name] for name in NORM.split()}
            s.update(std=B.std[:, tok], var=B.var[:, tok], rstd=B.rstd[:, tok])
            both.append((s, src, buf, ps[:, j, 0:T], B.h_hi[:, :, tok], B.h_lo[:, :, tok]))

        @block.scalar
        def _(act):
            s2, src2, buf2, _, hi2, _ = both[1]
            s, src, buf, _, hi, _ = both[0]
            norm_act(act, nc, s, src, buf, buf, hi, between=lambda: norm_squares(act, nc, s2, src2, buf2))
            norm_act(act, nc, s2, src2, buf2, buf2, hi2, squared=True)

        @block.tensor
        def _(pe):
            for s, _, buf, ms, _, _ in both:
                norm_pe(pe, nc, s, buf, ms, con("mean_d"))

        @block.vector
        def _(dve):
            for j, (s, src, buf, ms, hi, lo) in enumerate(both):
                norm_dve(dve, nc, s, src, buf, ms, B.gains[:, j, :], B.mod[:, 0:8, j], (hi, lo))
                dve.wait_ge(s["h_lo_done"], KD)


def kv_phase(nc, B, I):
    ps = B.ps
    ring = 2
    with phase(nc, project_sems("kv", ring) + "gw gw_hi gw_lo g_mm g_out") as (block, s):

        @block.sync
        def _(sp):
            sp.dma_start(B.w_mg, I["w_mg"]).then_inc(s["gw"], 16)
            project_sp(sp, s, "kv", lambda c: I["w_kv"][c], B.raw, ring, CX)

        @block.tensor
        def _(pe):
            project_pe(pe, nc, s, "kv", B, B.h_hi, B.h_lo, lambda r: ps[:, r, :], ring, CX, NT2)
            pe.wait_ge(s["gw_lo"], 1)
            for t in range(NT2 // P):
                for k in range(KD):
                    tok = slice(t * P, (t + 1) * P)
                    mm = product(nc, ps[:, 7, 16 * t:16 * t + 16], B.h_hi[:, k, tok], B.h_lo[:, k, tok], B.w_mg_hi[:, k, :],
                                 B.w_mg_lo[:, k, :], k == 0, k == KD - 1)
            mm.then_inc(s["g_mm"], 1)

        @block.scalar
        def _(act):
            project_act(act, nc, s, "kv", B, ring, CX, lambda c, r: nc.scalar.copy(B.kv[:, c, :], ps[:, r, :]))

        @block.vector
        def _(dve):
            dve.wait_ge(s["gw"], 16)
            split_dve(dve, nc, B.w_mg, B.w_mg_hi, B.w_mg_lo, s["gw_hi"], s["gw_lo"], 1)
            project_dve(dve, nc, s, "kv", B, ring, CX)
            dve.wait_ge(s["g_mm"], 1)
            nc.vector.tensor_copy(B.mg, ps[:, 7, 0:64].rearrange("p (t g) -> p t g", g=16)).then_inc(s["g_out"], 1)
            dve.wait_ge(s["g_out"], 1)


def plain_project_phase(nc, B, wsrc, dst, ring, n, func):
    ps = B.ps
    with phase(nc, project_sems("q", ring)) as (block, s):

        @block.sync
        def _(sp):
            project_sp(sp, s, "q", wsrc, B.raw, ring, n)

        @block.tensor
        def _(pe):
            project_pe(pe, nc, s, "q", B, B.h_hi[:, :, 0:T], B.h_lo[:, :, 0:T], lambda r: ps[:, r, :], ring, n, T)

        @block.scalar
        def _(act):
            project_act(act, nc, s, "q", B, ring, n, lambda c, r: nc.scalar.activation(dst[:, c, :], ps[:, r, 0:T], func))

        @block.vector
        def _(dve):
            project_dve(dve, nc, s, "q", B, ring, n)


NAK, NAV, MLK, MLV = 0, 4, 8, 10
NAQ, MLQ, MLO = 0, 4, 6


def prepare2_phase(nc, B, I):
    ps, con, kv, q = B.ps, B.con, B.kv, B.q10
    with phase(nc, "v_turned v_copied q_scaled turned_mm rope chain tanh_in tanh exp_in exp ln_in ln table_in masked") as (block, s):

        @block.sync
        def _(sp):
            rows_kept = 2 * ROWS - 1
            copy = NA_HEADS * rows_kept * P
            for h in range(NA_HEADS):
                for qc in range(TC):
                    for r2 in range(P // GRID_W):
                        r = qc * (P // GRID_W) + r2
                        first = (h * rows_kept + ROWS - 1 - r) * P + GRID_W - 1
                        skew = bass.AP(tensor=I["rpb"].tensor, offset=first, ap=[[copy - 1, GRID_W], [P, ROWS], [1, GRID_W]])
                        dst = B.na_table[r2 * GRID_W:(r2 + 1) * GRID_W, h * TC + qc, :].rearrange("p (r c) -> p r c", c=GRID_W)
                        sp.dma_start(dst, skew).then_inc(s["table_in"], 16)

        @block.tensor
        def _(pe):
            for j, c0 in enumerate((NAV, MLV)):
                for t in range(NT2 // P):
                    for c in range(4):
                        mm = nc.tensor.transpose(ps[:, 4 * j + t, c * P:(c + 1) * P], kv[:, c0 + c, t * P:(t + 1) * P], con("ident"))
            mm.then_inc(s["v_turned"], 1)
            pe.wait_ge(s["v_copied"], 8)
            pe.wait_ge(s["q_scaled"], 1)
            for j in range(4):
                x = q[:, MLQ + j, :] if j < 2 else kv[:, MLK + j - 2, 0:T]
                mm = nc.tensor.matmul(ps[:, j // 2, (j % 2) * T:(j % 2 + 1) * T], con("turn"), x, start=(j % 2 == 0),
                                      stop=True, skip_group_check=True)
            mm.then_inc(s["turned_mm"], 1)

        @block.scalar
        def _(act):
            act.wait_ge(s["tanh_in"], 1)
            nc.scalar.activation(B.mg, B.mg, ACT.Tanh, scale=1.0 / CAP).then_inc(s["tanh"], 1)
            act.wait_ge(s["exp_in"], 1)
            nc.scalar.activation(B.mge, B.mgn, ACT.Exp).then_inc(s["exp"], 1)
            act.wait_ge(s["ln_in"], 1)
            nc.scalar.activation(B.mgn, B.mge, ACT.Ln).then_inc(s["ln"], 1)

        @block.vector
        def _(dve):
            ch = Chain(dve, s["chain"])
            nc.vector.tensor_scalar(q[:, 0:6, :], q[:, 0:6, :], HD ** -0.5, None, ALU.mult).then_inc(s["q_scaled"], 1)
            nc.vector.tensor_tensor(B.mg, B.mg, bcast(B.v2("gates"), 1, 4), ALU.add).then_inc(s["tanh_in"], 1)
            dve.wait_ge(s["v_turned"], 1)
            for j, dst in enumerate((B.v_na, B.v_ml)):
                for t in range(NT2 // P):
                    nc.vector.tensor_copy(dst[:, t, :], ps[:, 4 * j + t, :]).then_inc(s["v_copied"], 1)
            dve.wait_ge(s["tanh"], 1)
            ch.link(nc.vector.tensor_scalar(B.mg, B.mg, CAP, None, ALU.mult))
            ch.link(nc.vector.tensor_scalar(B.mge, B.mg, -1.0, None, ALU.mult))
            nc.vector.tensor_tensor(B.mgn, B.mg, B.mge, ALU.min).then_inc(s["exp_in"], 1)
            dve.wait_ge(s["exp"], 1)
            nc.vector.tensor_scalar(B.mge, B.mge, 1.0, None, ALU.add).then_inc(s["ln_in"], 1)
            dve.wait_ge(s["ln"], 1)
            ch.link(nc.vector.tensor_scalar(B.mlf, B.mg, 0.0, None, ALU.min))
            ch.link(nc.vector.tensor_tensor(B.mlf, B.mlf, B.mgn, ALU.subtract))
            for h in range(ML_HEADS):
                up, fr = con("upto"), con("from")
                for dst, mask, t, col in ((B.lf_f0[:, h, :], up[:, 0, :], 0, 4 + h), (B.lf_f1[:, h, :], up[:, 1, P:T], 1, 4 + h),
                                          (B.lf_b0[:, h, :], fr[:, 0, 0:P], 0, 12 + h), (B.lf_b1[:, h, :], fr[:, 1, :], 1, 12 + h)):
                    ch.did(nc.vector.tensor_scalar(dst, mask, B.mlf[:, t, col:col + 1], None, ALU.mult))
            dve.wait_ge(s["turned_mm"], 1)
            for j in range(2):
                x = q[:, MLQ:MLQ + 2, :] if j == 0 else kv[:, MLK:MLK + 2, 0:T]
                ch.link(nc.vector.tensor_tensor(B.ropet[:, 0:2, :], ps[:, j, :].rearrange("p (c t) -> p c t", t=T),
                                                bcast(con("sin"), 1, 2), ALU.mult))
                ch.link(nc.vector.tensor_tensor(x, x, bcast(con("cos"), 1, 2), ALU.mult))
                ch.link(nc.vector.tensor_tensor(x, x, B.ropet[:, 0:2, :], ALU.add))
            dve.wait_ge(s["table_in"], 16 * NA_HEADS * TC * (P // GRID_W))
            mask = bcast(con("na_mask"), 1, NA_HEADS * TC)
            nc.vector.tensor_tensor(B.na_table, B.na_table, mask, ALU.add).then_inc(s["masked"], 1)
            dve.wait_ge(s["masked"], 1)


def neighbourhood(nc, B):
    units = []
    for h in range(NA_HEADS):
        lo = (h % 2) * HD
        for qc in range(TC):
            def scores(dst, h=h, lo=lo, qc=qc):
                return nc.tensor.matmul(dst, B.q10[lo:lo + HD, NAQ + h // 2, qc * P:(qc + 1) * P],
                                        B.kv[lo:lo + HD, NAK + h // 2, :], start=True, stop=True)

            units.append(dict(scores=scores, table=B.na_table[:, h * TC + qc, :], sink=None, row=lo,
                              values=[B.v_na[:, t, h * HD:(h + 1) * HD] for t in range(NT2 // P)],
                              out=B.b_na[lo:lo + HD, h // 2, qc * P:(qc + 1) * P]))
    attention_phase(nc, B, units, NT2)


def mlstm_phase(nc, B, prefetch):
    ps, con, q, kv = B.ps, B.con, B.q10, B.kv
    units = [(h, qc, d) for h in range(ML_HEADS) for qc in range(TC) for d in range(2)]
    n = len(units)
    with phase(nc, "scores_ready max_ready exp_ready probs_ready turned probs_t_ready out_ready out_copied chain added prefetched") as (block, s):

        @block.sync
        def _(sp):
            sp.dma_start(*prefetch).then_inc(s["prefetched"], 16)
            sp.wait_ge(s["prefetched"], 16)

        spread = {0: (B.lf_f0, B.lf_f1), 1: (B.lf_b0, B.lf_b1)}

        @block.tensor
        def _(pe):
            def scores(u):
                h, qc, d = units[u]
                lo = (h % 2) * HD
                if u >= 2:
                    pe.wait_ge(s["probs_ready"], u - 1)
                nc.tensor.matmul(ps[:, u % 2, :], q[lo:lo + HD, MLQ + h // 2, qc * P:(qc + 1) * P],
                                 kv[lo:lo + HD, MLK + h // 2, :], start=True, stop=True)
                dd = ps[:, 2 + u % 2, :]
                side = con("after") if d == 0 else con("before")
                lf = 4 + h if d == 0 else 12 + h
                li = h if d == 0 else 8 + h
                chunks = [c for c in range(TC) if (c <= qc if d == 0 else c >= qc)]
                for j, c in enumerate(chunks):
                    a = spread[d][c]
                    whole = (c == 0) == (d == 0)
                    lhs = a[:, h, qc * P:(qc + 1) * P] if whole else a[:, h, :]
                    nc.tensor.matmul(dd, lhs, side[:, c, :], start=(j == 0), stop=False, skip_group_check=True)
                for c in range(TC):
                    nc.tensor.matmul(dd[:, T:NT2], B.mlf[:, TC + c, lf:lf + 1].broadcast_to([P, P]), side[:, c, 0:T],
                                     start=False, stop=False, skip_group_check=True)
                for c in range(2 * TC):
                    mm = nc.tensor.matmul(dd[:, c * P:(c + 1) * P], B.mg[:, c, li:li + 1].broadcast_to([P, P]), con("ident"),
                                          start=False, stop=(c == 2 * TC - 1), skip_group_check=True)
                mm.then_inc(s["scores_ready"], 1)

            def turn(u):
                pe.wait_ge(s["probs_ready"], u + 1)
                if u >= 2:
                    pe.wait_ge(s["probs_t_ready"], u - 1)
                for j in range(4):
                    mm = nc.tensor.transpose(ps[:, 4 + u % 2, j * P:(j + 1) * P], B.prob[:, u % 2, j * P:(j + 1) * P], con("ident"))
                mm.then_inc(s["turned"], 1)

            def values(u):
                h, qc, d = units[u]
                pe.wait_ge(s["probs_t_ready"], u + 1)
                if d == 0 and u >= 4:
                    pe.wait_ge(s["out_copied"], u // 2 - 1)
                for j in range(4):
                    mm = nc.tensor.matmul(ps[:, 6 + (u // 2) % 2, 0:P], B.v_ml[:, j, h * P:(h + 1) * P],
                                          B.prob_t[:, u % 2, j * P:(j + 1) * P], start=(d == 0 and j == 0),
                                          stop=(d == 1 and j == 3))
                mm.then_inc(s["out_ready"], 1)

            scores(0)
            for u in range(n + 1):
                if u + 1 < n:
                    scores(u + 1)
                if u < n:
                    turn(u)
                if u >= 1:
                    values(u - 1)

        @block.scalar
        def _(act):
            for u in range(n + 1):
                if u >= 1:
                    act.wait_ge(s["turned"], u)
                    if u >= 3:
                        act.wait_ge(s["out_ready"], u - 2)
                    nc.scalar.copy(B.prob_t[:, (u - 1) % 2, :], ps[:, 4 + (u - 1) % 2, :]).then_inc(s["probs_t_ready"], 1)
                if u < n:
                    act.wait_ge(s["max_ready"], u + 1)
                    nc.scalar.activation(B.stat[:, u % 2, 2:3], B.stat[:, u % 2, 0:1], ACT.Exp)
                    nc.scalar.activation(B.prob[:, u % 2, :], B.prob[:, u % 2, :], ACT.Exp,
                                         bias=B.stat[:, u % 2, 0:1]).then_inc(s["exp_ready"], 1)

        @block.vector
        def _(dve):
            ch = Chain(dve, s["chain"])
            for u in range(n + 2):
                if u < n:
                    h, qc, d = units[u]
                    dve.wait_ge(s["scores_ready"], u + 1)
                    if u >= 2:
                        dve.wait_ge(s["turned"], u - 1)
                    dd = ps[:, 2 + u % 2, :]
                    mask = con("causal" if d == 0 else "anticausal")[:, qc, :]
                    ch.did(nc.vector.tensor_tensor(B.prob[:, u % 2, 0:T], dd[:, 0:T], mask, ALU.add))
                    ch.link(nc.vector.tensor_copy(B.prob[:, u % 2, T:NT2], dd[:, T:NT2]))
                    nc.vector.tensor_reduce(B.stat[:, u % 2, 0:1], B.prob[:, u % 2, :], AX, ALU.max,
                                            negate=True).then_inc(s["max_ready"], 1)
                    dve.wait_ge(s["exp_ready"], u + 1)
                    den, minus = B.stat[:, u % 2, 1:2], B.stat[:, u % 2, 3:4]
                    p = B.prob[:, u % 2, :]
                    ch.link(nc.vector.tensor_tensor(p, p, ps[:, u % 2, :], ALU.mult))
                    ch.link(nc.vector.tensor_reduce(den, p, AX, ALU.add))
                    ch.link(nc.vector.tensor_scalar(minus, den, -1.0, None, ALU.mult))
                    ch.link(nc.vector.tensor_tensor(den, den, minus, ALU.max))
                    ch.link(nc.vector.tensor_tensor(den, den, B.stat[:, u % 2, 2:3], ALU.max))
                    ch.link(nc.vector.reciprocal(minus, den))
                    nc.vector.tensor_scalar(p, p, minus, None, ALU.mult).then_inc(s["probs_ready"], 1)
                if u >= 2 and units[u - 2][2] == 1:
                    h, qc, _ = units[u - 2]
                    dve.wait_ge(s["out_ready"], u - 1)
                    nc.vector.tensor_copy(B.b_ml[:, h, qc * P:(qc + 1) * P],
                                          ps[:, 6 + ((u - 2) // 2) % 2, 0:P]).then_inc(s["out_copied"], 1)
            dve.wait_ge(s["out_copied"], n // 2)


def head_norm_phase(nc, B):
    ps, con = B.ps, B.con
    sq = B.sq[:, 0:ML_HEADS, :]
    with phase(nc, "sq ms var std sig chain") as (block, s):

        @block.scalar
        def _(act):
            nc.scalar.activation(sq, B.b_ml, ACT.Square).then_inc(s["sq"], 1)
            nc.scalar.activation(B.q10[:, MLO:MLO + 4, :], B.q10[:, MLO:MLO + 4, :], ACT.Sigmoid).then_inc(s["sig"], 1)
            act.wait_ge(s["var"], 1)
            nc.scalar.activation(sq, sq, ACT.Sqrt).then_inc(s["std"], 1)

        @block.tensor
        def _(pe):
            pe.wait_ge(s["sq"], 1)
            for j in range(2):
                mm = nc.tensor.matmul(ps[:, j, :], con("mean_head"), sq[:, 2 * j:2 * j + 2, :], start=True, stop=True)
            mm.then_inc(s["ms"], 1)

        @block.vector
        def _(dve):
            ch = Chain(dve, s["chain"])
            dve.wait_ge(s["ms"], 1)
            nc.vector.tensor_scalar(sq, ps[:, 0:2, :].rearrange("p b (c t) -> p (b c) t", t=T), EPS, None,
                                    ALU.add).then_inc(s["var"], 1)
            dve.wait_ge(s["std"], 1)
            ch.link(nc.vector.reciprocal(sq, sq))
            dve.wait_ge(s["sig"], 1)
            ch.did(nc.vector.tensor_tensor(sq, sq, B.q10[:, MLO:MLO + 4, :], ALU.mult))
            dve.wait_ge(s["chain"], ch.n)
            for h in range(ML_HEADS):
                ch.did(nc.vector.scalar_tensor_tensor(B.b_ml[:, h, :], B.b_ml[:, h, :], B.v2("head")[:, h:h + 1], sq[:, h, :],
                                                      ALU.mult, ALU.mult))
            dve.wait_ge(s["chain"], ch.n)


NB = 2 * E


def router_phase(nc, B, I):
    ps, con = B.ps, B.con
    with phase(nc, "in logits h_turned h_copied max_ready exp_ready sel_ready counted chain listed") as (block, s):

        @block.sync
        def _(sp):
            sp.dma_start(B.w_r, I["w_router"]).then_inc(s["in"], 16)

        @block.tensor
        def _(pe):
            pe.wait_ge(s["in"], 16)
            for t in range(TC):
                for k in range(KD):
                    mm = nc.tensor.matmul(ps[:, 0, t * E:(t + 1) * E], B.h2[:, k, t * P:(t + 1) * P], B.w_r[:, k, :],
                                          start=(k == 0), stop=(k == KD - 1))
            mm.then_inc(s["logits"], 1)
            for t in range(TC):
                for k in range(KD):
                    mm = nc.tensor.transpose(ps[:, 2 + 2 * t + k // 4, (k % 4) * P:(k % 4 + 1) * P],
                                             B.h2[:, k, t * P:(t + 1) * P], con("ident"))
            mm.then_inc(s["h_turned"], 1)
            pe.wait_ge(s["sel_ready"], 1)
            for t in range(TC):
                for c in range(t + 1):
                    nc.tensor.matmul(ps[:, 1, t * E:(t + 1) * E], con("before")[:, c, t * P:(t + 1) * P], B.sel[:, c, :],
                                     start=(c == 0), stop=(c == t))
            for c in range(TC):
                mm = nc.tensor.matmul(ps[:, 1, TC * E:(TC + 1) * E], con("ones"), B.sel[:, c, :], start=(c == 0), stop=(c == TC - 1))
            mm.then_inc(s["counted"], 1)

        @block.scalar
        def _(act):
            act.wait_ge(s["max_ready"], 1)
            for t in range(TC):
                nc.scalar.activation(B.wtok[:, t, :], B.lg[:, t, :], ACT.Exp, bias=B.rmax[:, t:t + 1]).then_inc(s["exp_ready"], 1)
            act.wait_ge(s["h_turned"], 1)
            for t in range(TC):
                nc.scalar.copy(B.htok[:, t, :], ps[:, 2 + 2 * t:4 + 2 * t, :].rearrange("p b c -> p (b c)")).then_inc(s["h_copied"], 1)
            act.wait_ge(s["h_copied"], TC)

        @block.vector
        def _(dve):
            ch = Chain(dve, s["chain"])
            tt, ts, red = nc.vector.tensor_tensor, nc.vector.tensor_scalar, nc.vector.tensor_reduce
            dve.wait_ge(s["logits"], 1)
            ch.link(tt(B.lg, ps[:, 0, 0:TC * E].rearrange("p (t e) -> p t e", e=E), bcast(B.v2("b_router"), 1, TC), ALU.add))
            red(B.rmax, B.lg, AX, ALU.max, negate=True).then_inc(s["max_ready"], 1)
            for t in range(TC):
                other, this = bcast(B.lg[:, t, :], 1, E), bcast(B.lg[:, t, :], 2, E)
                ch.link(tt(B.cmp, other, this, ALU.is_equal))
                ch.link(tt(B.cmp, B.cmp, con("earlier"), ALU.mult))
                ch.link(tt(B.cmp2, other, this, ALU.is_gt))
                ch.link(tt(B.cmp, B.cmp, B.cmp2, ALU.add))
                ch.link(red(B.sel[:, t, :], B.cmp, AX, ALU.add))
            ts(B.sel, B.sel, TOPK - 0.5, None, ALU.is_lt).then_inc(s["sel_ready"], 1)
            dve.wait_ge(s["sel_ready"], 1)
            dve.wait_ge(s["exp_ready"], TC)
            ch.link(tt(B.wtok, B.wtok, B.sel, ALU.mult))
            ch.link(red(B.rsum, B.wtok, AX, ALU.add))
            ch.link(nc.vector.reciprocal(B.rsum, B.rsum))
            for t in range(TC):
                ch.did(ts(B.wtok[:, t, :], B.wtok[:, t, :], B.rsum[:, t:t + 1], None, ALU.mult))
            dve.wait_ge(s["counted"], 1)
            pos = ps[:, 1, 0:TC * E].rearrange("p (t e) -> p t e", e=E)
            for o in range(PER):
                part = B.slot[:, :, o:PER * E:PER]
                ch.link(ts(part, pos, 1.0 - o * SLOTS, None, ALU.add))
                ch.link(tt(part, part, B.sel, ALU.mult))
                ch.link(ts(part, part, -1.0, None, ALU.add))
            cnt = ps[:, 1, TC * E:(TC + 1) * E]
            ch.link(ts(B.nb[:, 0, :], cnt, 0.5, None, ALU.is_gt))
            for o in range(1, PER):
                ch.link(ts(B.nb[:, 1, :], cnt, o * SLOTS + 0.5, None, ALU.is_gt))
                ch.link(tt(B.nb[:, 0, :], B.nb[:, 0, :], B.nb[:, 1, :], ALU.add))
            ch.link(ts(B.nb[:, 0, 0:1], B.nb[:, 0, 0:1], 1.0, None, ALU.max))
            ch.link(tt(B.cmp, bcast(B.nb[:, 0, :], 1, E), con("earlier"), ALU.mult))
            ch.link(red(B.nb[:, 1, :], B.cmp, AX, ALU.add))
            ch.link(tt(B.nb[:, 1, :], B.nb[:, 1, :], B.nb[:, 0, :], ALU.add))
            blocks = B.list[:, 0, PER:PER + NB]
            ch.link(nc.vector.memset(B.list, -1.0))
            ch.link(tt(B.listc, bcast(B.nb[:, 1, :], 1, NB), bcast(con("block_no"), 2, E), ALU.is_le))
            ch.link(red(blocks, B.listc, AX, ALU.add))
            ch.link(ts(blocks, blocks, E - 1.0, None, ALU.min))
            col = B.list[:, 1, PER:PER + NB]
            ch.link(ts(col, blocks, float(PER), None, ALU.mult))
            for o in range(1, PER):
                ch.link(tt(B.same, blocks, B.list[:, 0, PER - o:PER - o + NB], ALU.is_equal))
                ch.link(tt(col, col, B.same, ALU.add))
            ch.link(nc.vector.tensor_copy(B.list[:, 1, 0:1], B.nb[:, 1, E - 1:E]))
            ch.link(nc.vector.tensor_copy(B.listi, B.list))


def expert_weights(sp, B, I, e, kind, half, sem):
    src = {"g": I["w_gate2"], "l": I["w_lin2"], "d": I["w_down2"]}[kind][e]
    sp.dma_start(B.wexp[2 * "gld".index(kind) + half],
                 src.rearrange("(k p) n -> p k n", p=P)[:, 4 * half:4 * half + 4, :]).then_inc(sem, 16)


def moe_phase(nc, B, I, first_in):
    ps, con = B.ps, B.con
    names = ("wg0 wg1 wl0 wl1 wd0 wd1 gate_half lin_half down_half g_ready sig_ready a_ready scattered0 scattered1 added0 added1 st_turned "
             "st_copied s_ready gathered hg_ready a_turned at_ready y_ready bias_in bias_spread t_read l_read g_read m_ready zeroed tick_ready")
    with phase(nc, names) as (block, s):
        G, L, Y, X, H, A, S_t = ps[:, 0, :], ps[:, 1, :], ps[:, 2, :], ps[:, 3:5, :], ps[:, 5, :], ps[:, 6, :], ps[:, 7, :]
        HALF = D // 2
        side = lambda half: slice(half * SLOTS, (half + 1) * SLOTS)

        def blocks(eng):
            return eng.value_load(B.listi[0:1, 1, 0:1], min_val=T * TOPK // SLOTS, max_val=NB - 1)

        def entry(eng, row, j, top):
            return eng.value_load(B.listi[0:1, row, bass.ds(j, 1)], min_val=0, max_val=top)

        @block.sync
        def _(sp):
            total = blocks(sp)
            e = entry(sp, 0, PER, E - 1)
            sp.dma_start(B.brow, I["bias2"][bass.ds(e, 1), :]).then_inc(s["bias_in"], 16)
            with sp.Fori(1, total) as j:
                e = entry(sp, 0, j + PER, E - 1)
                sp.wait_ge(s["bias_spread"], j)
                sp.dma_start(B.brow, I["bias2"][bass.ds(e, 1), :]).then_inc(s["bias_in"], 16)
                for kind, used in (("g", "gate_half"), ("l", "lin_half"), ("d", "down_half")):
                    for half in range(2):
                        sp.wait_ge(s[used], 2 * j + (half - 1))
                        expert_weights(sp, B, I, e, kind, half, s[f"w{kind}{half}"])

        @block.gpsimd
        def _(pool):
            total = blocks(pool)
            nc.gpsimd.memset(B.tick, 0.0).then_inc(s["tick_ready"], 1)
            pool.wait_ge(s["tick_ready"], 1)
            pool.wait_ge(s["bias_in"], 16)
            nc.gpsimd.partition_broadcast(B.bias, B.brow).then_inc(s["bias_spread"], 1)
            with pool.Fori(1, total) as j:
                pool.wait_ge(s["bias_in"], 16 * j + 16)
                pool.wait_ge(s["y_ready"], j)
                nc.gpsimd.tensor_tensor(B.tick[:, 1:2], B.tick[:, 0:1], B.tick[:, 0:1], ALU.add)
                nc.gpsimd.partition_broadcast(B.bias, B.brow).then_inc(s["bias_spread"], 1)

        @block.tensor
        def _(pe):
            total = blocks(pe)

            def gather():
                for k in range(KD):
                    for t in range(TC):
                        mm = nc.tensor.matmul(H[:, k * SLOTS:(k + 1) * SLOTS], B.htok[:, t, k * P:(k + 1) * P],
                                              B.S[:, t, 0:SLOTS], start=(t == 0), stop=(t == TC - 1))
                mm.then_inc(s["gathered"], 1)

            def wide(j, kind, lhs, dst, done):
                for part in range(2):
                    wait(pe, s[f"w{kind}{part}"], 16 * j)
                    for k in range(4 * part, 4 * part + 4):
                        for half in range(2):
                            mm = nc.tensor.matmul(dst[side(half), :], lhs(k),
                                                  B.wexp[2 * "gld".index(kind) + part][:, k % 4, half * HALF:(half + 1) * HALF],
                                                  start=(k == 0), stop=(k == KD - 1), skip_group_check=True)
                    mm.then_inc(s[done], 1)

            def scatter(t):
                for half in range(2):
                    mm = nc.tensor.matmul(X[:, half, :], B.ST[side(half), t, :], B.y[side(half), :], start=True, stop=True)
                mm.then_inc(s[f"scattered{t}"], 1)

            def block_turn(j, first):
                pe.wait_ge(s["hg_ready"], j + 1)
                if not first:
                    pe.wait_ge(s["g_read"], j)
                wide(j, "g", lambda k: B.hg[:, k, :], G, "gate_half")
                if not first:
                    pe.wait_ge(s["st_copied"], j)
                for t in range(TC):
                    mm = nc.tensor.transpose(S_t[:, t * P:(t + 1) * P], B.S[:, t, :], con("ident"))
                mm.then_inc(s["st_turned"], 1)
                if not first:
                    pe.wait_ge(s["y_ready"], j)
                    scatter(0)
                    pe.wait_ge(s["l_read"], j)
                wide(j, "l", lambda k: B.hg[:, k, :], L, "lin_half")
                if not first:
                    pe.wait_ge(s["added0"], j)
                    scatter(1)
                pe.wait_ge(s["s_ready"], j + 2)
                gather()
                pe.wait_ge(s["a_ready"], j + 1)
                for k in range(4):
                    mm = nc.tensor.transpose(A[:, k * P:(k + 1) * P], B.a[:, k * P:(k + 1) * P], con("ident"))
                mm.then_inc(s["a_turned"], 1)
                pe.wait_ge(s["at_ready"], j + 1)
                wide(j, "d", lambda k: B.aT[:, k % 4, side(k // 4)], Y, "down_half")

            pe.wait_ge(s["s_ready"], 1)
            gather()
            pe.wait_ge(first_in, 6 * 16)
            block_turn(0, True)
            with pe.Fori(1, total) as j:
                block_turn(j, False)
            pe.wait_ge(s["y_ready"], total)
            scatter(0)
            pe.wait_ge(s["added0"], total)
            scatter(1)

        @block.scalar
        def _(act):
            total = blocks(act)

            def gathered_copy(n):
                act.wait_ge(s["gathered"], n + 1)
                nc.scalar.copy(B.hg, H.rearrange("p (k t) -> p k t", t=SLOTS)).then_inc(s["hg_ready"], 1)

            def block_turn(j, first):
                act.wait_ge(s["g_ready"], j + 1)
                nc.scalar.activation(B.sg, B.g, ACT.Sigmoid, scale=ALPHA).then_inc(s["sig_ready"], 1)
                act.wait_ge(s["st_turned"], j + 1)
                if not first:
                    act.wait_ge(s["scattered1"], j)
                nc.scalar.copy(B.ST, S_t[:, 0:T].rearrange("p (a b) -> p a b", b=P)).then_inc(s["st_copied"], 1)
                gathered_copy(j + 1)
                act.wait_ge(s["a_turned"], j + 1)
                nc.scalar.copy(B.aT, A.rearrange("p (k t) -> p k t", t=P)).then_inc(s["at_ready"], 1)

            gathered_copy(0)
            block_turn(0, True)
            with act.Fori(1, total) as j:
                block_turn(j, False)

        @block.vector
        def _(dve):
            total = blocks(dve)
            tt, ts, stt = nc.vector.tensor_tensor, nc.vector.tensor_scalar, nc.vector.scalar_tensor_tensor

            def one_hot(j):
                col = entry(dve, 1, j + PER, PER * E - 1)
                for t in range(TC):
                    last = ts(B.S[:, t, :], con("slots"), B.slot[:, t, bass.ds(col, 1)], None, ALU.is_equal)
                last.then_inc(s["s_ready"], 1)

            def biased(dst, bank, n):
                for half in range(2):
                    last = tt(dst[side(half), :], bank[side(half), :],
                              B.bias[side(half), n * D + half * HALF:n * D + (half + 1) * HALF], ALU.add)
                return last

            def add(t, n, e):
                dve.wait_ge(s[f"scattered{t}"], n)
                stt(B.acc[:, t, :], X.rearrange("p b c -> p (b c)"), B.wtok[:, t, bass.ds(e, 1)], B.acc[:, t, :], ALU.mult, ALU.add).then_inc(s[f"added{t}"], 1)

            def block_turn(j, first):
                e = None if first else entry(dve, 0, j + (PER - 1), E - 1)
                dve.wait_ge(s["bias_spread"], j + 1)
                dve.wait_ge(s["gate_half"], 2 * j + 2)
                biased(B.g, G, 0).then_inc(s["g_read"], 1)
                dve.wait_ge(s["g_read"], j + 1)
                ts(B.g, B.g, LIMIT, None, ALU.min).then_inc(s["g_ready"], 1)
                dve.wait_ge(s["st_turned"], j + 1)
                one_hot(j + 1)
                if not first:
                    add(0, j, e)
                dve.wait_ge(s["sig_ready"], j + 1)
                tt(B.g, B.g, B.sg, ALU.mult).then_inc(s["t_read"], 1)
                dve.wait_ge(s["lin_half"], 2 * j + 2)
                biased(B.l, L, 1).then_inc(s["l_read"], 1)
                dve.wait_ge(s["l_read"], j + 1)
                ts(B.l, B.l, LIMIT, -LIMIT, ALU.min, ALU.max).then_inc(s["m_ready"], 1)
                dve.wait_ge(s["m_ready"], j + 1)
                dve.wait_ge(s["t_read"], j + 1)
                stt(B.a, B.l, 1.0, B.g, ALU.add, ALU.mult).then_inc(s["a_ready"], 1)
                if not first:
                    add(1, j, e)
                dve.wait_ge(s["down_half"], 2 * j + 2)
                biased(B.y, Y, 2).then_inc(s["y_ready"], 1)

            nc.vector.memset(B.acc, 0.0).then_inc(s["zeroed"], 1)
            dve.wait_ge(s["zeroed"], 1)
            one_hot(0)
            block_turn(0, True)
            with dve.Fori(1, total) as j:
                block_turn(j, False)
            e = entry(dve, 0, total + (PER - 1), E - 1)
            add(0, total, e)
            add(1, total, e)


def turn_back_phase(nc, B):
    ps = B.ps
    with phase(nc, "turned copied") as (block, s):

        @block.tensor
        def _(pe):
            for k in range(KD):
                for t in range(TC):
                    mm = nc.tensor.transpose(ps[:, k // 2, (k % 2) * T + t * P:(k % 2) * T + (t + 1) * P],
                                             B.acc[:, t, k * P:(k + 1) * P], B.con("ident"))
            mm.then_inc(s["turned"], 1)

        @block.vector
        def _(dve):
            dve.wait_ge(s["turned"], 1)
            nc.vector.tensor_copy(B.h2, ps[:, 0:4, :].rearrange("p b (c t) -> p (b c) t", t=T)).then_inc(s["copied"], 1)
            dve.wait_ge(s["copied"], 1)


def second_block_program(nc, B, I, out):
    B.stage = "second"
    mod = lambda c: B.mod[:, c:c + KD, 0]
    with ExitStack() as outer:
        (B.vec2, B.gains, B.h2) = alloc(
            nc, outer, B, vec2=(P, NVEC2), gains=(P, 5, KD), h2=(P, KD, T))
        B.v2 = lambda name: B.vec2[:, VEC2[name][0]:VEC2[name][0] + VEC2[name][1]]
        B.ctx = B.h2
        load2_phase(nc, B, I)
        with ExitStack() as ctx:
            (B.kv, B.q10, B.mg, B.mge, B.mgn, B.mlf, B.gates) = alloc(
                nc, ctx, B, kv=(P, CX, NT2), q10=(P, LX, T), mg=(P, 4, 16), mge=(P, 4, 16), mgn=(P, 4, 16), mlf=(P, 4, 16),
                gates=(P, G2, T))
            halves = B.kv[:, NAV:NAV + 4, :].rearrange("p c (b t) -> p (c b) t", t=T)
            B.b_na, B.b_ml = halves[:, 0:4, :], halves[:, 4:8, :]
            with ExitStack() as proj:
                (B.w_mg,) = alloc(nc, proj, B, w_mg=(P, KD, 16))
                B.h_hi, B.h_lo, B.w_mg_hi, B.w_mg_lo = alloc(
                    nc, proj, B, F32R, h_hi=(P, KD, NT2), h_lo=(P, KD, NT2), w_mg_hi=(P, KD, 16), w_mg_lo=(P, KD, 16))
                split_ring(nc, proj, B, 4)
                norm_pair_phase(nc, B)
                kv_phase(nc, B, I)
                plain_project_phase(nc, B, lambda c: I["w_q2"][c], B.q10, 2, LX, ACT.Copy)
                plain_project_phase(nc, B, lambda c: I["w_g2"][c], B.gates, 4, G2, ACT.Sigmoid)
            with ExitStack() as branches:
                (B.prob, B.prob_t, B.stat) = alloc(
                    nc, branches, B, prob=(P, DEPTH_A, 512), prob_t=(P, 2, 512), stat=(P, DEPTH_A, 4))
                B.ropet = B.prob_t.rearrange("p a (b t) -> p (a b) t", t=T)
                B.mtmp = B.ropet
                B.h_hi, B.h_lo = alloc(nc, branches, B, F32R, m_hi=(P, KD, T), m_lo=(P, KD, T))
                with ExitStack() as ml:
                    (B.lf_f0, B.lf_f1, B.lf_b0, B.lf_b1, B.v_ml) = alloc(
                        nc, ml, B, lf_f0=(P, 4, T), lf_f1=(P, 4, P), lf_b0=(P, 4, P), lf_b1=(P, 4, T), v_ml=(P, 4, 512))
                    with ExitStack() as near:
                        (B.na_table, B.v_na) = alloc(nc, near, B, na_table=(P, NA_HEADS * TC, T), v_na=(P, 4, 512))
                        prepare2_phase(nc, B, I)
                        neighbourhood(nc, B)
                    (B.wb,) = alloc(nc, ml, B, wb=(P, 8, D))
                    mlstm_phase(nc, B, (B.wb, I["w_branch2"]))
                    head_norm_phase(nc, B)
                    merge_phase(nc, B, [B.b_na, B.b_ml], 4, B.gates, 2)
                split_ring(nc, branches, B, 4)
                out_phase(nc, B, lambda c: I["w_out2"][c], B.h2, False)
        with ExitStack() as ctx:
            (B.wexp_all,) = alloc(nc, ctx, B, wexp_all=(P, 6, 4, D))
            B.wexp = [B.wexp_all[:, i] for i in range(6)]
            first_in = nc.alloc_semaphore("expert0_in")

            def prefetch(sp):
                for kind in "gld":
                    for half in range(2):
                        expert_weights(sp, B, I, 0, kind, half, first_in)

            norm_phase(nc, B, B.h2, B.h2, B.gains[:, 3, :], None, add_to=B.x, prefetch=prefetch)
            norm_phase(nc, B, B.x, B.h2, B.gains[:, 2, :], mod(24))
            (B.w_r, B.lg, B.rmax, B.rsum, B.sel, B.wtok, B.slot, B.nb, B.same, B.list, B.htok, B.acc) = alloc(
                nc, ctx, B, w_r=(P, KD, E), lg=(P, TC, E), rmax=(P, TC), rsum=(P, TC), sel=(P, TC, E),
                wtok=(P, TC, E), slot=(P, TC, PER * E), nb=(P, 2, E), same=(P, NB),
                list=(P, 2, PER + NB), htok=(P, TC, D),
                acc=(P, TC, D))
            B.listi = ctx.enter_context(nc.sbuf_tensor("listi", [P, 2, PER + NB], I32))[:, :, :]
            with ExitStack() as small:
                (B.cmp, B.cmp2, B.listc) = alloc(
                    nc, small, B, cmp=(P, E, E), cmp2=(P, E, E), listc=(P, NB, E))
                router_phase(nc, B, I)
            (B.S, B.ST, B.y, B.aT, B.hg, B.tick) = alloc(
                nc, ctx, B, S=(P, TC, P), ST=(P, TC, P), y=(P, D // 2), aT=(P, 4, P), hg=(P, KD, SLOTS),
                tick=(P, 2))
            spent = B.con_all[:, B.con_kept:]
            B.bias, B.brow = spent[:, 0:3 * D], spent[0:1, 3 * D:6 * D]
            rows = B.sq.rearrange("p (h k) t -> p h (k t)", h=4)
            B.g, B.sg, B.l, B.a = [rows[:, i] for i in range(4)]
            moe_phase(nc, B, I, first_in)
            nc.clear_and_free_semaphores([first_in])
            nc.all_engine_barrier()
            turn_back_phase(nc, B)
            norm_phase(nc, B, B.h2, B.h2, B.gains[:, 4, :], None, add_to=B.x)
        with phase(nc, "stored") as (block, s):
            @block.sync
            def _(sp):
                sp.dma_start(out, B.x).then_inc(s["stored"], 16)
                sp.wait_ge(s["stored"], 16)



def build(nc, I, out, stop=None):
    PHASES.clear()
    _, at = _constants()
    with ExitStack() as ctx:
        B = Bufs()
        width = I["const"].shape[1]
        (B.x, B.con_all, B.sq, B.var, B.std, B.rstd, B.mod) = alloc(
            nc, ctx, B, x=(P, KD, T), con_all=(P, width), sq=(P, KD, T), var=(P, 512), std=(P, 512), rstd=(P, 512),
            mod=(P, 48, 2))
        B.ps = ctx.enter_context(nc.psum_tensor("ps", [P, 8, 512], F32))[:, :, :]
        B.d_cond = nc.dram_tensor("cond_scratch", (1, 2 * D), F32, kind="Internal").ap()
        B.d_line = nc.dram_tensor("line_scratch", (P, 4, 512), F32, kind="Internal").ap()

        def con(name):
            n, shape = at[name]
            size = int(np.prod(shape[1:]))
            a = B.con_all[:, n:n + size]
            if len(shape) == 3:
                a = a.rearrange("p (a b) -> p a b", b=shape[2])
            return a

        B.con = con
        B.con_kept = at["ones"][0]
        B.con_tables = (at["window"][0], at["na_mask"][0])
        first_block_program(nc, B, I)
        if stop == "first":
            with phase(nc, "stored") as (block, s):
                @block.sync
                def _(sp):
                    sp.dma_start(out, B.x).then_inc(s["stored"], 16)
                    sp.wait_ge(s["stored"], 16)
            return
        second_block_program(nc, B, I, out)


def _chunk_rows(w):
    *lead, d, f = w.shape
    w = w.reshape(*lead, d // P, P, f // P, P)
    n = len(lead)
    return np.ascontiguousarray(w.transpose(*range(n), n + 2, n + 1, n, n + 3)).reshape(*lead, f // P, P, d)


def _cols(v):
    return v.reshape(-1, P).T


def _rep(v):
    return np.tile(v.reshape(1, -1), (P, 1))


def layout(a):
    I = {}
    I["const"] = _constants()[0]
    I["x"] = a["x"][0].T.reshape(KD, P, T).transpose(1, 0, 2)
    I["rel_bias"] = a["rel_bias"]
    for f in ("ffn1", "ffn2"):
        I[f + "_wg"] = _chunk_rows(a[f + "_w_gate"])
        I[f + "_wu"] = _chunk_rows(a[f + "_w_up"])
        I[f + "_wd"] = a[f + "_w_down"].reshape(DEPTH, FC, P, D)
    w = a["w_in"]
    zc = ZC * P
    I["w_z"] = _chunk_rows(w[:, :, :zc])
    I["w_ff"] = w[:, :, zc:zc + 4].reshape(DEPTH, KD, P, 4).transpose(0, 2, 1, 3)
    I["w_g"] = _chunk_rows(w[:, :, zc + 4:])
    I["w_branch"] = np.stack([a[n].reshape(DEPTH, 2, P, D) for n in ("conf_w_out", "sc_w_out", "swa_w_o", "fox_w_o")],
                             1).reshape(DEPTH, 8, P, D).transpose(0, 2, 1, 3)
    I["w_out"] = _chunk_rows(a["w_out"])
    rows = []
    for l in range(DEPTH):
        rows.append(np.concatenate([
            _cols(a["ffn1_norm"][l]), _cols(a["mix_norm"][l]), _cols(a["ffn2_norm"][l]),
            a["conf_dw"][l].T[:P], a["conf_dw"][l].T[P:], _cols(a["conf_dw_b"][l]), _cols(a["conf_ln_g"][l]),
            _cols(a["conf_ln_b"][l]), a["sc_conv"][l].T[:P], a["sc_conv"][l].T[P:],
            *[np.tile(a[n][l], 2)[:, None] for n in ("swa_q_norm", "swa_k_norm", "fox_q_norm", "fox_k_norm")],
            _rep(a["b_forget"][l]), _rep(a["swa_sink"][l])], 1))
    I["vec"] = np.stack(rows)
    kv_cols = 4 * P + 4 * P + 2 * P + 4 * P
    w = a["w_in_2"][0]
    I["w_kv"] = _chunk_rows(w[:, :kv_cols])
    I["w_mg"] = w[:, kv_cols:kv_cols + 16].reshape(KD, P, 16).transpose(1, 0, 2)
    I["w_q2"] = _chunk_rows(w[:, kv_cols + 16:kv_cols + 16 + LX * P])
    I["w_g2"] = _chunk_rows(w[:, kv_cols + 16 + LX * P:])
    I["w_ada"] = a["w_ada_2"][0].T.reshape(48, P, D)
    I["c_row"] = np.concatenate([a["c_2"].reshape(1, D), a["c_ctx_2"].reshape(1, D)], 1)
    I["ctx"] = a["ctx_2"][0].T.reshape(KD, P, T).transpose(1, 0, 2)
    rpb = np.zeros((GRID_W, NA_HEADS, 2 * ROWS - 1, P), np.float32)
    rpb[:, :, :, GRID_W - WIN_W:GRID_W + WIN_W - 1] = a["rpb_2"][0][:, WIN_H - ROWS:WIN_H + ROWS - 1]
    I["rpb"] = rpb
    I["w_branch2"] = np.concatenate([a["w_branch_na_2"][0].reshape(4, P, D), a["w_branch_ml_2"][0].reshape(4, P, D)]).transpose(1, 0, 2)
    I["w_out2"] = _chunk_rows(a["w_out_2"][0])
    I["w_router"] = a["w_router_2"][0].reshape(KD, P, E).transpose(1, 0, 2)
    I["w_gate2"], I["w_lin2"], I["w_down2"] = a["w_gate_2"][0], a["w_lin_2"][0], a["w_down_2"][0]
    I["bias2"] = np.concatenate([a["b_gate_2"][0], a["b_lin_2"][0], a["b_down_2"][0]], 1)
    I["vec2"] = np.concatenate([
        _cols(a["b_ada_2"][0]), _cols(a["g_mix_pre_2"][0]), _cols(a["g_mix_post_2"][0]),
        _cols(a["g_ffn_pre_2"][0]), _cols(a["g_ffn_post_2"][0]), _rep(a["b_mlstm_gates_2"][0]), _cols(a["g_mlstm_head_2"][0]),
        _rep(a["b_router_2"][0])], 1)
    return {k: np.ascontiguousarray(v) for k, v in I.items()}


def kernel(**inputs):
    import concourse.bacc as _bacc
    from concourse.bass_utils import run_bass_kernel_spmd as _run

    arrays = layout({k: np.asarray(v) for k, v in inputs.items()})
    nc = _bacc.Bacc("TRN2", target_bir_lowering=False, num_devices=1)
    I = {k: nc.dram_tensor(f"in_{k}", v.shape, F32, kind="ExternalInput").ap() for k, v in arrays.items()}
    out = nc.dram_tensor("out", (P, KD, T), F32, kind="ExternalOutput").ap()
    build(nc, I, out, stop=STOP)
    r = _run(nc, [{f"in_{k}": v for k, v in arrays.items()}], core_ids=[0])
    o = r.results[0]["out"]
    return np.ascontiguousarray(o.transpose(2, 1, 0).reshape(1, T, D))


STOP = None
```
